# Optimizing a Trainium2 kernel written in Bass

```python
import jax, jax.numpy as jnp
from jax import lax
import numpy as np
import math
import functools
import jax
import jax.numpy as jnp

D_MODEL = 1024
BATCH = 1
SEQ = 256
DEPTH = 2

N_HEADS = 16
HEAD_DIM = 64
N_KV_HEADS = 4
ROT_DIM = HEAD_DIM // 4
ROPE_THETA = 500000.0
MOBA_BLOCK = 256
MOBA_TOPK = 3
MOBA_QCHUNK = 32
WINDOW = 128
D_FF = 2816
CONV_W = 3
N_A = DEPTH // 2
N_B = DEPTH - N_A
EPS = 1e-6
NEG = -1e30


def rmsnorm(x, g):
    xf = x.astype(jnp.float32)
    y = xf * lax.rsqrt(jnp.mean(xf * xf, axis=-1, keepdims=True) + EPS)
    return (y * g.astype(jnp.float32)).astype(x.dtype)

def rope_tables(positions):
    inv_freq = ROPE_THETA ** (-jnp.arange(0, ROT_DIM, 2, dtype=jnp.float32) / ROT_DIM)
    ang = positions.astype(jnp.float32)[..., None] * inv_freq
    return jnp.cos(ang)[:, :, None, :], jnp.sin(ang)[:, :, None, :]

def partial_rope(x, cos, sin):
    half = ROT_DIM // 2
    x1 = x[..., :half].astype(jnp.float32)
    x2 = x[..., half:ROT_DIM].astype(jnp.float32)
    r1 = (x1 * cos - x2 * sin).astype(x.dtype)
    r2 = (x2 * cos + x1 * sin).astype(x.dtype)
    return jnp.concatenate([r1, r2, x[..., ROT_DIM:]], axis=-1)

def moba_attention(q, k, v):
    B_, H_, S_, dh = q.shape
    nb = -(-S_ // MOBA_BLOCK)
    pad = nb * MOBA_BLOCK - S_
    kp = jnp.pad(k, ((0, 0), (0, 0), (0, pad), (0, 0)))
    vp = jnp.pad(v, ((0, 0), (0, 0), (0, pad), (0, 0)))
    kb = kp.reshape(B_, H_, nb, MOBA_BLOCK, dh)
    vb = vp.reshape(B_, H_, nb, MOBA_BLOCK, dh)
    k_mean = jnp.mean(kb.astype(jnp.float32), axis=3)
    q_blk = jnp.arange(S_) // MOBA_BLOCK
    gate = jnp.einsum('bhsd,bhnd->bhsn', q.astype(jnp.float32), k_mean)
    past = jnp.arange(nb)[None, :] < q_blk[:, None]
    gate = jnp.where(past, gate, NEG)
    n_sel = min(MOBA_TOPK, nb)
    _, sel_idx = lax.top_k(gate, n_sel)
    sel_valid = jnp.arange(n_sel)[None, :] < q_blk[:, None]
    scale = HEAD_DIM ** -0.5
    bi = jnp.arange(B_)[:, None, None, None]
    hi = jnp.arange(H_)[None, :, None, None]
    qpos_local = jnp.arange(MOBA_QCHUNK)
    kpos_local = jnp.arange(MOBA_BLOCK)

    def chunk(c):
        q0 = c * MOBA_QCHUNK
        qc = lax.dynamic_slice_in_dim(q, q0, MOBA_QCHUNK, axis=2)
        idx = lax.dynamic_slice_in_dim(sel_idx, q0, MOBA_QCHUNK, axis=2)
        valid = lax.dynamic_slice_in_dim(sel_valid, q0, MOBA_QCHUNK, axis=0)
        k_g = kb[bi, hi, idx]
        v_g = vb[bi, hi, idx]
        l_sel = jnp.einsum('bhqd,bhqnpd->bhqnp', qc, k_g).astype(jnp.float32) * scale
        l_sel = jnp.where(valid[None, None, :, :, None], l_sel, NEG)
        l_sel = l_sel.reshape(B_, H_, MOBA_QCHUNK, n_sel * MOBA_BLOCK)
        own0 = (q0 // MOBA_BLOCK) * MOBA_BLOCK
        k_own = lax.dynamic_slice_in_dim(kp, own0, MOBA_BLOCK, axis=2)
        v_own = lax.dynamic_slice_in_dim(vp, own0, MOBA_BLOCK, axis=2)
        l_own = jnp.einsum('bhqd,bhpd->bhqp', qc, k_own).astype(jnp.float32) * scale
        causal = (own0 + kpos_local)[None, :] <= (q0 + qpos_local)[:, None]
        l_own = jnp.where(causal, l_own, NEG)
        p = jax.nn.softmax(jnp.concatenate([l_sel, l_own], axis=-1), axis=-1).astype(v.dtype)
        p_sel = p[..., :n_sel * MOBA_BLOCK].reshape(B_, H_, MOBA_QCHUNK, n_sel, MOBA_BLOCK)
        p_own = p[..., n_sel * MOBA_BLOCK:]
        return (jnp.einsum('bhqnp,bhqnpd->bhqd', p_sel, v_g)
                + jnp.einsum('bhqp,bhpd->bhqd', p_own, v_own))

    out = lax.map(chunk, jnp.arange(S_ // MOBA_QCHUNK))
    return out.transpose(1, 2, 0, 3, 4).reshape(B_, H_, S_, dh)

def swa_sink_attention(q, k, v, sinks):
    B_, Hq, S_, dh = q.shape
    G = Hq // N_KV_HEADS
    nq = S_ // WINDOW
    qb = q.reshape(B_, N_KV_HEADS, G, nq, WINDOW, dh)
    kb = k.reshape(B_, N_KV_HEADS, nq, WINDOW, dh)
    vb = v.reshape(B_, N_KV_HEADS, nq, WINDOW, dh)
    kcat = jnp.concatenate([jnp.pad(kb, ((0, 0), (0, 0), (1, 0), (0, 0), (0, 0)))[:, :, :-1], kb], axis=3)
    vcat = jnp.concatenate([jnp.pad(vb, ((0, 0), (0, 0), (1, 0), (0, 0), (0, 0)))[:, :, :-1], vb], axis=3)
    logits = jnp.einsum('bkgnqd,bknpd->bkgnqp', qb, kcat).astype(jnp.float32) * (HEAD_DIM ** -0.5)
    rel = (jnp.arange(WINDOW)[:, None] + WINDOW) - jnp.arange(2 * WINDOW)[None, :]
    band = (rel >= 0) & (rel < WINDOW)
    key_pos = jnp.arange(nq)[:, None, None] * WINDOW - WINDOW + jnp.arange(2 * WINDOW)[None, None, :]
    mask = band[None] & (key_pos >= 0)
    logits = jnp.where(mask, logits, NEG)
    sink = sinks.astype(jnp.float32).reshape(N_KV_HEADS, G)[None, :, :, None, None, None]
    m = jnp.maximum(jnp.max(logits, axis=-1, keepdims=True), sink)
    e = jnp.exp(logits - m)
    p = e / (jnp.sum(e, axis=-1, keepdims=True) + jnp.exp(sink - m))
    out = jnp.einsum('bkgnqp,bknpd->bkgnqd', p.astype(v.dtype), vcat)
    return out.reshape(B_, Hq, S_, dh)

def conv_ffn(h, w_up, conv_w, conv_b, w_down):
    S_ = h.shape[1]
    u = h @ w_up
    up = jnp.pad(u, ((0, 0), (CONV_W - 1, 0), (0, 0)))
    u = conv_b + sum(conv_w[j] * up[:, j:j + S_] for j in range(CONV_W))
    gate, val = jnp.split(u, 2, axis=-1)
    return (jax.nn.silu(gate) * val) @ w_down

def first_inputs(seed: int = 0) -> dict:
    key = jax.random.key(seed)
    ks = jax.random.split(key, 20)
    D = D_MODEL
    kv_w = 2 * N_KV_HEADS * HEAD_DIM
    res_scale = (2 * DEPTH) ** -0.5

    def nrm(k, shape, fan_in, extra=1.0):
        return jax.random.normal(k, shape, jnp.float32) * (fan_in ** -0.5) * extra

    def gain(k, shape):
        return 1.0 + 0.02 * jax.random.normal(k, shape, jnp.float32)

    offset = jax.random.randint(ks[1], (BATCH, 1), 0, 1024, dtype=jnp.int32)
    positions = offset + jnp.arange(SEQ, dtype=jnp.int32)[None, :]
    return {
        'x': jax.random.normal(ks[0], (BATCH, SEQ, D), jnp.float32),
        'positions': positions,
        'attn_norm': gain(ks[2], (DEPTH, D)),
        'w_qkv_a': nrm(ks[3], (N_A, D, 3 * N_HEADS * HEAD_DIM), D),
        'w_o_a': nrm(ks[4], (N_A, N_HEADS * HEAD_DIM, D), N_HEADS * HEAD_DIM, res_scale),
        'kv_norm': gain(ks[5], (D,)),
        'w_kv_b': nrm(ks[6], (D, kv_w), D),
        'w_q_b': nrm(ks[7], (N_B, D, N_HEADS * HEAD_DIM), D),
        'sinks_b': 0.5 * jax.random.normal(ks[8], (N_B, N_HEADS), jnp.float32),
        'w_o_b': nrm(ks[9], (N_B, N_HEADS * HEAD_DIM, D), N_HEADS * HEAD_DIM, res_scale),
        'ffn_norm': gain(ks[10], (DEPTH, D)),
        'w_up': nrm(ks[11], (DEPTH, D, 2 * D_FF), D),
        'conv_w': nrm(ks[12], (DEPTH, CONV_W, 2 * D_FF), CONV_W),
        'conv_b': 0.01 * jax.random.normal(ks[13], (DEPTH, 2 * D_FF), jnp.float32),
        'w_down': nrm(ks[14], (DEPTH, D_FF, D), D_FF, res_scale),
        'final_norm': gain(ks[15], (D,)),
    }

def first_block(x, positions, attn_norm, w_qkv_a, w_o_a, kv_norm, w_kv_b, w_q_b, sinks_b,
              w_o_b, ffn_norm, w_up, conv_w, conv_b, w_down, final_norm):
    B_, S_, _ = x.shape
    cos, sin = rope_tables(positions)

    def heads(t, n):
        return t.reshape(B_, S_, n, HEAD_DIM)

    def to_bhsd(t):
        return t.transpose(0, 2, 1, 3)

    shared_k = None
    shared_v = None
    for l in range(DEPTH):
        if l < N_A:
            h = rmsnorm(x, attn_norm[l])
            q, k, v = jnp.split(h @ w_qkv_a[l], 3, axis=-1)
            q = partial_rope(heads(q, N_HEADS), cos, sin)
            k = partial_rope(heads(k, N_HEADS), cos, sin)
            o = moba_attention(to_bhsd(q), to_bhsd(k), to_bhsd(heads(v, N_HEADS)))
            w_o = w_o_a[l]
        else:
            if l == N_A:
                hk = rmsnorm(x, kv_norm)
                k, v = jnp.split(hk @ w_kv_b, 2, axis=-1)
                shared_k = to_bhsd(partial_rope(heads(k, N_KV_HEADS), cos, sin))
                shared_v = to_bhsd(heads(v, N_KV_HEADS))
            i = l - N_A
            h = rmsnorm(x, attn_norm[l])
            q = partial_rope(heads(h @ w_q_b[i], N_HEADS), cos, sin)
            o = swa_sink_attention(to_bhsd(q), shared_k, shared_v, sinks_b[i])
            w_o = w_o_b[i]
        x = x + o.transpose(0, 2, 1, 3).reshape(B_, S_, N_HEADS * HEAD_DIM) @ w_o
        x = x + conv_ffn(rmsnorm(x, ffn_norm[l]), w_up[l], conv_w[l], conv_b[l], w_down[l])
    return rmsnorm(x, final_norm)


DEPTH_2 = 1

N_MIXERS = 4
CHUNK = 64
CONV_K = 5
PLE_DIM = 256

GDN_QK_HEADS = 8
GDN_V_HEADS = 16
GDN_HEAD_DIM = 128
GDN_KEY_WIDTH = GDN_QK_HEADS * GDN_HEAD_DIM
GDN_VAL_WIDTH = GDN_V_HEADS * GDN_HEAD_DIM
GDN_CONV_CH = 2 * GDN_KEY_WIDTH + GDN_VAL_WIDTH
GDN_IN = GDN_CONV_CH + GDN_VAL_WIDTH + 4 * GDN_V_HEADS

M2_D_INNER = 2 * D_MODEL
M2_HEAD_DIM = 64
M2_HEADS = M2_D_INNER // M2_HEAD_DIM
M2_GROUPS = 4
M2_HEADS_PER_GROUP = M2_HEADS // M2_GROUPS
M2_STATE = 128
M2_CONV_CH = M2_D_INNER + 2 * M2_GROUPS * M2_STATE
M2_IN = M2_D_INNER + M2_CONV_CH + 2 * M2_HEADS

HG_EXPAND = 128
HG_HEADS = D_MODEL // HG_EXPAND
HG_WIDTH = HG_HEADS * HG_EXPAND
HG_IN = 5 * HG_WIDTH

GLA_HEADS = 4
GLA_KEY_WIDTH = D_MODEL // 2
GLA_VAL_WIDTH = D_MODEL
GLA_K = GLA_KEY_WIDTH // GLA_HEADS
GLA_V = GLA_VAL_WIDTH // GLA_HEADS
GLA_GATE_RANK = 16
GLA_GATE_TEMP = 16.0
GLA_IN = 2 * GLA_KEY_WIDTH + 2 * GLA_VAL_WIDTH + 2 * GLA_GATE_RANK

MOE_GROUPS = 4
MOE_EXPERTS_PER_GROUP = 8
MOE_EXPERTS = MOE_GROUPS * MOE_EXPERTS_PER_GROUP
MOE_TOPK = 2
MOE_HIDDEN = 256

DEEPNORM_ALPHA = (2 * DEPTH_2) ** 0.25
DEEPNORM_BETA = (8 * DEPTH_2) ** -0.25
LN_EPS = 1e-5
NORM_EPS = 1e-6
F32 = jnp.float32


def _n_uses(m):
    return (DEPTH_2 - m + N_MIXERS - 1) // N_MIXERS

def _layernorm(t, g, b):
    tf = t.astype(F32)
    mu = jnp.mean(tf, axis=-1, keepdims=True)
    var = jnp.mean(jnp.square(tf - mu), axis=-1, keepdims=True)
    return ((tf - mu) * lax.rsqrt(var + LN_EPS) * g.astype(F32) + b.astype(F32)).astype(t.dtype)

def _rms(t):
    tf = t.astype(F32)
    return tf * lax.rsqrt(jnp.mean(tf * tf, axis=-1, keepdims=True) + NORM_EPS)

def _l2norm(t):
    tf = t.astype(F32)
    return tf * lax.rsqrt(jnp.sum(tf * tf, axis=-1, keepdims=True) + NORM_EPS)

def _dwconv(t, w):
    return lax.conv_general_dilated(
        t, w[:, None, :].astype(t.dtype), window_strides=(1,),
        padding=[(CONV_K // 2, CONV_K // 2)],
        dimension_numbers=("NWC", "WIO", "NWC"),
        feature_group_count=t.shape[-1])

def _rev(t):
    return jnp.flip(t, axis=1)

def _chunks(t):
    bsz, seq = t.shape[:2]
    t = t.reshape(bsz, seq // CHUNK, CHUNK, *t.shape[2:])
    return jnp.swapaxes(jnp.swapaxes(t, 0, 1), 2, 3)

def _unchunks(t):
    t = jnp.swapaxes(jnp.swapaxes(t, 2, 3), 0, 1)
    return t.reshape(t.shape[0], t.shape[1] * t.shape[2], *t.shape[3:])

def _gated_delta_rule(q, k, v, beta, g):
    q, k, v, beta, g = (_chunks(t.astype(F32)) for t in (q, k, v, beta, g))
    gc = jnp.cumsum(g, axis=-1)
    incl = jnp.tril(jnp.ones((CHUNK, CHUNK), dtype=bool))
    decay = jnp.exp(jnp.where(incl, gc[..., :, None] - gc[..., None, :], -jnp.inf))
    eye = jnp.eye(CHUNK, dtype=F32)
    kb = k * beta[..., None]
    lhs = eye + jnp.einsum("nbhik,nbhjk->nbhij", kb, k) * decay * (1.0 - eye)
    solve = functools.partial(lax.linalg.triangular_solve, left_side=True, lower=True,
                              unit_diagonal=True)
    u = solve(lhs, v * beta[..., None])
    w = solve(lhs, kb * jnp.exp(gc)[..., None])
    attn = jnp.einsum("nbhik,nbhjk->nbhij", q, k) * decay
    q_dec = q * jnp.exp(gc)[..., None]
    k_dec = k * jnp.exp(gc[..., -1:] - gc)[..., None]
    g_last = jnp.exp(gc[..., -1])

    def step(state, inp):
        attn_c, q_c, k_c, u_c, w_c, gl = inp
        v_new = u_c - jnp.einsum("bhck,bhkv->bhcv", w_c, state)
        o = jnp.einsum("bhck,bhkv->bhcv", q_c, state) + jnp.einsum("bhij,bhjv->bhiv", attn_c, v_new)
        state = state * gl[..., None, None] + jnp.einsum("bhck,bhcv->bhkv", k_c, v_new)
        return state, o

    s0 = jnp.zeros(q.shape[1:3] + (q.shape[-1], v.shape[-1]), F32)
    _, o = lax.scan(step, s0, (attn, q_dec, k_dec, u, w, g_last))
    return _unchunks(o)

def _ssd_grouped(c, b, u, g):
    c, b, u, g = (_chunks(t.astype(F32)) for t in (c, b, u, g))
    gc = jnp.cumsum(g, axis=3)
    tril = jnp.tril(jnp.ones((CHUNK, CHUNK), dtype=bool))[:, :, None]
    seg = gc[:, :, :, :, None, :] - gc[:, :, :, None, :, :]
    decay = jnp.exp(jnp.where(tril, seg, -jnp.inf))
    scores = jnp.einsum("nbgis,nbgjs->nbgij", c, b)[..., None] * decay
    y_intra = jnp.einsum("nbgijr,nbgjrp->nbgirp", scores, u)

    def step(state, inp):
        c_c, b_c, u_c, gc_c = inp
        y = jnp.exp(gc_c)[..., None] * jnp.einsum("bgis,bgrsp->bgirp", c_c, state)
        g_last = gc_c[:, :, -1]
        u_dec = u_c * jnp.exp(g_last[:, :, None] - gc_c)[..., None]
        state = state * jnp.exp(g_last)[..., None, None] + jnp.einsum("bgjs,bgjrp->bgrsp", b_c, u_dec)
        return state, y

    s0 = jnp.zeros((c.shape[1], c.shape[2], u.shape[4], c.shape[4], u.shape[5]), F32)
    _, y_inter = lax.scan(step, s0, (c, b, u, gc))
    return _unchunks(y_intra + y_inter)

def _gla_chunked(q, k, v, g):
    q, k, v, g = (_chunks(t.astype(F32)) for t in (q, k, v, g))
    gc = jnp.cumsum(g, axis=3)
    tril = jnp.tril(jnp.ones((CHUNK, CHUNK), dtype=bool))[:, :, None]

    def step(state, inp):
        q_c, k_c, v_c, gc_c = inp
        seg = gc_c[:, :, :, None, :] - gc_c[:, :, None, :, :]
        decay = jnp.exp(jnp.where(tril, seg, -jnp.inf))
        attn = jnp.einsum("bhijk,bhjk->bhij", decay * q_c[:, :, :, None, :], k_c)
        g_last = gc_c[:, :, -1]
        o = (jnp.einsum("bhij,bhjv->bhiv", attn, v_c)
             + jnp.einsum("bhik,bhkv->bhiv", q_c * jnp.exp(gc_c), state))
        state = (state * jnp.exp(g_last)[..., None]
                 + jnp.einsum("bhjk,bhjv->bhkv", k_c * jnp.exp(g_last[:, :, None] - gc_c), v_c))
        return state, o

    s0 = jnp.zeros(q.shape[1:3] + (q.shape[-1], v.shape[-1]), F32)
    _, o = lax.scan(step, s0, (q, k, v, gc))
    return _unchunks(o)

def _gdn_mixer(x, w_in, conv_w, a_log, dt_bias, norm_w, w_out):
    bsz, seq, _ = x.shape
    qkv, z, ab = jnp.split(x @ w_in, [GDN_CONV_CH, GDN_CONV_CH + GDN_VAL_WIDTH], axis=-1)
    qkv = jax.nn.silu(_dwconv(qkv, conv_w))
    q, k, v = jnp.split(qkv, [GDN_KEY_WIDTH, 2 * GDN_KEY_WIDTH], axis=-1)
    rep = GDN_V_HEADS // GDN_QK_HEADS
    qk_shape = (bsz, seq, GDN_QK_HEADS, GDN_HEAD_DIM)
    q = jnp.repeat(_l2norm(q.reshape(qk_shape)), rep, axis=2) * GDN_HEAD_DIM ** -0.5
    k = jnp.repeat(_l2norm(k.reshape(qk_shape)), rep, axis=2)
    v = v.reshape(bsz, seq, GDN_V_HEADS, GDN_HEAD_DIM).astype(F32)
    ab = ab.astype(F32).reshape(bsz, seq, 2, 2, GDN_V_HEADS)
    g = -jnp.exp(a_log.astype(F32)) * jax.nn.softplus(ab[:, :, 0] + dt_bias.astype(F32))
    beta = jax.nn.sigmoid(ab[:, :, 1])
    o = (_gated_delta_rule(q, k, v, beta[:, :, 0], g[:, :, 0])
         + _rev(_gated_delta_rule(_rev(q), _rev(k), _rev(v), _rev(beta[:, :, 1]), _rev(g[:, :, 1]))))
    o = _rms(o) * norm_w.astype(F32) * jax.nn.silu(
        z.astype(F32).reshape(bsz, seq, GDN_V_HEADS, GDN_HEAD_DIM))
    return o.reshape(bsz, seq, GDN_VAL_WIDTH).astype(x.dtype) @ w_out

def _mamba2_mixer(x, w_in, conv_w, conv_b, a_log, dt_bias, d_skip, norm_w, w_out):
    bsz, seq, _ = x.shape
    z, xbc, dt = jnp.split(x @ w_in, [M2_D_INNER, M2_D_INNER + M2_CONV_CH], axis=-1)
    xbc = jax.nn.silu(_dwconv(xbc, conv_w) + conv_b).astype(F32)
    xs, b_in, c_out = jnp.split(xbc, [M2_D_INNER, M2_D_INNER + M2_GROUPS * M2_STATE], axis=-1)
    xs = xs.reshape(bsz, seq, M2_GROUPS, M2_HEADS_PER_GROUP, M2_HEAD_DIM)
    b_in = b_in.reshape(bsz, seq, M2_GROUPS, M2_STATE)
    c_out = c_out.reshape(bsz, seq, M2_GROUPS, M2_STATE)
    hshape = (2, M2_GROUPS, M2_HEADS_PER_GROUP)
    dt = jax.nn.softplus(dt.astype(F32).reshape(bsz, seq, *hshape) + dt_bias.astype(F32).reshape(hshape))
    g = -jnp.exp(a_log.astype(F32)).reshape(hshape) * dt
    u_f = xs * dt[:, :, 0, :, :, None]
    u_b = xs * dt[:, :, 1, :, :, None]
    y = (_ssd_grouped(c_out, b_in, u_f, g[:, :, 0])
         + _rev(_ssd_grouped(_rev(c_out), _rev(b_in), _rev(u_b), _rev(g[:, :, 1]))))
    y = y + d_skip.astype(F32).reshape(M2_GROUPS, M2_HEADS_PER_GROUP, 1) * xs
    y = y.reshape(bsz, seq, M2_GROUPS, -1) * jax.nn.silu(z.astype(F32).reshape(bsz, seq, M2_GROUPS, -1))
    y = _rms(y) * norm_w.astype(F32).reshape(M2_GROUPS, -1)
    return y.reshape(bsz, seq, M2_D_INNER).astype(x.dtype) @ w_out

def _hgrn2_mixer(x, w_in, lb, norm_w, w_out):
    bsz, seq, _ = x.shape
    hs = (bsz, seq, HG_HEADS, HG_EXPAND)
    q, f_fwd, f_bwd, i_in, gate = jnp.split((x @ w_in).astype(F32), 5, axis=-1)
    q = jax.nn.silu(q).reshape(hs)
    i_in = i_in.reshape(hs)
    lb = lb.reshape(HG_HEADS, HG_EXPAND)

    def forget(f):
        f = f.reshape(hs)
        log_f = jnp.logaddexp(jnp.log(lb), jnp.log1p(-lb) + jax.nn.log_sigmoid(f))
        return (1.0 - lb) * jax.nn.sigmoid(-f), log_f

    k_f, g_f = forget(f_fwd)
    k_b, g_b = forget(f_bwd)
    o = (_gla_chunked(q, k_f, i_in, g_f)
         + _rev(_gla_chunked(_rev(q), _rev(k_b), _rev(i_in), _rev(g_b))))
    o = _rms(o) * norm_w.astype(F32) * jax.nn.silu(gate.reshape(hs))
    return o.reshape(bsz, seq, HG_WIDTH).astype(x.dtype) @ w_out

def _gla_mixer(x, w_in, w_gk, b_gk, norm_w, w_out):
    bsz, seq, _ = x.shape
    splits = [GLA_KEY_WIDTH, 2 * GLA_KEY_WIDTH, 2 * GLA_KEY_WIDTH + GLA_VAL_WIDTH,
              2 * GLA_KEY_WIDTH + 2 * GLA_VAL_WIDTH]
    q, k, v, gate, r = jnp.split((x @ w_in).astype(F32), splits, axis=-1)
    ks = (bsz, seq, GLA_HEADS, GLA_K)
    vs = (bsz, seq, GLA_HEADS, GLA_V)
    q = q.reshape(ks) * GLA_K ** -0.5
    k = k.reshape(ks)
    v = v.reshape(vs)
    r = r.reshape(bsz, seq, 2, GLA_GATE_RANK)
    gk = jax.nn.log_sigmoid(jnp.einsum("blzr,zrk->blzk", r, w_gk.astype(F32))
                            + b_gk.astype(F32)) / GLA_GATE_TEMP
    g_f = gk[:, :, 0].reshape(ks)
    g_b = gk[:, :, 1].reshape(ks)
    o = (_gla_chunked(q, k, v, g_f)
         + _rev(_gla_chunked(_rev(q), _rev(k), _rev(v), _rev(g_b))))
    o = _rms(o) * norm_w.astype(F32) * jax.nn.silu(gate.reshape(vs))
    return o.reshape(bsz, seq, GLA_VAL_WIDTH).astype(x.dtype) @ w_out

def _hier_moe(x, w_group, b_group, w_router, b_router, w_gate, w_up, w_down):
    bsz, seq, d = x.shape
    xt = x.reshape(bsz * seq, d)
    g_logits = (xt @ w_group).astype(F32) + b_group.astype(F32)
    g_onehot = jax.nn.one_hot(jnp.argmax(g_logits, axis=-1), MOE_GROUPS, dtype=F32)
    g_prob = jnp.sum(jax.nn.softmax(g_logits, axis=-1) * g_onehot, axis=-1)
    e_logits = ((xt @ w_router).astype(F32) + b_router.astype(F32)).reshape(
        -1, MOE_GROUPS, MOE_EXPERTS_PER_GROUP)
    e_logits = jnp.einsum("tge,tg->te", e_logits, g_onehot)
    top_val, top_idx = lax.top_k(e_logits, MOE_TOPK)
    top_w = jax.nn.softmax(top_val, axis=-1) * g_prob[:, None]
    within = jnp.einsum("tk,tke->te", top_w,
                        jax.nn.one_hot(top_idx, MOE_EXPERTS_PER_GROUP, dtype=F32))
    comb = (g_onehot[:, :, None] * within[:, None, :]).astype(x.dtype)
    out = jnp.zeros_like(xt)
    for grp in range(MOE_GROUPS):
        h = (jax.nn.silu(jnp.einsum("td,edf->tef", xt, w_gate[grp]))
             * jnp.einsum("td,edf->tef", xt, w_up[grp]))
        out = out + jnp.einsum("tef,efd->td", h * comb[:, grp, :, None], w_down[grp])
    return out.reshape(bsz, seq, d)

def second_inputs(seed: int = 0) -> dict:
    key = jax.random.key(seed)
    ks = iter(jax.random.split(key, 48))

    def nrm(shape, scale):
        return jax.random.normal(next(ks), shape, F32) * scale

    def a_log(shape):
        return jnp.log(jax.random.uniform(next(ks), shape, F32, 1.0, 16.0))

    def dt_bias(shape):
        dt = jnp.exp(jax.random.uniform(next(ks), shape, F32, math.log(1e-3), math.log(1e-1)))
        return dt + jnp.log(-jnp.expm1(-dt))

    na, nb, nc, nd = (_n_uses(m) for m in range(N_MIXERS))
    D = D_MODEL
    sd = D ** -0.5
    beta = DEEPNORM_BETA
    return {
        "x": nrm((BATCH, SEQ, D), 1.0),
        "p": nrm((DEPTH_2, BATCH, SEQ, PLE_DIM), 1.0),
        "gdn_w_in": nrm((na, D, GDN_IN), sd),
        "gdn_conv_w": nrm((na, CONV_K, GDN_CONV_CH), CONV_K ** -0.5),
        "gdn_a_log": a_log((na, 2, GDN_V_HEADS)),
        "gdn_dt_bias": dt_bias((na, 2, GDN_V_HEADS)),
        "gdn_norm_w": 1.0 + nrm((na, GDN_HEAD_DIM), 0.02),
        "gdn_w_out": nrm((na, GDN_VAL_WIDTH, D), GDN_VAL_WIDTH ** -0.5 * beta),
        "m2_w_in": nrm((nb, D, M2_IN), sd),
        "m2_conv_w": nrm((nb, CONV_K, M2_CONV_CH), CONV_K ** -0.5),
        "m2_conv_b": nrm((nb, M2_CONV_CH), 0.02),
        "m2_a_log": a_log((nb, 2, M2_HEADS)),
        "m2_dt_bias": dt_bias((nb, 2, M2_HEADS)),
        "m2_d": 1.0 + nrm((nb, M2_HEADS), 0.1),
        "m2_norm_w": 1.0 + nrm((nb, M2_D_INNER), 0.02),
        "m2_w_out": nrm((nb, M2_D_INNER, D), M2_D_INNER ** -0.5 * beta),
        "hg_w_in": nrm((nc, D, HG_IN), sd),
        "hg_lb_logits": nrm((DEPTH_2, HG_WIDTH), 0.1),
        "hg_norm_w": 1.0 + nrm((nc, HG_EXPAND), 0.02),
        "hg_w_out": nrm((nc, HG_WIDTH, D), HG_WIDTH ** -0.5 * beta),
        "gla_w_in": nrm((nd, D, GLA_IN), sd),
        "gla_w_gk": nrm((nd, 2, GLA_GATE_RANK, GLA_KEY_WIDTH), GLA_GATE_RANK ** -0.5),
        "gla_b_gk": nrm((nd, 2, GLA_KEY_WIDTH), 0.1),
        "gla_norm_w": 1.0 + nrm((nd, GLA_V), 0.02),
        "gla_w_out": nrm((nd, GLA_VAL_WIDTH, D), GLA_VAL_WIDTH ** -0.5 * beta),
        "ln_g": 1.0 + nrm((DEPTH_2, 2, D), 0.02),
        "ln_b": nrm((DEPTH_2, 2, D), 0.02),
        "moe_w_group": nrm((DEPTH_2, D, MOE_GROUPS), sd),
        "moe_b_group": nrm((DEPTH_2, MOE_GROUPS), 0.01),
        "moe_w_router": nrm((DEPTH_2, D, MOE_EXPERTS), sd),
        "moe_b_router": nrm((DEPTH_2, MOE_EXPERTS), 0.01),
        "moe_w_gate": nrm((DEPTH_2, MOE_GROUPS, MOE_EXPERTS_PER_GROUP, D, MOE_HIDDEN), sd),
        "moe_w_up": nrm((DEPTH_2, MOE_GROUPS, MOE_EXPERTS_PER_GROUP, D, MOE_HIDDEN), sd),
        "moe_w_down": nrm((DEPTH_2, MOE_GROUPS, MOE_EXPERTS_PER_GROUP, MOE_HIDDEN, D),
                          MOE_HIDDEN ** -0.5 * beta),
        "pe_w_gate": nrm((DEPTH_2, D, D), sd),
        "pe_w_proj": nrm((DEPTH_2, PLE_DIM, D), PLE_DIM ** -0.5 * beta),
    }

def second_block(x, p, gdn_w_in, gdn_conv_w, gdn_a_log, gdn_dt_bias, gdn_norm_w, gdn_w_out,
              m2_w_in, m2_conv_w, m2_conv_b, m2_a_log, m2_dt_bias, m2_d, m2_norm_w, m2_w_out,
              hg_w_in, hg_lb_logits, hg_norm_w, hg_w_out,
              gla_w_in, gla_w_gk, gla_b_gk, gla_norm_w, gla_w_out,
              ln_g, ln_b, moe_w_group, moe_b_group, moe_w_router, moe_b_router,
              moe_w_gate, moe_w_up, moe_w_down, pe_w_gate, pe_w_proj):
    lb_all = jnp.cumsum(jax.nn.softmax(hg_lb_logits.astype(F32), axis=0), axis=0)
    lb_all = lb_all - lb_all[0]
    for i in range(DEPTH_2):
        m, j = i % N_MIXERS, i // N_MIXERS
        if m == 0:
            h = _gdn_mixer(x, gdn_w_in[j], gdn_conv_w[j], gdn_a_log[j], gdn_dt_bias[j],
                           gdn_norm_w[j], gdn_w_out[j])
        elif m == 1:
            h = _mamba2_mixer(x, m2_w_in[j], m2_conv_w[j], m2_conv_b[j], m2_a_log[j],
                              m2_dt_bias[j], m2_d[j], m2_norm_w[j], m2_w_out[j])
        elif m == 2:
            h = _hgrn2_mixer(x, hg_w_in[j], lb_all[i], hg_norm_w[j], hg_w_out[j])
        else:
            h = _gla_mixer(x, gla_w_in[j], gla_w_gk[j], gla_b_gk[j], gla_norm_w[j], gla_w_out[j])
        x = _layernorm(DEEPNORM_ALPHA * x + h, ln_g[i, 0], ln_b[i, 0])
        h = _hier_moe(x, moe_w_group[i], moe_b_group[i], moe_w_router[i], moe_b_router[i],
                      moe_w_gate[i], moe_w_up[i], moe_w_down[i])
        x = _layernorm(DEEPNORM_ALPHA * x + h, ln_g[i, 1], ln_b[i, 1])
        x = x + jax.nn.sigmoid(x @ pe_w_gate[i]) * (p[i].astype(x.dtype) @ pe_w_proj[i])
    return x


def setup_inputs(seed=0):
    out = dict(first_inputs(seed))
    for name, value in second_inputs(seed + 1).items():
        if name != "x":
            out[name + "_2"] = value
    return out


def reference(
    x, positions, attn_norm, w_qkv_a, w_o_a, kv_norm, w_kv_b, w_q_b, sinks_b, w_o_b, ffn_norm,
    w_up, conv_w, conv_b, w_down, final_norm, p_2, gdn_w_in_2, gdn_conv_w_2, gdn_a_log_2,
    gdn_dt_bias_2, gdn_norm_w_2, gdn_w_out_2, m2_w_in_2, m2_conv_w_2, m2_conv_b_2, m2_a_log_2,
    m2_dt_bias_2, m2_d_2, m2_norm_w_2, m2_w_out_2, hg_w_in_2, hg_lb_logits_2, hg_norm_w_2,
    hg_w_out_2, gla_w_in_2, gla_w_gk_2, gla_b_gk_2, gla_norm_w_2, gla_w_out_2, ln_g_2, ln_b_2,
    moe_w_group_2, moe_b_group_2, moe_w_router_2, moe_b_router_2, moe_w_gate_2, moe_w_up_2,
    moe_w_down_2, pe_w_gate_2, pe_w_proj_2,
):
    x = first_block(
        x, positions, attn_norm, w_qkv_a, w_o_a, kv_norm, w_kv_b, w_q_b, sinks_b, w_o_b,
        ffn_norm, w_up, conv_w, conv_b, w_down, final_norm,
    )
    return second_block(
        x, p_2, gdn_w_in_2, gdn_conv_w_2, gdn_a_log_2, gdn_dt_bias_2, gdn_norm_w_2, gdn_w_out_2,
        m2_w_in_2, m2_conv_w_2, m2_conv_b_2, m2_a_log_2, m2_dt_bias_2, m2_d_2, m2_norm_w_2,
        m2_w_out_2, hg_w_in_2, hg_lb_logits_2, hg_norm_w_2, hg_w_out_2, gla_w_in_2, gla_w_gk_2,
        gla_b_gk_2, gla_norm_w_2, gla_w_out_2, ln_g_2, ln_b_2, moe_w_group_2, moe_b_group_2,
        moe_w_router_2, moe_b_router_2, moe_w_gate_2, moe_w_up_2, moe_w_down_2, pe_w_gate_2,
        pe_w_proj_2,
    )


_drawn_inputs = setup_inputs


def setup_inputs(seed=0):
    import zlib

    import numpy as np

    out = dict(_drawn_inputs(seed))
    spreads = {}
    factors = {'attn_norm': 8.0,
     'kv_norm': 7.343,
     'sinks_b': 33.605,
     'ffn_norm': 3.127,
     'conv_b': 5.176,
     'gdn_norm_w_2': 16.321,
     'moe_b_group_2': 64.0,
     'moe_b_router_2': 21.67}
    for name, (base, spread) in spreads.items():
        noise = np.random.default_rng([zlib.crc32(name.encode()), seed]).standard_normal(out[name].shape)
        drawn = base * np.exp(spread * noise) if base else spread * noise
        out[name] = jnp.asarray(drawn.astype(out[name].dtype))
    for name, factor in factors.items():
        out[name] = (out[name] * factor).astype(out[name].dtype)
    return out
```

```python
from contextlib import ExitStack

import numpy as np

import concourse.bass as bass
from concourse import mybir

F32 = mybir.dt.float32
BF16 = mybir.dt.bfloat16
I32 = mybir.dt.int32
ALU = mybir.AluOpType
ACT = mybir.ActivationFunctionType
AX = mybir.AxisListType

P = 128
T = 256
TT = T // P
D = 1024
KT = D // P
HD = 64
ROT = 16
FF = 2816
FT = FF // P
GH = 8
GV = 16
EXPERTS = 32
HID = 256
GROUPS = 4
SLOT = 8 * 1024
UNIT = 2 * 1024
EPS = 1e-6
LN_EPS = 1e-5
ALPHA = 2.0 ** 0.25
NEG = -1e30
LEVELS = (2, 4, 8, 16, 32, 64)
CAP = 64
PAIRS = EXPERTS // 2
TWO_PI = 6.283185307179586
MAGIC = 12582912.0


def level_mask(s):
    r = np.arange(P)
    same = (r[:, None] // (2 * s)) == (r[None, :] // (2 * s))
    return (same & ((r[:, None] // s) % 2 == 1) & ((r[None, :] // s) % 2 == 0)).astype(np.float32)


def constant_columns():
    r = np.arange(P)
    le = (r[:, None] <= r[None, :]).astype(np.float32)
    neg_above = np.where(r[None, :] > r[:, None], NEG, 0.0)
    neg_below = np.where(r[None, :] <= r[:, None], NEG, 0.0)
    zero = np.zeros((P, P))
    parts = {
        "ident": np.eye(P),
        "ones": np.ones((P, P)),
        "le": le,
        "ge": le.T,
        "mask0": np.concatenate([neg_above, zero, neg_above], 1),
        "mask1": np.concatenate([neg_above, neg_below, neg_above], 1),
        "lim": np.concatenate([np.where(le > 0, 0.0, NEG), np.where(le.T > 0, 0.0, NEG)], 1),
        "first": np.concatenate([-level_mask(1).T, -level_mask(1)], 1),
        "levels": np.concatenate([m for s in LEVELS for m in (level_mask(s), level_mask(s).T)], 1),
        "freq": np.broadcast_to(500000.0 ** (-np.arange(0, ROT, 2, dtype=np.float32) / ROT), (P, ROT // 2)),
        "rank": np.broadcast_to(np.arange(8, 0, -1), (P, 8)),
        "eps": np.full((P, 1), EPS),
        "qscale": np.full((P, 1), np.log(0.5 * P ** -0.5)),
        "kscale": np.full((P, 1), np.log(0.5)),
        "lneps": np.full((P, 1), LN_EPS),
        "place": np.broadcast_to(np.arange(CAP), (P, CAP)),
        "place_col": (r % CAP)[:, None],
    }
    return {k: np.ascontiguousarray(v, dtype=np.float32) for k, v in parts.items()}


def constant_slices():
    at, out = 0, {}
    for k, v in constant_columns().items():
        out[k] = (at, at + v.shape[1])
        at += v.shape[1]
    return out, at


class Chain:

    def __init__(self, eng, sem):
        self.eng, self.sem = eng, sem
        self.base, self.start, self.per, self.k = 0, 0, 0, 0

    def loop(self, per):
        self.base, self.per, self.k = self.start + self.k, per, per

    def iteration(self, i):
        assert self.k == self.per, (self.k, self.per)
        self.start, self.k = self.base + self.per * i, 0

    def end(self, n, fewer=0):
        assert self.k == self.per - fewer, (self.k, self.per)
        self.start, self.k = self.base + n * self.per - fewer, 0

    def __call__(self, ins):
        self.k += 1
        ins.then_inc(self.sem, 1)
        self.eng.wait_ge(self.sem, self.start + self.k)


def in_pairs(eng, n, body):
    m = 2 * ((n - 1) // 2)
    if m:
        with eng.Fori(0, m, 2) as i:
            body(i, 0, True)
            body(i + 1, 1, True)
    for j in range(m, n):
        body(j, j % 2, j < n - 1)


def build(nc, a, consts, comb_dram, out, last=9):
    ctx = ExitStack()
    with ctx:
        def sb(name, shape, dt=F32):
            return ctx.enter_context(nc.sbuf_tensor(name, shape, dt))

        def sem(name):
            return ctx.enter_context(nc.semaphore(name))

        where, n_const = constant_slices()
        cst = sb("cst", [P, n_const])

        def const(name):
            lo, hi = where[name]
            return cst[:, lo:hi]

        ident, ones = const("ident"), const("ones")

        class Arena:

            def __init__(self, name, words):
                self.words, self.mem, self.at = words, sb(name, [P, words]), 0

            def again(self):
                self.at = 0

            def take(self, *shape):
                n = int(np.prod(shape))
                ap = self.mem[:, self.at:self.at + n]
                self.at += n
                assert self.at <= self.words, (self.at, self.words)
                names = "abcd"[:len(shape)]
                if len(shape) > 1:
                    ap = ap.rearrange(f"p ({' '.join(names)}) -> p {' '.join(names)}",
                                      **dict(zip(names[1:], shape[1:])))
                return ap

        W = sb("W", [P, 2, SLOT])
        xres = sb("xres", [P, TT, D])
        wide = Arena("wide", GV * T)
        xn = wide.take(TT, D)
        hT = sb("hT", [P, KT, T])
        hkT = wide.take(KT, T)
        wide.again()
        OT = wide.take(GV, T)
        cols = sb("cols", [P, 7, 96])
        sink = sb("sink", [P, 16])
        gain = sb("gain", [P, D])
        offset = sb("offset", [P, D])
        pos_i = sb("pos_i", [P, TT], I32)
        pos_f = sb("pos_f", [P, TT])
        ang = sb("ang", [P, 4, TT, ROT // 2])
        cos16 = sb("cos16", [P, TT, ROT])
        sin16 = sb("sin16", [P, TT, ROT])
        ss = sb("ss", [P, TT])
        rstd = sb("rstd", [P, TT])
        zeros = sb("zeros", [P, 512], BF16)
        work = Arena("work", 12416)
        rows = work.take(7, P)[0:96]
        AW = 448
        st = work.take(2, TT, AW)
        rt = work.take(2, TT, 6, ROT)
        qT = work.take(2, T)
        kT = work.take(T)
        SM = work.take(2, 386)
        PR = work.take(2, 386)
        nm = work.take(2, 2)
        rs = work.take(2, 2)
        rr = work.take(2, 2)
        PT = work.take(2, 384)
        oT = work.take(2, T)
        cg = work.take(2, 2, T)
        sg = work.take(2, T)
        aT = work.take(2, 2, T)
        cb = work.take(2, T)
        work.again()
        sel_in = work.take(TT, 2, CAP)
        xg = work.take(KT, 2 * CAP)
        sgr = work.take(HID)
        aS = work.take(HID)
        aR = work.take(2, 2 * CAP)
        yR = work.take(D)
        sel_out = work.take(T)
        rows_r = work.take(2, 2, T)
        wd_odd = work.take(2, 2, D)
        wide.again()
        wd_even = wide.take(2, 2, D)
        work.again()
        wab = sb("wab", [P, KT, 4 * GV])
        gate_in = sb("gate_in", [P, 6, TT, 2 * GV])
        dtb = sb("dtb", [P, 2 * GV])
        alog = sb("alog", [P, 2 * GV])
        gG = sb("gG", [P, TT, 2, GV])
        gB = sb("gB", [P, TT, 2, GV])
        gC = sb("gC", [P, TT, 2, GV])
        gE = sb("gE", [P, TT, 2, GV])
        gK = sb("gK", [P, TT, 2, GV])
        nwh = sb("nwh", [P, P])
        cq = sb("cq", [P, 4, T])
        th = sb("th", [P, 4, T])
        sq = sb("sq", [P, 2, T])
        lnq = sq
        kq = sb("kq", [P, TT, 2, P])
        zt = sb("zt", [P, TT, 2 * P])
        zs = zt
        zn = sb("zn", [P, TT, 2 * P])
        vtok = sb("vtok", [P, TT, 2, P])
        ktok = sb("ktok", [P, TT, P])
        gU = work.take(2, TT, 2, P)
        LG = work.take(2, TT, 2, P)
        DM = work.take(2, TT, 2, P)
        DB = LG
        QA = work.take(2, TT, 2, P)
        AM = work.take(2, TT, 2, P)
        XI = work.take(2, TT, 2, P)
        YI = work.take(2, TT, 2, P)
        GI = work.take(2, TT, 2, P)
        vn1 = work.take(TT, 2, P)
        vdec = work.take(TT, 2, P)
        vn2 = vdec
        Sst = work.take(2, 2, P)
        rb = work.take(TT, 2, P)
        qse = work.take(TT, 2, P)
        og = work.take(TT, 2, P)
        oss = sb("oss", [P, 4])
        osl = sb("osl", [P, 4])
        osr = sb("osr", [P, 4])
        wr = sb("wr", [P, KT, 36])
        br = sb("br", [P, 36])
        bst = sb("bst", [P, TT, 2, 6])
        mv = sb("mv", [P, TT, 2])
        lrs = sb("lrs", [P, TT])
        lg = sb("lg", [P, TT, 36])
        rA = sb("rA", [P, 16, TT])
        rB = sb("rB", [P, 8, TT, 8])
        goh = sb("goh", [P, TT, GROUPS])
        gex = sb("gex", [P, TT, GROUPS])
        sel = sb("sel", [P, TT, GROUPS, 8])
        comb = sb("comb", [P, TT, GROUPS, 8])
        chosen = sb("chosen", [P, TT, EXPERTS])
        place = sb("place", [P, TT, EXPERTS])
        most = sb("most", [P, 1])
        most_i = sb("most_i", [P, 1], I32)
        combT = sb("combT", [EXPERTS, 2, T])
        pt_in = sb("pt_in", [P, TT, 2 * P])
        pT = sb("pT", [P, 2, T])
        acc = ctx.enter_context(nc.psum_tensor("acc", [P, 4, 512], F32))
        wb = ctx.enter_context(nc.psum_tensor("wb", [P, 4, 512], F32))
        all_acc = [acc[:, b, :] for b in range(4)]

        def bcast(ap, axis, n):
            x = ap.unsqueeze(axis)
            shape = list(x.shape)
            shape[axis] = n
            return x.to_broadcast(shape)

        s_const, s_x, s_rows, s_vec, s_pos = (sem(n) for n in ("const", "x_in", "rows_in", "vec_in", "pos_in"))
        s_zero = sem("zeros_set")
        dve_chain, act_chain, pool_chain = sem("dve_chain"), sem("act_chain"), sem("pool_chain")
        s_colT, s_cols = sem("cols_transposed"), sem("cols_ready")
        s_ang, s_sin, s_rope = sem("angles_ready"), sem("sines_ready"), sem("rope_tables_ready")
        s_sum, s_ms, s_root, s_rstd = sem("squares_summed"), sem("mean_square"), sem("root"), sem("rstd_ready")
        s_xn, s_trn, s_hT = sem("xn_ready"), sem("xn_transposed"), sem("hT_ready")
        s_hTa = sem("hT_ready_act")
        s_acc, s_xres = sem("acc_done"), sem("xres_ready")
        s_out = sem("out_written")
        s_ln = sem("layernorm_vectors_in")

        class Stage:

            def __init__(self, name, n, front_loads, back_loads, counts, like=None):
                self.n, self.front_loads, self.back_loads, self.counts = n, front_loads, back_loads, counts
                self.before = {**{k: 0 for k in counts}, "front_in": [0, 0], "back_in": [0, 0]}
                if like is None:
                    self.before["used"] = 1
                    self.front_in = [sem(f"{name}_front_loaded{s}") for s in range(2)]
                    self.back_in = [sem(f"{name}_back_loaded{s}") for s in range(2)]
                    return
                self.front_in, self.back_in = like.front_in, like.back_in
                old = like.before
                self.before = {k: old[k] + like.counts[k] * like.n for k in like.counts}
                uses = [(like.n + 1) // 2, like.n // 2]
                self.before["front_in"] = [old["front_in"][s] + 16 * like.front_loads * uses[s] for s in range(2)]
                self.before["back_in"] = [old["back_in"][s] + 16 * like.back_loads * uses[s] for s in range(2)]

            def front_loaded(self, eng, i, s):
                half = i // 2 if isinstance(i, int) else (i - s) // 2
                eng.wait_ge(self.front_in[s], self.before["front_in"][s] + 16 * self.front_loads * (half + 1))

            def back_loaded(self, eng, i, s):
                half = i // 2 if isinstance(i, int) else (i - s) // 2
                eng.wait_ge(self.back_in[s], self.before["back_in"][s] + 16 * self.back_loads * (half + 1))

        att = []
        for l, (n, pairs) in enumerate(((8, 1), (4, 2))):
            once = ("proj", "copied", "roped", "heads_transposed", "qT_ready", "kT_ready", "used")
            by_pair = ("scored", "probs_transposed", "pt_ready_act", "pt_ready_dve", "pv", "oT_ready")
            counts = {**{k: 1 for k in once}, **{k: pairs for k in by_pair},
                      "max_ready": 2 * pairs, "exped": 4 * pairs, "normed": 4 * pairs}
            att.append(Stage(f"att{l}", n, 3 + l, 1, counts, att[0] if l else None))
            att[l].pairs = pairs
        for g in att:
            first = g is att[0]
            g.proj = sem("att_proj") if first else att[0].proj
            g.copied = sem("att_copied") if first else att[0].copied
            g.roped = sem("att_roped") if first else att[0].roped
            g.heads_transposed = sem("att_heads_transposed") if first else att[0].heads_transposed
            g.qT_ready = sem("att_qT_ready") if first else att[0].qT_ready
            g.kT_ready = sem("att_kT_ready") if first else att[0].kT_ready
            g.scored = sem("att_scored") if first else att[0].scored
            g.max_ready = sem("att_max_ready") if first else att[0].max_ready
            g.exped = sem("att_exped") if first else att[0].exped
            g.normed = sem("att_normed") if first else att[0].normed
            g.probs_transposed = sem("att_probs_transposed") if first else att[0].probs_transposed
            g.pt_ready_act = sem("att_pt_ready_act") if first else att[0].pt_ready_act
            g.pt_ready_dve = sem("att_pt_ready_dve") if first else att[0].pt_ready_dve
            g.pv = sem("att_pv") if first else att[0].pv
            g.oT_ready = sem("att_oT_ready") if first else att[0].oT_ready
            g.used = sem("att_used") if first else att[0].used
        ffn = []
        for name, n in (("ffn0", FT // 2), ("ffn1", FT // 2), ("moe", EXPERTS)):
            counts = {"up": 2, "first": 4, "conv": 2, "silu": 2, "act": 2, "used": 1}
            ffn.append(Stage(name, n, 2, 2 if name == "moe" else 1, counts, ffn[-1] if ffn else None))
        for g in ffn:
            first = g is ffn[0]
            g.up = sem("ffn_up") if first else ffn[0].up
            g.first = sem("ffn_first") if first else ffn[0].first
            g.conv = sem("ffn_conv") if first else ffn[0].conv
            g.silu = sem("ffn_silu") if first else ffn[0].silu
            g.act = sem("ffn_act") if first else ffn[0].act
            g.used = sem("ffn_used") if first else ffn[0].used
        moe = ffn[2]

        gd = Stage("gdn", GH, 4, 1, {})
        gd.fronts = sem("gdn_projected")
        (gd.gates_in, gd.gates_added, gd.gates_exp, gd.gates_set, gd.gates_summed, gd.gates_ready) = (
            sem(f"gdn_gates_{n}") for n in ("projected", "added", "exp", "set", "summed", "ready"))
        gd.qk, gd.v, gd.z = sem("gdn_qk_projected"), sem("gdn_v_projected"), gd.fronts
        (gd.first, gd.taps, gd.tanh, gd.silu, gd.ztanh, gd.zsilu, gd.zready, gd.sq) = (
            sem(f"gdn_{n}") for n in ("first_tap", "taps", "tanh", "silu", "z_tanh", "z_silu", "z_ready", "squared"))
        (gd.ss, gd.vt, gd.row, gd.qkr, gd.kq, gd.vtok, gd.gu, gd.lgr, gd.expo, gd.decay) = (
            sem(f"gdn_{n}") for n in ("norms_summed", "v_transposed", "rows_summed", "norms_ready", "kq_ready",
                                      "vtok_ready", "gU_ready", "LG_ready", "exponent_ready", "decay_ready"))
        (gd.kk, gd.kt, gd.ktok, gd.db, gd.am, gd.y2, gd.x2t, gd.x2) = (
            sem(f"gdn_{n}") for n in ("products", "k_transposed", "ktok_ready", "decay_beta_ready",
                                      "matrix_ready", "first_inverse_T", "first_transposed",
                                      "first_inverse"))
        (gd.g, gd.gev, gd.xg, gd.xev, gd.t, gd.yev) = (
            sem(f"gdn_{n}") for n in ("level_row", "level_row_ready", "level_product", "level_inverse_ready",
                                      "level_transposed", "level_inverse_T_ready"))
        (gd.r1, gd.vn1, gd.vdec, gd.s, gd.sev, gd.ks, gd.rb, gd.qse, gd.r2, gd.vn2, gd.o, gd.osum, gd.orms,
         gd.on, gd.ot, gd.OT) = (
            sem(f"gdn_{n}") for n in ("first_solved", "vn1_ready", "vdec_ready", "state", "state_ready",
                                      "state_products", "rhs_ready", "state_out_ready", "second_solved", "vn2_ready",
                                      "output", "output_ready", "output_rms", "output_gated",
                                      "output_transposed", "OT_ready"))
        s_wout = [sem(f"w_out_loaded{s}") for s in range(2)]
        s_mixed = sem("gdn_output_projected")
        s_added, s_lnroot, s_lnvar = sem("ln_input_ready"), sem("ln_root"), sem("ln_var")
        s_small = sem("small_weights_in")
        rt_pe, rt_dve, rt_act = sem("router_tensor"), sem("router_vector"), sem("router_scalar")
        RT_LOGITS, RT_COUNTED, RT_TRANSPOSED = 1, 2, 3
        RT_GROUP_SHIFTED, RT_PAIR_DIFFERENCE, RT_COMB, RT_CHOSEN, RT_PLACES = 1, 2, 3, 4, 5
        RT_GROUP_EXP, RT_PAIR_EXP = 1, 2
        s_most, s_combT, s_comb_out = (sem(f"router_{n}") for n in ("most_ready", "combT_ready", "comb_stored"))
        s_moe_done = sem("experts_done")
        (r_sel, r_gath, r_xa, r_xd, r_up, r_silu, r_act, r_turned, r_aR, r_down, r_selout, r_ya, r_yd) = (
            sem(f"routed_{n}") for n in ("sel_in_ready", "gathered", "xg_ready_act", "xg_ready_dve", "up", "silu",
                                         "act", "act_transposed", "aR_ready", "down", "sel_out_ready",
                                         "y_ready_act", "y_ready_dve"))
        r_front = [sem(f"routed_front_loaded{s}") for s in range(2)]
        r_back = [sem(f"routed_back_loaded{s}") for s in range(2)]
        ple_pe, ple_act, s_wpe, s_prod = (sem(f"ple_{n}") for n in ("tensor", "scalar", "weights_in", "result"))

        def view(s, unit, shape):
            n = shape[0] * shape[1]
            return W[:, s, unit:unit + n].rearrange("p (a b) -> p a b", a=shape[0])

        def w_gate(s):
            return view(s, 0, (KT, 256))

        def w_up(s):
            return view(s, UNIT, (KT, 256))

        def w_down(s):
            return view(s, 2 * UNIT, (2, D))

        def w_both(s, x):
            return W[:, s, 2 * x * UNIT:(2 * x + 2) * UNIT].rearrange("p (h k c) -> p k h c", h=2, k=KT)

        def w_down_of(s):
            return wd_odd if s else wd_even

        def w_z(s):
            return view(s, 2 * UNIT, (KT, 256))

        def w_out(s):
            return view(s, 0, (8, D))

        def w_heads(l, s):
            return view(s, 0, (KT, 384 if l == 0 else 448))

        def w_o(l, s):
            return view(s, KT * 448, (l + 1, D))

        order = [att[0], ffn[0], att[1], ffn[1], ffn[2]]

        block = ctx.enter_context(nc.Block())


        @block.sync
        def _(sp):
            sp.sem_inc(att[0].used, 1)
            sp.sem_inc(ffn[0].used, 1)

            def stage(k, g, fronts, fronts_before, per, load_front, load_back):
                for j in range(2):
                    if k:
                        prev = order[k - 1]
                        sp.wait_ge(prev.used, prev.before["used"] + prev.n - (prev.n - 1 - j) % 2)
                    load_front(j, j)
                    load_back(j, j)

                def later(i, s, _more):
                    sp.wait_ge(fronts, fronts_before + per * (i + 1))
                    load_front(i + 2, s)
                    sp.wait_ge(g.used, g.before["used"] + i + 1)
                    load_back(i + 2, s)

                in_pairs(sp, g.n - 2, later)

            def heads(l):
                g = att[l]
                w = a["w_qkv_a"][0] if l == 0 else a["w_q_b"][0]
                wo = a["w_o_a"][0] if l == 0 else a["w_o_b"][0]
                hw = 128 if l == 0 else 256

                def front(i, s):
                    dst = w_heads(l, s)
                    src = w.rearrange("(k p) c -> p k c", p=P)
                    if l == 0:
                        for part in range(3):
                            sp.dma_start(dst[:, :, part * P:(part + 1) * P],
                                         src[:, :, bass.ds(i * P + part * D, P)])\
                                .then_inc(g.front_in[s], 16)
                    else:
                        kv = a["w_kv_b"].rearrange("(k p) c -> p k c", p=P)
                        sp.dma_start(dst[:, :, 0:256], src[:, :, bass.ds(i * 256, 256)])\
                            .then_inc(g.front_in[s], 16)
                        for c in range(2):
                            sp.dma_start(dst[:, :, 256 + c * HD:256 + (c + 1) * HD],
                                         kv[:, :, bass.ds(i * HD, HD)]).then_inc(g.front_in[s], 16)
                        sp.dma_start(dst[:, :, 384:448], kv[:, :, bass.ds(i * HD + 256, HD)])\
                            .then_inc(g.front_in[s], 16)

                def back(i, s):
                    sp.dma_start(w_o(l, s), wo[bass.ds(i * hw, hw), :].rearrange("(f p) n -> p f n", p=P))\
                        .then_inc(g.back_in[s], 16)
                return front, back

            def feed(l):
                g = ffn[l]
                up = a["w_up"][l].rearrange("(k p) c -> p k c", p=P)

                def front(i, s):
                    sp.dma_start(w_gate(s), up[:, :, bass.ds(i * 256, 256)]).then_inc(g.front_in[s], 16)
                    sp.dma_start(w_up(s), up[:, :, bass.ds(i * 256 + FF, 256)]).then_inc(g.front_in[s], 16)

                def back(i, s):
                    sp.dma_start(w_down(s), a["w_down"][l][bass.ds(i * 256, 256), :]
                                 .rearrange("(f p) n -> p f n", p=P)).then_inc(g.back_in[s], 16)
                return front, back

            stage(0, att[0], att[0].proj, att[0].before["proj"], 1, *heads(0))
            if last >= 2:
                stage(1, ffn[0], ffn[0].up, ffn[0].before["up"], 2, *feed(0))
            if last >= 3:
                stage(2, att[1], att[1].proj, att[1].before["proj"], 1, *heads(1))
            if last >= 4:
                stage(3, ffn[1], ffn[1].up, ffn[1].before["up"], 2, *feed(1))
            def ln_vectors(c, version):
                sp.wait_ge(s_xres, 2 * version)
                sp.dma_start(gain[:], a["ln_g_2"][0, c:c + 1, :].to_broadcast([P, D])).then_inc(s_ln, 16)
                sp.dma_start(offset[:], a["ln_b_2"][0, c:c + 1, :].to_broadcast([P, D])).then_inc(s_ln, 16)

            if last >= 6:
                w_in = a["gdn_w_in_2"][0].rearrange("(k p) c -> p k c", p=P)

                def gfront(i, s):
                    for half, lo in ((0, 0), (1, D)):
                        sp.dma_start(w_gate(s)[:, :, half * P:(half + 1) * P], w_in[:, :, bass.ds(i * P + lo, P)])\
                            .then_inc(gd.front_in[s], 16)
                    sp.dma_start(w_up(s), w_in[:, :, bass.ds(i * 256 + 2 * D, 256)]).then_inc(gd.front_in[s], 16)
                    sp.dma_start(w_z(s), w_in[:, :, bass.ds(i * 256 + 4 * D, 256)]).then_inc(gd.front_in[s], 16)

                for j in range(2):
                    sp.wait_ge(ffn[1].used, ffn[1].before["used"] + ffn[1].n - (ffn[1].n - 1 - j) % 2)
                    gfront(j, j)

                def glater(i, s, _more):
                    sp.wait_ge(gd.fronts, i + 1)
                    gfront(i + 2, s)

                ln_vectors(0, 5)
                in_pairs(sp, GH - 2, glater)
                for s in range(2):
                    sp.wait_ge(gd.fronts, GH - 1 + s)
                    sp.dma_start(w_out(s), a["gdn_w_out_2"][0][s * D:(s + 1) * D, :]
                                 .rearrange("(f p) n -> p f n", p=P)).then_inc(s_wout[s], 16)
            if last >= 8:
                wg, wu, wd = (a[f"moe_w_{n}_2"][0].rearrange("g e r c -> (g e) r c") for n in ("gate", "up", "down"))

                def mfront(i, s):
                    for dst, w in ((w_gate(s), wg), (w_up(s), wu)):
                        sp.dma_start(dst, w[bass.ds(i, 1)].rearrange("e (k p) c -> p (e k) c", p=P))\
                            .then_inc(moe.front_in[s], 16)

                def mdown(i, s):
                    sp.dma_start(w_down(s), wd[bass.ds(i, 1)].rearrange("e (f p) n -> p (e f) n", p=P))\
                        .then_inc(moe.back_in[s], 16)

                def mcomb(i, s):
                    sp.dma_start(cb[:, s, :], comb_dram[bass.ds(i, 1), 0, :].to_broadcast([P, T]))\
                        .then_inc(moe.back_in[s], 16)

                def rfront(j, s):
                    for x in range(2):
                        for half, w in enumerate((wg, wu)):
                            sp.dma_start(w_both(s, x)[:, :, half, :],
                                         w[bass.ds(2 * j + x, 1)].rearrange("e (k p) c -> p (e k) c", p=P))\
                                .then_inc(r_front[s], 16)

                def rdown(j, s):
                    for x in range(2):
                        sp.dma_start(w_down_of(s)[:, x],
                                     wd[bass.ds(2 * j + x, 1)].rearrange("e (f p) n -> p (e f) n", p=P))\
                            .then_inc(r_back[s], 16)

                def rrows(j, s):
                    for x in range(2):
                        sp.dma_start(rows_r[x * CAP:(x + 1) * CAP, s],
                                     comb_dram[bass.ds(2 * j + x, 1)].to_broadcast([CAP, 2, T]))\
                            .then_inc(r_back[s], 16)

                def ple_gate(half):
                    sp.dma_start(W[:, 0, half * 4 * D:(half + 1) * 4 * D].rearrange("p (k n) -> p k n", k=4),
                                 a["pe_w_gate_2"][0].rearrange("(k p) n -> p k n", p=P)[:, half * 4:half * 4 + 4, :])\
                        .then_inc(s_wpe, 16)

                def ple_proj():
                    sp.dma_start(view(1, 0, (2, D)), a["pe_w_proj_2"][0].rearrange("(k p) n -> p k n", p=P))\
                        .then_inc(s_wpe, 16)

                sp.wait_ge(s_mixed, 1)
                for j in range(2):
                    rfront(j, j)
                    rdown(j, j)
                sp.wait_ge(s_combT, 1)
                sp.dma_start(comb_dram, combT[:]).then_inc(s_comb_out, 16)
                sp.wait_ge(s_comb_out, 16)
                ln_vectors(1, 6)

                def routed_later(j, s, _more):
                    sp.wait_ge(r_up, j + 1)
                    rfront(j + 2, s)
                    sp.wait_ge(r_selout, j + 1)
                    rrows(j + 2, s)
                    sp.wait_ge(r_down, 2 * j + 2)
                    rdown(j + 2, s)

                def mlater(i, s, _more):
                    sp.wait_ge(moe.up, moe.before["up"] + 2 * i + 2)
                    mfront(i + 2, s)
                    sp.wait_ge(moe.used, moe.before["used"] + i + 1)
                    mdown(i + 2, s)
                    mcomb(i + 2, s)

                sp.wait_ge(s_most, 1)
                with sp.If(sp.value_load(most_i[0:1, 0:1]) < CAP + 1):
                    for j in range(2):
                        rrows(j, j)
                    in_pairs(sp, PAIRS - 2, routed_later)
                    sp.wait_ge(r_up, PAIRS - 1)
                    for half in range(2):
                        ple_gate(half)
                    sp.wait_ge(r_up, PAIRS)
                    ple_proj()
                with sp.Else():
                    for j in range(2):
                        sp.wait_ge(r_front[j], 64)
                        sp.wait_ge(r_back[j], 32)
                    for j in range(2):
                        mfront(j, j)
                        mdown(j, j)
                        mcomb(j, j)
                    in_pairs(sp, EXPERTS - 2, mlater)
                    sp.wait_ge(s_moe_done, 1)
                    for half in range(2):
                        ple_gate(half)
                    ple_proj()
            if last >= 9:
                for t in range(TT):
                    sp.wait_ge(s_prod, t + 1)
                    sp.dma_start(out[0, t * P:(t + 1) * P, :], xn[:, t, :]).then_inc(s_out, 16)
                sp.wait_ge(s_out, 32)
            else:
                if last == 6:
                    sp.wait_ge(s_added, 2)
                else:
                    sp.wait_ge(s_xres, 2 * {5: 5, 7: 6, 8: 7}.get(last, last))
                sp.dma_start(out.rearrange("a (t p) n -> p (a t) n", p=P), xres[:]).then_inc(s_out, 16)
                sp.wait_ge(s_out, 16)

        @block.tensor
        def _(pe):
            pe.wait_ge(s_const, 16)
            pe.wait_ge(s_rows, ROW_LOADS * 16)
            for n, r in enumerate(ROW_TILES):
                ins = pe.transpose(wb[:, n // 4, (n % 4) * 128:(n % 4) * 128 + r], rows[0:r, n, :],
                                   ident[0:r, 0:r])
            ins.then_inc(s_colT, 1)

            def transpose_norm(c):
                if c == 0:
                    pe.wait_ge(s_cols, 1)
                pe.wait_ge(s_xn, 2 * (c + 1))
                for b in range(4):
                    for j in range(2):
                        for t in range(TT):
                            ins = pe.transpose(wb[:, b, (2 * j + t) * P:(2 * j + t + 1) * P],
                                               xn[:, t, (2 * b + j) * P:(2 * b + j + 1) * P], ident)
                    ins.then_inc(s_trn, 1)

            def clear_acc(c):
                if c == 0:
                    pe.wait_ge(s_zero, 1)
                else:
                    pe.wait_ge(s_xres, 2 * c)
                for b in range(4):
                    pe.matmul(all_acc[b], zeros[:, 0:P], zeros[:], start=True, stop=False, skip_group_check=True)

            def heads(l, c):
                g = att[l]
                kcol, vcol = g.pairs * P, g.pairs * P + P

                def proj(i, s, q):
                    t, half = q // 2, q % 2
                    if q == 0:
                        if not isinstance(i, int) or i > 0:
                            pe.wait_ge(g.copied, g.before["copied"] + i)
                        g.front_loaded(pe, i, s)
                    w = w_heads(l, s)
                    for k in range(4 * half, 4 * half + 4):
                        tok = slice(t * P, (t + 1) * P)
                        if l == 0:
                            ins = pe.matmul(wb[:, t, 0:384], hT[:, k, tok], w[:, k, :],
                                            start=k == 0, stop=k == KT - 1)
                        else:
                            ins = pe.matmul(wb[:, t, 0:256], hT[:, k, tok], w[:, k, 0:256],
                                            start=k == 0, stop=k == KT - 1)
                    if l == 1 and half == 1:
                        for k in range(KT):
                            ins = pe.matmul(wb[:, t, 256:448], hkT[:, k, tok], w[:, k, 256:448],
                                            start=k == 0, stop=k == KT - 1)
                    if q == 3:
                        ins.then_inc(g.proj, 1)

                def body(i, s, more):
                    chunks = list(range(4)) if more else []

                    def fill():
                        if chunks:
                            proj(i + 1, 1 - s, chunks.pop(0))

                    pe.wait_ge(g.roped, g.before["roped"] + i + 1)
                    for p in range(g.pairs):
                        for t in range(TT):
                            pe.transpose(wb[:, 2, (2 * p + t) * P:(2 * p + t + 1) * P],
                                         st[:, s, t, p * P:(p + 1) * P], ident)
                    for t in range(TT):
                        ins = pe.transpose(wb[:, 3, t * P:(t + 1) * P], st[:, s, t, kcol:kcol + P], ident)
                    ins.then_inc(g.heads_transposed, 1)
                    fill()
                    for p in range(g.pairs):
                        m = g.pairs * i + p
                        if p == 0:
                            pe.wait_ge(g.qT_ready, g.before["qT_ready"] + i + 1)
                            pe.wait_ge(g.kT_ready, g.before["kT_ready"] + i + 1)
                        else:
                            pe.wait_ge(g.oT_ready, g.before["oT_ready"] + m)
                        for h in range(2):
                            rw = slice(h * HD, (h + 1) * HD)
                            pe.matmul(wb[:, 2 + h, 0:P], qT[rw, p, 0:P], kT[rw, 0:P], start=True, stop=True)
                            ins = pe.matmul(wb[:, 2 + h, P:3 * P], qT[rw, p, P:T], kT[rw, :], start=True, stop=True)
                        ins.then_inc(g.scored, 1)
                        fill()
                        pe.wait_ge(g.normed, g.before["normed"] + 4 * (m + 1))
                        for h in range(2):
                            pe.transpose(wb[:, 2 + h, 0:P], PR[:, h, 0:P], ident)
                            pe.transpose(wb[:, 2 + h, P:2 * P], PR[:, h, 129:257], ident)
                            ins = pe.transpose(wb[:, 2 + h, 2 * P:3 * P], PR[:, h, 257:385], ident)
                        ins.then_inc(g.probs_transposed, 1)
                        fill()
                        pe.wait_ge(g.pt_ready_act, g.before["pt_ready_act"] + m + 1)
                        pe.wait_ge(g.pt_ready_dve, g.before["pt_ready_dve"] + m + 1)
                        for h in range(2):
                            v = slice(vcol + h * HD, vcol + (h + 1) * HD) if l == 0 else slice(vcol, vcol + HD)
                            rw = slice(h * HD, (h + 1) * HD)
                            pe.matmul(wb[rw, 2, 0:T], st[:, s, 0, v], PT[:, h, 0:T], start=True, stop=False,
                                      skip_group_check=True)
                            ins = pe.matmul(wb[rw, 2, P:T], st[:, s, 1, v], PT[:, h, T:T + P], start=False,
                                            stop=True, skip_group_check=True)
                        ins.then_inc(g.pv, 1)
                    while chunks:
                        fill()
                    pe.wait_ge(g.oT_ready, g.before["oT_ready"] + g.pairs * (i + 1))
                    g.back_loaded(pe, i, s)
                    for f in range(g.pairs):
                        for t in range(TT):
                            for n in range(2):
                                ins = pe.matmul(all_acc[2 * t + n], oT[:, f, t * P:(t + 1) * P],
                                                w_o(l, s)[:, f, n * 512:(n + 1) * 512],
                                                start=False, stop=False, skip_group_check=True)
                    ins.then_inc(g.used, 1)

                pe.wait_ge(s_hT, 4 * (c + 1) + (4 if l else 0))
                pe.wait_ge(s_hTa, 4 * (c + 1) + (4 if l else 0))
                for q in range(4):
                    proj(0, 0, q)
                clear_acc(c)
                in_pairs(pe, g.n, body)

            def feed(k, c):
                g = ffn[k]

                def up(i, s):
                    g.front_loaded(pe, i, s)
                    for f in range(2):
                        bank = 2 * s + f
                        for half, w in enumerate((w_gate(s), w_up(s))):
                            for kt in range(KT):
                                ins = pe.matmul(wb[:, bank, half * T:(half + 1) * T],
                                                w[:, kt, f * P:(f + 1) * P], hT[:, kt, :],
                                                start=kt == 0, stop=kt == KT - 1)
                        ins.then_inc(g.up, 1)

                def body(i, s, more):
                    if more:
                        up(i + 1, 1 - s)
                    g.back_loaded(pe, i, s)
                    for f in range(2):
                        pe.wait_ge(g.act, g.before["act"] + 2 * i + f + 1)
                        for t in range(TT):
                            for n in range(2):
                                ins = pe.matmul(all_acc[2 * t + n], aT[:, s, f, t * P:(t + 1) * P],
                                                w_down(s)[:, f, n * 512:(n + 1) * 512],
                                                start=False, stop=False, skip_group_check=True)
                    ins.then_inc(g.used if k < 2 or more else s_moe_done, 1)

                if k < 2:
                    pe.wait_ge(s_hT, 4 * (c + 1) + (4 if c > 1 else 0))
                    pe.wait_ge(s_hTa, 4 * (c + 1) + (4 if c > 1 else 0))
                    clear_acc(c)
                    up(0, 0)
                else:
                    clear_acc(c)
                    up(0, 0)
                in_pairs(pe, g.n, body)

            def transpose_res(c, need):
                pe.wait_ge(s_xres, 2 * need)
                for b in range(4):
                    for j in range(2):
                        for t in range(TT):
                            ins = pe.transpose(wb[:, b, (2 * j + t) * P:(2 * j + t + 1) * P],
                                               xres[:, t, (2 * b + j) * P:(2 * b + j + 1) * P], ident)
                    ins.then_inc(s_trn, 1)

            def hT_plain(c):
                pe.wait_ge(s_hT, 20 + 2 * (c + 1))
                pe.wait_ge(s_hTa, 20 + 2 * (c + 1))

            def delta_rule():
                def problems():
                    return [(t, v) for t in range(TT) for v in range(2)]

                def col(ap, t, v):
                    return ap[:, (2 * t + v) * P:(2 * t + v + 1) * P]

                hT_plain(0)
                pe.wait_ge(s_small, 16 * SMALL_LOADS)
                for t in range(TT):
                    for k in range(KT):
                        ins = pe.matmul(acc[:, 0, t * 64:(t + 1) * 64], hT[:, k, t * P:(t + 1) * P], wab[:, k, :],
                                        start=k == 0, stop=k == KT - 1)
                ins.then_inc(gd.gates_in, 1)
                pe.wait_ge(gd.gates_set, 1)
                for t in range(TT):
                    for d, m in ((0, const("le")), (1, const("ge"))):
                        pe.matmul(acc[:, 1, (2 * t + d) * GV:(2 * t + d + 1) * GV], m, gG[:, t, d, :],
                                  start=True, stop=True)
                    ins = pe.matmul(acc[:, 1, 64 + t * 32:64 + (t + 1) * 32], ones,
                                    gG[:, t].rearrange("p d h -> p (d h)"), start=True, stop=True)
                ins.then_inc(gd.gates_summed, 1)

                def proj(i, s, q):
                    tile, half = q // 2, q % 2
                    if q == 0:
                        gd.front_loaded(pe, i, s)
                        if not isinstance(i, int) or i > 0:
                            pe.wait_ge(gd.taps, 4 * i)
                            pe.wait_ge(gd.zsilu, i)
                    for k in range(4 * half, 4 * half + 4):
                        if tile < 4:
                            w = w_gate(s) if tile < 2 else w_up(s)
                            ins = pe.matmul(wb[:, tile // 2, tile % 2 * T:(tile % 2 + 1) * T],
                                            w[:, k, tile % 2 * P:(tile % 2 + 1) * P], hT[:, k, :],
                                            start=k == 0, stop=k == KT - 1)
                        else:
                            t = tile - 4
                            ins = pe.matmul(wb[:, 2, t * T:(t + 1) * T], hT[:, k, t * P:(t + 1) * P],
                                            w_z(s)[:, k, :], start=k == 0, stop=k == KT - 1)
                    if q in (3, 7, 11):
                        ins.then_inc({3: gd.qk, 7: gd.v, 11: gd.z}[q], 1)

                def body(i, s, more):
                    chunks = list(range(12)) if more else []

                    def fill(n):
                        for _ in range(n):
                            if chunks:
                                proj(i + 1, 1 - s, chunks.pop(0))

                    pe.wait_ge(gd.sq, i + 1)
                    pe.matmul(acc[:, 0, :], ones, sq[:].rearrange("p a b -> p (a b)"), start=True, stop=True)\
                        .then_inc(gd.ss, 1)
                    pe.wait_ge(gd.silu, 4 * (i + 1))
                    for t, v in problems():
                        ins = pe.transpose(col(acc[:, 1, :], t, v), cq[:, 2 + v, t * P:(t + 1) * P], ident)
                    ins.then_inc(gd.vt, 1)
                    for d in range(2):
                        pe.wait_ge(gd.gu, 2 * i + d + 1)
                        pe.matmul(acc[:, 2 + d, :], ones, gU[:, d].rearrange("p t v c -> p (t v c)"),
                                  start=True, stop=True).then_inc(gd.row, 1)
                    fill(1)
                    pe.wait_ge(gd.kq, 2 * (i + 1))
                    for t in range(TT):
                        ins = pe.matmul(wb[:, 3, t * T:(t + 1) * T], kq[:, t, 0, :],
                                        kq[:, t].rearrange("p a b -> p (a b)"), start=True, stop=True)
                    ins.then_inc(gd.kk, 1)
                    for t in range(TT):
                        ins = pe.transpose(acc[:, 0, t * P:(t + 1) * P], kq[:, t, 0, :], ident)
                    ins.then_inc(gd.kt, 1)
                    fill(2)
                    for d in range(2):
                        pe.wait_ge(gd.y2, 2 * i + d + 1)
                        pe.wait_ge(gd.expo, 2 * i + d + 1)
                        for t, v in problems():
                            ins = pe.transpose(col(acc[:, 2 + d, :], t, v), YI[:, d, t, v, :], ident)
                        ins.then_inc(gd.x2t, 1)
                    fill(1)
                    for n in range(len(LEVELS)):
                        end = n == len(LEVELS) - 1
                        for d in range(2):
                            if n == 0:
                                pe.wait_ge(gd.x2, 2 * i + d + 1)
                                if d == 0:
                                    pe.wait_ge(gd.ktok, i + 1)
                                    pe.wait_ge(gd.vtok, i + 1)
                            else:
                                pe.wait_ge(gd.yev, 10 * i + 2 * (n - 1) + d + 1)
                            for t, v in problems():
                                ins = pe.matmul(col(acc[:, d, :], t, v), AM[:, d, t, v, :], XI[:, d, t, v, :],
                                                start=True, stop=True)
                            ins.then_inc(gd.g, 1)
                        fill(1)
                        for d in range(2):
                            pe.wait_ge(gd.gev, 12 * i + 2 * n + d + 1)
                            for t, v in problems():
                                if end:
                                    ins = pe.matmul(col(acc[:, 2 + d, :], t, v), GI[:, d, t, v, :],
                                                    YI[:, d, t, v, :], start=True, stop=True)
                                else:
                                    ins = pe.matmul(col(acc[:, 2 + d, :], t, v), YI[:, d, t, v, :],
                                                    GI[:, d, t, v, :], start=True, stop=True)
                            ins.then_inc(gd.xg, 1)
                        if end:
                            break
                        fill(1)
                        for d in range(2):
                            pe.wait_ge(gd.xev, 12 * i + 2 * n + d + 1)
                            for t, v in problems():
                                ins = pe.transpose(col(acc[:, d, :], t, v), XI[:, d, t, v, :], ident)
                            ins.then_inc(gd.t, 1)
                    fill(12)
                    pe.wait_ge(gd.xev, 12 * (i + 1))
                    for t, v in problems():
                        ins = pe.matmul(col(acc[:, 0, :], t, v), YI[:, t, t, v, :], vtok[:, t, v, :],
                                        start=True, stop=True)
                    ins.then_inc(gd.r1, 1)
                    pe.wait_ge(gd.vdec, i + 1)
                    for t in range(TT):
                        ins = pe.matmul(acc[:, 1, t * T:(t + 1) * T], ktok[:, t, :],
                                        vdec[:, t].rearrange("p v c -> p (v c)"), start=True, stop=True)
                    ins.then_inc(gd.s, 1)
                    pe.wait_ge(gd.sev, i + 1)
                    for which in range(2):
                        for t in range(TT):
                            ins = pe.matmul(acc[:, 2 + which, t * T:(t + 1) * T], kq[:, t, which, :],
                                            Sst[:, 1 - t].rearrange("p v c -> p (v c)"), start=True, stop=True)
                        ins.then_inc(gd.ks, 1)
                    pe.wait_ge(gd.rb, i + 1)
                    for t, v in problems():
                        ins = pe.matmul(col(acc[:, 0, :], t, v), YI[:, 1 - t, t, v, :], rb[:, t, v, :],
                                        start=True, stop=True)
                    ins.then_inc(gd.r2, 1)
                    pe.wait_ge(gd.vn2, i + 1)
                    for t, v in problems():
                        pe.matmul(col(acc[:, 1, :], t, v), QA[:, t, t, v, :], vn1[:, t, v, :],
                                  start=True, stop=False)
                        ins = pe.matmul(col(acc[:, 1, :], t, v), QA[:, 1 - t, t, v, :], vn2[:, t, v, :],
                                        start=False, stop=True)
                    ins.then_inc(gd.o, 1)
                    pe.wait_ge(gd.on, i + 1)
                    for v in range(2):
                        for t in range(TT):
                            ins = pe.transpose(acc[:, 2, (2 * v + t) * P:(2 * v + t + 1) * P], og[:, t, v, :], ident)
                    ins.then_inc(gd.ot, 1)
                    pe.wait_ge(gd.OT, i + 1)

                for q in range(12):
                    proj(0, 0, q)
                pe.wait_ge(gd.gates_ready, 1)
                in_pairs(pe, GH, body)
                for f in range(GV):
                    if f % 8 == 0:
                        pe.wait_ge(s_wout[f // 8], 16)
                    for t in range(TT):
                        for n in range(2):
                            ins = pe.matmul(all_acc[2 * t + n], OT[:, f, t * P:(t + 1) * P],
                                            w_out(f // 8)[:, f % 8, n * 512:(n + 1) * 512],
                                            start=f == 0, stop=f == GV - 1)
                ins.then_inc(s_mixed, 1)

            def experts():
                hT_plain(1)
                for t in range(TT):
                    for k in range(KT):
                        ins = pe.matmul(acc[:, 0, t * 36:(t + 1) * 36], hT[:, k, t * P:(t + 1) * P], wr[:, k, :],
                                        start=k == 0, stop=k == KT - 1)
                ins.then_inc(rt_pe, 1)

            def route():
                pe.wait_ge(rt_dve, RT_COMB)
                for t in range(TT):
                    ins = pe.transpose(acc[0:EXPERTS, 1, t * P:(t + 1) * P],
                                       comb[:, t].rearrange("p g e -> p (g e)"), ident)
                pe.wait_ge(rt_dve, RT_CHOSEN)
                for t in range(TT):
                    for tile in range(t + 1):
                        pe.matmul(acc[:, 2, t * EXPERTS:(t + 1) * EXPERTS], const("le") if tile == t else ones,
                                  chosen[:, tile, :], start=tile == 0, stop=tile == t)
                for tile in range(TT):
                    ins = pe.matmul(acc[:, 2, TT * EXPERTS:(TT + 1) * EXPERTS], ones, chosen[:, tile, :],
                                    start=tile == 0, stop=tile == TT - 1)
                ins.then_inc(rt_pe, 1)
                pe.wait_ge(rt_dve, RT_PLACES)
                for t in range(TT):
                    ins = pe.transpose(acc[0:EXPERTS, 1, T + t * P:T + (t + 1) * P], place[:, t, :], ident)
                ins.then_inc(rt_pe, 1)
                pe.wait_ge(s_combT, 1)
                pe.wait_ge(s_most, 1)

            def routed():
                def gather(j, half):
                    for k in range(4 * half, 4 * half + 4):
                        for t in range(TT):
                            ins = pe.matmul(wb[:, half, (k % 4) * P:(k % 4 + 1) * P],
                                            xres[:, t, k * P:(k + 1) * P],
                                            sel_in[:, t].rearrange("p x c -> p (x c)"),
                                            start=t == 0, stop=t == TT - 1)
                    ins.then_inc(r_gath, 1)

                def body(j, s, more):
                    half = j // 2 if isinstance(j, int) else (j - s) // 2
                    pe.wait_ge(r_xa, j + 1)
                    pe.wait_ge(r_xd, j + 1)
                    pe.wait_ge(r_front[s], 64 * (half + 1))
                    for k in range(KT):
                        for x in range(2):
                            ins = pe.matmul(wb[x * CAP:(x + 1) * CAP, 2, :].rearrange("p (h c) -> p h c", h=2),
                                            xg[:, k, x * CAP:(x + 1) * CAP], w_both(s, x)[:, k],
                                            start=k == 0, stop=k == KT - 1)
                    ins.then_inc(r_up, 1)
                    if more:
                        pe.wait_ge(r_sel, j + 2)
                        gather(j + 1, 0)
                    pe.wait_ge(r_act, j + 1)
                    for f in range(2):
                        ins = pe.transpose(wb[:, 3, f * P:(f + 1) * P], aS[:, f * P:(f + 1) * P], ident)
                    ins.then_inc(r_turned, 1)
                    if more:
                        gather(j + 1, 1)
                    pe.wait_ge(r_aR, j + 1)
                    pe.wait_ge(r_back[s], 64 * (half + 1))
                    for h in range(2):
                        for f in range(2):
                            for x in range(2):
                                ins = pe.matmul(wb[x * CAP:(x + 1) * CAP, 2 + h, :],
                                                aR[:, f, x * CAP:(x + 1) * CAP],
                                                w_down_of(s)[:, x, f, h * 512:(h + 1) * 512],
                                                start=f == 0, stop=f == 1)
                        ins.then_inc(r_down, 1)
                    pe.wait_ge(r_selout, j + 1)
                    for h, ready in enumerate((r_ya, r_yd)):
                        pe.wait_ge(ready, j + 1)
                        for t in range(TT):
                            ins = pe.matmul(all_acc[2 * t + h], sel_out[:, t * P:(t + 1) * P],
                                            yR[:, h * 512:(h + 1) * 512],
                                            start=False, stop=False, skip_group_check=True)
                    if not more:
                        ins.then_inc(s_moe_done, 1)

                clear_acc(6)
                pe.wait_ge(r_sel, 1)
                for half in range(2):
                    gather(0, half)
                in_pairs(pe, PAIRS, body)

            transpose_norm(0)
            heads(0, 0)
            if last >= 2:
                transpose_norm(1)
                feed(0, 1)
            if last >= 3:
                transpose_norm(2)
                heads(1, 2)
            if last >= 4:
                transpose_norm(3)
                feed(1, 3)
            if last >= 6:
                transpose_res(0, 5)
                delta_rule()
            if last >= 8:
                transpose_res(1, 6)
                experts()
                route()
                with pe.If(pe.value_load(most_i[0:1, 0:1]) < CAP + 1):
                    routed()
                with pe.Else():
                    feed(2, 6)
            if last >= 9:
                for k in range(2):
                    for t in range(TT):
                        ins = pe.transpose(wb[:, 0, (2 * k + t) * P:(2 * k + t + 1) * P],
                                           pt_in[:, t, k * P:(k + 1) * P], ident)
                ins.then_inc(ple_pe, 1)
                pe.wait_ge(ple_act, 1)
                transpose_res(2, 7)
                hT_plain(2)
                pe.wait_ge(s_wpe, 48)
                for t in range(TT):
                    for n in range(2):
                        for k in range(KT):
                            pe.matmul(all_acc[2 * t + n], hT[:, k, t * P:(t + 1) * P],
                                      W[:, 0, k * D + n * 512:k * D + (n + 1) * 512],
                                      start=k == 0, stop=k == KT - 1)
                        for k in range(2):
                            ins = pe.matmul(wb[:, 2 * t + n, :], pT[:, k, t * P:(t + 1) * P],
                                            view(1, 0, (2, D))[:, k, n * 512:(n + 1) * 512],
                                            start=k == 0, stop=k == 1)
                    ins.then_inc(ple_pe, 1)

        @block.scalar
        def _(act):
            link = Chain(act, act_chain)
            act.wait_ge(s_ang, 1)
            act.activation(sin16[:, :, 8:16], ang[:, 0], ACT.Sin).then_inc(s_sin, 1)
            act.activation(cos16[:, :, 0:8], ang[:, 0], ACT.Sin, scale=0.5).then_inc(s_sin, 1)

            def squares(c, normalise=True):
                act.wait_ge(s_xres, 2 * c) if c else act.wait_ge(s_x, 16)
                if c:
                    act.wait_ge(s_trn, 4 * c)
                for t in range(TT):
                    act.activation(xn[:, t, :], xres[:, t, :], ACT.Square, accum_out=ss[:, t:t + 1])\
                        .then_inc(s_sum, 1)
                act.wait_ge(s_ms, c + 1)
                act.activation(rstd[:], ss[:], ACT.Sqrt).then_inc(s_root, 1)
                if not normalise:
                    return
                act.wait_ge(s_rstd, c + 1)
                act.activation(xn[:, 1, :], xres[:, 1, :], ACT.Copy, scale=rstd[:, 1:2]).then_inc(s_xn, 1)

            def evac_norm(c, gains):
                act.wait_ge(s_cols, 1)
                for b in (1, 3):
                    act.wait_ge(s_trn, 4 * c + b + 1)
                    for k in (2 * b, 2 * b + 1):
                        for dst, base in gains:
                            act.activation(dst[:, k, :], wb[:, b, k % 2 * T:(k % 2 + 1) * T], ACT.Copy,
                                           scale=cols[:, 0, base + k:base + k + 1]).then_inc(s_hTa, 1)

            def heads(l):
                g = att[l]
                width = 384 if l == 0 else 448

                def body(i, s, more):
                    act.wait_ge(g.proj, g.before["proj"] + i + 1)
                    act.activation(st[:, s, :, 0:width], wb[:, 0:2, 0:width], ACT.Copy).then_inc(g.copied, 1)
                    act.wait_ge(g.heads_transposed, g.before["heads_transposed"] + i + 1)
                    act.activation(qT[:, 0:g.pairs, :], wb[:, 2, 0:g.pairs * T].rearrange("p (a b) -> p a b", b=T),
                                   ACT.Copy, scale=HD ** -0.5).then_inc(g.qT_ready, 1)
                    for p in range(g.pairs):
                        m = g.pairs * i + p
                        act.wait_ge(g.max_ready, g.before["max_ready"] + 2 * (m + 1))
                        w0 = 128 + l
                        for h in range(2):
                            for q, (lo, hi) in enumerate(((0, w0), (129, 385 + l))):
                                act.activation(PR[:, h, lo:hi], SM[:, h, lo:hi], ACT.Exp, bias=nm[:, q, h:h + 1],
                                               accum_out=rs[:, h, q:q + 1]).then_inc(g.exped, 1)
                        act.wait_ge(g.probs_transposed, g.before["probs_transposed"] + m + 1)
                        act.activation(PT[:, 0, :], wb[:, 2, 0:384], ACT.Copy).then_inc(g.pt_ready_act, 1)
                        act.wait_ge(g.pv, g.before["pv"] + m + 1)
                        act.activation(oT[:, p, :], wb[:, 2, 0:T], ACT.Copy).then_inc(g.oT_ready, 1)

                in_pairs(act, g.n, body)

            def feed(l):
                g = ffn[l]
                w2, bias = cols[:, 2 + 2 * l, 0:2 * FT], cols[:, 2 + 2 * l, 2 * FT:4 * FT]

                def body(i, s, more):
                    for f in range(2):
                        act.wait_ge(g.up, g.before["up"] + 2 * i + f + 1)
                        for half in range(2):
                            col = 2 * i + f + half * FT
                            act.activation(cg[:, f, half, :], wb[:, 2 * s + f, half * T:(half + 1) * T],
                                           ACT.Identity, bias=bias[:, bass.ds(col, 1)],
                                           scale=w2[:, bass.ds(col, 1)]).then_inc(g.first, 1)
                    for f in range(2):
                        act.wait_ge(g.conv, g.before["conv"] + 2 * i + f + 1)
                        act.activation(sg[:, f, :], cg[:, f, 0, :], ACT.Silu).then_inc(g.silu, 1)
                    act.wait_ge(g.act, g.before["act"] + 2 * (i + 1))

                in_pairs(act, g.n, body)

            def evac_plain(c):
                for b in (1, 3):
                    act.wait_ge(s_trn, 16 + 4 * c + b + 1)
                    act.activation(hT[:, 2 * b:2 * b + 2, :], wb[:, b, :].rearrange("p (a b) -> p a b", a=2),
                                   ACT.Copy).then_inc(s_hTa, 1)

            def delta_rule():
                act.wait_ge(gd.gates_added, 1)
                act.activation(gate_in[:, 3], gate_in[:, 2], ACT.Exp).then_inc(gd.gates_exp, 1)
                act.activation(gate_in[:, 4], gate_in[:, 1], ACT.Exp, scale=-1.0).then_inc(gd.gates_exp, 1)
                act.wait_ge(s_small, 16 * SMALL_LOADS)
                act.activation(alog[:], alog[:], ACT.Exp).then_inc(gd.gates_exp, 1)
                act.wait_ge(gd.gates_exp, 3)
                act.activation(gate_in[:, 5], gate_in[:, 3], ACT.Ln, bias=ones[:, 0:1]).then_inc(gd.gates_exp, 1)
                act.wait_ge(gd.gates_summed, 1)
                link(act.activation(gC[:].rearrange("p t d h -> p (t d h)"), acc[:, 1, 0:64], ACT.Copy))
                act.activation(gE[:], gC[:], ACT.Exp).then_inc(gd.gates_exp, 1)
                act.wait_ge(gd.gates_added, 2)
                act.activation(gK[:], gK[:], ACT.Exp).then_inc(gd.gates_exp, 1)

                def first(i, s, tile):
                    bank = wb[:, tile // 2, tile % 2 * T:(tile % 2 + 1) * T]
                    act.activation(cq[:, tile, :], bank, ACT.Copy,
                                   scale=cols[:, 5, bass.ds(tap_col(2, tile, i), 1)]).then_inc(gd.first, 1)

                def tanh(i, tile):
                    act.wait_ge(gd.taps, 4 * i + tile + 1)
                    act.activation(th[:, tile, :], cq[:, tile, :], ACT.Tanh, scale=0.5).then_inc(gd.tanh, 1)

                def ztanh(i):
                    act.wait_ge(gd.z, i + 1)
                    if not isinstance(i, int) or i > 0:
                        act.wait_ge(gd.zready, i)
                    act.activation(zt[:], wb[:, 2, :].rearrange("p (t c) -> p t c", t=TT), ACT.Tanh, scale=0.5)\
                        .then_inc(gd.ztanh, 1)

                def front(i, s, step):
                    if step == 0:
                        act.wait_ge(gd.qk, i + 1)
                        act.wait_ge(gd.kq, 2 * i) if not isinstance(i, int) or i > 0 else None
                        first(i, s, 0)
                        first(i, s, 1)
                    elif step == 1:
                        tanh(i, 0)
                    elif step == 2:
                        tanh(i, 1)
                        act.wait_ge(gd.v, i + 1)
                        act.wait_ge(gd.vt, i) if not isinstance(i, int) or i > 0 else None
                        first(i, s, 2)
                        first(i, s, 3)
                    elif step == 3:
                        tanh(i, 2)
                    elif step == 4:
                        tanh(i, 3)
                        ztanh(i)
                        act.wait_ge(gd.silu, 4 * i + 2)
                        act.activation(sq[:], cq[:, 0:2, :], ACT.Square).then_inc(gd.sq, 1)

                def body(i, s, more):
                    link.iteration(i)
                    act.wait_ge(gd.ss, i + 1)
                    link(act.activation(lnq[:], acc[:, 0, :].rearrange("p (a b) -> p a b", a=2), ACT.Ln, scale=0.25,
                                        bias=const("eps")))
                    act.activation(lnq[:, 0], lnq[:, 0], ACT.Exp, scale=-0.5, bias=const("qscale"))\
                        .then_inc(gd.qkr, 1)
                    act.activation(lnq[:, 1], lnq[:, 1], ACT.Exp, scale=-0.5, bias=const("kscale"))\
                        .then_inc(gd.qkr, 1)
                    act.wait_ge(gd.vt, i + 1)
                    act.activation(vtok[:].rearrange("p t v c -> p (t v c)"), acc[:, 1, :], ACT.Copy, scale=0.5)\
                        .then_inc(gd.vtok, 1)
                    for d in range(2):
                        act.wait_ge(gd.expo, 2 * i + d + 1)
                        act.activation(DM[:, d], DM[:, d], ACT.Exp).then_inc(gd.decay, 1)
                    act.wait_ge(gd.kt, i + 1)
                    act.activation(ktok[:].rearrange("p t c -> p (t c)"), acc[:, 0, 0:T], ACT.Copy)\
                        .then_inc(gd.ktok, 1)
                    for d in range(2):
                        act.wait_ge(gd.x2t, 2 * i + d + 1)
                        act.activation(XI[:, d].rearrange("p t v c -> p (t v c)"), acc[:, 2 + d, :], ACT.Copy)\
                            .then_inc(gd.x2, 1)
                    for n in range(len(LEVELS) - 1):
                        for d in range(2):
                            act.wait_ge(gd.t, 10 * i + 2 * n + d + 1)
                            act.activation(YI[:, d].rearrange("p t v c -> p (t v c)"), acc[:, d, :], ACT.Copy)\
                                .then_inc(gd.yev, 1)
                        if more:
                            front(i + 1, 1 - s, n)
                    act.wait_ge(gd.s, i + 1)
                    act.activation(Sst[:].rearrange("p d v c -> p (d v c)"), acc[:, 1, :], ACT.Copy)\
                        .then_inc(gd.sev, 1)
                    act.wait_ge(gd.osum, 2 * (i + 1))
                    for n, (t, v) in enumerate((t, v) for t in range(TT) for v in range(2)):
                        link(act.activation(rb[:, t, v, :], og[:, t, v, :], ACT.Square, accum_out=oss[:, n:n + 1]))
                    link(act.activation(osl[:], oss[:], ACT.Ln, scale=1.0 / P, bias=const("eps")))
                    act.activation(osr[:], osl[:], ACT.Exp, scale=-0.5).then_inc(gd.orms, 1)
                    act.wait_ge(gd.ot, i + 1)
                    act.activation(OT[:, bass.ds(2 * i, 2), :], acc[:, 2, :].rearrange("p (v c) -> p v c", v=2),
                                   ACT.Copy).then_inc(gd.OT, 1)

                for step in range(5):
                    front(0, 0, step)
                link.loop(6)
                in_pairs(act, GH, body)
                link.end(GH)

            def layernorm(c):
                act.wait_ge(s_lnvar, c + 1)
                act.activation(lrs[:], mv[:, :, 1], ACT.Sqrt, bias=const("lneps")).then_inc(s_lnroot, 1)

            def experts():
                g = moe
                act.wait_ge(rt_dve, RT_GROUP_SHIFTED)
                act.activation(gex[:], gex[:], ACT.Exp).then_inc(rt_act, 1)
                act.wait_ge(rt_dve, RT_PAIR_DIFFERENCE)
                act.activation(rA[:, 9, :], rA[:, 8, :], ACT.Exp).then_inc(rt_act, 1)
                act.wait_ge(rt_pe, RT_TRANSPOSED)
                act.activation(combT[:], acc[0:EXPERTS, 1, :].rearrange("p (a b) -> p a b", a=2), ACT.Copy)\
                    .then_inc(s_combT, 1)

                def gathered(j):
                    act.wait_ge(r_gath, 2 * j + 1)
                    act.activation(xg[:, 0:4, :].rearrange("p k c -> p (k c)"), wb[:, 0, :], ACT.Copy)\
                        .then_inc(r_xa, 1)

                def routed(j, s, more):
                    act.wait_ge(r_up, j + 1)
                    act.activation(sgr, wb[:, 2, 0:HID], ACT.Silu).then_inc(r_silu, 1)
                    if more:
                        gathered(j + 1)
                    act.wait_ge(r_turned, j + 1)
                    act.activation(aR.rearrange("p f c -> p (f c)"), wb[:, 3, 0:2 * P], ACT.Copy).then_inc(r_aR, 1)
                    act.wait_ge(r_down, 2 * j + 1)
                    act.activation(yR[:, 0:512], wb[:, 2, :], ACT.Copy).then_inc(r_ya, 1)

                def body(i, s, more):
                    for f in range(2):
                        act.wait_ge(g.up, g.before["up"] + 2 * i + f + 1)
                        act.activation(sg[:, f, :], wb[:, 2 * s + f, 0:T], ACT.Silu).then_inc(g.silu, 1)
                    act.wait_ge(g.act, g.before["act"] + 2 * (i + 1))

                act.wait_ge(s_most, 1)
                with act.If(act.value_load(most_i[0:1, 0:1]) < CAP + 1):
                    gathered(0)
                    in_pairs(act, PAIRS, routed)
                with act.Else():
                    in_pairs(act, g.n, body)

            squares(0)
            evac_norm(0, [(hT, 0)])
            heads(0)
            if last >= 2:
                squares(1)
                evac_norm(1, [(hT, 24)])
                feed(0)
            if last >= 3:
                squares(2)
                evac_norm(2, [(hT, 8), (hkT, 16)])
                heads(1)
            if last >= 4:
                squares(3)
                evac_norm(3, [(hT, 32)])
                feed(1)
            if last >= 5:
                squares(4, normalise=False)
            if last >= 6:
                evac_plain(0)
                delta_rule()
            if last >= 7:
                layernorm(0)
            if last >= 8:
                evac_plain(1)
                experts()
                layernorm(1)
            if last >= 9:
                act.wait_ge(ple_pe, 1)
                act.activation(pT[:], wb[:, 0, :].rearrange("p (a b) -> p a b", a=2), ACT.Copy).then_inc(ple_act, 1)
                evac_plain(2)
                for t in range(TT):
                    act.wait_ge(ple_pe, t + 2)
                    act.activation(xn[:, t, :].rearrange("p (n c) -> p n c", n=2), acc[:, 2 * t:2 * t + 2, :],
                                   ACT.Sigmoid).then_inc(ple_act, 1)

        @block.vector
        def _(dve):
            link = Chain(dve, dve_chain)
            dve.memset(zeros[:], 0.0).then_inc(s_zero, 1)
            dve.wait_ge(s_const, 16)
            dve.wait_ge(s_pos, 16)
            link(dve.tensor_copy(pos_f[:], pos_i[:]))
            link(dve.tensor_tensor(ang[:, 0], bcast(pos_f[:], 2, 8), bcast(const("freq"), 1, TT), ALU.mult))
            link(dve.tensor_scalar(ang[:, 1], ang[:, 0], 1.0 / TWO_PI, MAGIC, ALU.mult, ALU.add))
            link(dve.tensor_scalar(ang[:, 2], ang[:, 1], -MAGIC, None, ALU.add))
            for part in TWO_PI_PARTS:
                link(dve.scalar_tensor_tensor(ang[:, 0], ang[:, 2], -part, ang[:, 0], ALU.mult, ALU.add))
            dve.tensor_scalar(ang[:, 0], ang[:, 0], 3.1415925, -3.1415925, ALU.min, ALU.max).then_inc(s_ang, 1)
            dve.wait_ge(s_colT, 1)
            link(dve.memset(cols[:, 0:1, 40:96], 0.0))
            for n, r in enumerate(ROW_TILES):
                ins = dve.tensor_copy(cols[:, n, 0:r], wb[:, n // 4, (n % 4) * P:(n % 4) * P + r])
            ins.then_inc(s_cols, 1)
            dve.wait_ge(s_sin, 2)
            link(dve.tensor_tensor(cos16[:, :, 8:16], cos16[:, :, 0:8], cos16[:, :, 0:8], ALU.mult))
            link(dve.tensor_scalar(cos16[:, :, 0:8], cos16[:, :, 8:16], -2.0, 1.0, ALU.mult, ALU.add))
            link(dve.tensor_copy(cos16[:, :, 8:16], cos16[:, :, 0:8]))
            link(dve.tensor_scalar(sin16[:, :, 0:8], sin16[:, :, 8:16], -1.0, None, ALU.mult))

            def rms(c):
                dve.wait_ge(s_sum, 2 * (c + 1))
                dve.tensor_scalar(ss[:], ss[:], 1.0 / D, EPS, ALU.mult, ALU.add).then_inc(s_ms, 1)
                dve.wait_ge(s_root, c + 1)
                dve.reciprocal(rstd[:], rstd[:]).then_inc(s_rstd, 1)
                dve.wait_ge(s_rstd, c + 1)
                dve.tensor_scalar(xn[:, 0, :], xres[:, 0, :], rstd[:, 0:1], None, ALU.mult).then_inc(s_xn, 1)

            def evac_norm(c, gains):
                dve.wait_ge(s_cols, 1)
                for b in (0, 2):
                    dve.wait_ge(s_trn, 4 * c + b + 1)
                    for k in (2 * b, 2 * b + 1):
                        for dst, base in gains:
                            dve.tensor_scalar(dst[:, k, :], wb[:, b, k % 2 * T:(k % 2 + 1) * T],
                                              cols[:, 0, base + k:base + k + 1], None, ALU.mult).then_inc(s_hT, 1)

            def add_acc(c, g):
                dve.wait_ge(g.used, g.before["used"] + g.n)
                for t in range(TT):
                    dve.tensor_tensor(xres[:, t, :].rearrange("p (n c) -> p n c", n=2), acc[:, 2 * t:2 * t + 2, :],
                                      xres[:, t, :].rearrange("p (n c) -> p n c", n=2), ALU.add)\
                        .then_inc(s_xres, 1)

            def heads(l):
                g = att[l]
                nh = 2 * g.pairs + 2
                mask = const(f"mask{l}")
                per = 3 + g.pairs * (3 + l)

                def body(i, s, more):
                    link.iteration(i)
                    dve.wait_ge(g.copied, g.before["copied"] + i + 1)
                    sv = st[:, s, :, 0:nh * HD].rearrange("p t (h e) -> p t h e", e=HD)
                    c16, s16 = bcast(cos16[:], 2, nh), bcast(sin16[:], 2, nh)
                    link(dve.tensor_tensor(rt[:, 0, :, 0:nh, :], sv[:, :, :, 0:ROT], c16, ALU.mult))
                    link(dve.tensor_tensor(rt[:, 1, :, 0:nh, 0:8], sv[:, :, :, 8:16], s16[:, :, :, 0:8], ALU.mult))
                    link(dve.tensor_tensor(rt[:, 1, :, 0:nh, 8:16], sv[:, :, :, 0:8], s16[:, :, :, 8:16], ALU.mult))
                    dve.tensor_tensor(sv[:, :, :, 0:ROT], rt[:, 0, :, 0:nh, :], rt[:, 1, :, 0:nh, :], ALU.add)\
                        .then_inc(g.roped, 1)
                    dve.wait_ge(g.heads_transposed, g.before["heads_transposed"] + i + 1)
                    dve.tensor_copy(kT[:], wb[:, 3, 0:T]).then_inc(g.kT_ready, 1)
                    for p in range(g.pairs):
                        m = g.pairs * i + p
                        dve.wait_ge(g.scored, g.before["scored"] + m + 1)
                        link(dve.tensor_tensor(SM[:, :, 0:P], wb[:, 2:4, 0:P], bcast(mask[:, 0:P], 1, 2), ALU.add))
                        link(dve.tensor_tensor(SM[:, :, 129:385], wb[:, 2:4, P:3 * P],
                                               bcast(mask[:, P:3 * P], 1, 2), ALU.add))
                        if l:
                            link(dve.tensor_copy(SM[:, :, 128:386:257],
                                                 bcast(sink[:, bass.ds(2 * m, 2)], 2, 2)))
                        for q, (lo, hi) in enumerate(((0, 128 + l), (129, 385 + l))):
                            dve.tensor_reduce(nm[:, q, :], SM[:, :, lo:hi], AX.X, ALU.max, negate=True)\
                                .then_inc(g.max_ready, 1)
                        dve.wait_ge(g.exped, g.before["exped"] + 4 * (m + 1))
                        link(dve.reciprocal(rr[:], rs[:]))
                        for h in range(2):
                            for q, (lo, hi) in enumerate(((0, 128), (129, 385))):
                                dve.tensor_scalar(PR[:, h, lo:hi], PR[:, h, lo:hi], rr[:, h, q:q + 1], None,
                                                  ALU.mult).then_inc(g.normed, 1)
                        dve.wait_ge(g.probs_transposed, g.before["probs_transposed"] + m + 1)
                        dve.tensor_copy(PT[:, 1, :], wb[:, 3, 0:384]).then_inc(g.pt_ready_dve, 1)

                link.loop(per)
                in_pairs(dve, g.n, body)
                link.end(g.n)

            def feed(l):
                g = ffn[l]
                taps = [cols[:, 1 + 2 * l, j * 2 * FT:(j + 1) * 2 * FT] for j in range(2)]

                def body(i, s, more):
                    link.iteration(i)
                    for f in range(2):
                        dve.wait_ge(g.first, g.before["first"] + 4 * i + 2 * f + 2)
                        for half in range(2):
                            col = 2 * i + f + half * FT
                            u = wb[:, 2 * s + f, half * T:(half + 1) * T]
                            c = cg[:, f, half, :]
                            link(dve.scalar_tensor_tensor(c[:, 1:T], u[:, 0:T - 1], taps[1][:, bass.ds(col, 1)],
                                                          c[:, 1:T], ALU.mult, ALU.add))
                            ins = dve.scalar_tensor_tensor(c[:, 2:T], u[:, 0:T - 2], taps[0][:, bass.ds(col, 1)],
                                                           c[:, 2:T], ALU.mult, ALU.add)
                            if half:
                                ins.then_inc(g.conv, 1)
                            else:
                                link(ins)
                    for f in range(2):
                        dve.wait_ge(g.silu, g.before["silu"] + 2 * i + f + 1)
                        dve.wait_ge(g.conv, g.before["conv"] + 2 * i + f + 1)
                        dve.wait_ge(g.used, g.before["used"] + i)
                        dve.tensor_tensor(aT[:, s, f, :], sg[:, f, :], cg[:, f, 1, :], ALU.mult).then_inc(g.act, 1)

                link.loop(6)
                in_pairs(dve, g.n, body)
                link.end(g.n)

            def final_norm():
                dve.wait_ge(s_sum, 2 * 5)
                dve.tensor_scalar(ss[:], ss[:], 1.0 / D, EPS, ALU.mult, ALU.add).then_inc(s_ms, 1)
                dve.wait_ge(s_root, 5)
                link(dve.reciprocal(rstd[:], rstd[:]))
                for t in range(TT):
                    dve.scalar_tensor_tensor(xres[:, t, :], xres[:, t, :], rstd[:, t:t + 1], gain[:], ALU.mult,
                                             ALU.mult).then_inc(s_xres, 1)

            def evac_plain(c):
                for b in (0, 2):
                    dve.wait_ge(s_trn, 16 + 4 * c + b + 1)
                    dve.tensor_copy(hT[:, 2 * b:2 * b + 2, :], wb[:, b, :].rearrange("p (a b) -> p a b", a=2))\
                        .then_inc(s_hT, 1)

            def pairs_at(ap, i, lo, hi, step):
                x = ap[:].rearrange("p t d h -> p (t d) h")[:, lo:hi:step, bass.ds(2 * i, 2)]
                return bcast(x, 3, P)

            def delta_rule():
                dve.wait_ge(gd.gates_in, 1)
                dve.wait_ge(s_small, 16 * SMALL_LOADS)
                ab = acc[:, 0, 0:128].rearrange("p (t c) -> p t c", t=TT)
                link(dve.tensor_tensor(gate_in[:, 0], ab[:, :, 0:32], bcast(dtb[:], 1, TT), ALU.add))
                link(dve.tensor_copy(gate_in[:, 1], ab[:, :, 32:64]))
                link(dve.tensor_scalar(gate_in[:, 2], gate_in[:, 0], -1.0, None, ALU.mult))
                dve.tensor_tensor(gate_in[:, 2], gate_in[:, 2], gate_in[:, 0], ALU.min).then_inc(gd.gates_added, 1)
                link(dve.tensor_scalar(gate_in[:, 0], gate_in[:, 0], 0.0, None, ALU.max))
                dve.wait_ge(gd.gates_exp, 4)
                link(dve.tensor_tensor(gate_in[:, 0], gate_in[:, 0], gate_in[:, 5], ALU.add))
                gg = gG[:].rearrange("p t d h -> p t (d h)")
                link(dve.tensor_tensor(gg, gate_in[:, 0], bcast(alog[:], 1, TT), ALU.mult))
                dve.tensor_scalar(gG[:], gG[:], -1.0, None, ALU.mult).then_inc(gd.gates_set, 1)
                link(dve.tensor_scalar(gate_in[:, 4], gate_in[:, 4], 1.0, None, ALU.add))
                link(dve.reciprocal(gB[:].rearrange("p t d h -> p t (d h)"), gate_in[:, 4]))
                dve.wait_ge(gd.gates_exp, 5)
                dve.tensor_tensor(gK[:].rearrange("p t d h -> p (t d h)"), acc[:, 1, 64:128],
                                  gC[:].rearrange("p t d h -> p (t d h)"), ALU.subtract)\
                    .then_inc(gd.gates_added, 1)
                dve.wait_ge(gd.gates_exp, 6)
                link(dve.tensor_scalar(nwh[:], nwh[:], 0.5, None, ALU.mult))
                dve.memset(gate_in[:, 0], 0.0).then_inc(gd.gates_ready, 1)

                def taps(i, tile):
                    u = wb[:, tile // 2, tile % 2 * T:(tile % 2 + 1) * T]
                    c = cq[:, tile, :]
                    for n, (j, dst, src) in enumerate(((0, slice(2, T), slice(0, T - 2)),
                                                       (1, slice(1, T), slice(0, T - 1)),
                                                       (3, slice(0, T - 1), slice(1, T)),
                                                       (4, slice(0, T - 2), slice(2, T)))):
                        row = 5 if j < 3 else 6
                        ins = dve.scalar_tensor_tensor(c[:, dst], u[:, src],
                                                       cols[:, row, bass.ds(tap_col(j, tile, i), 1)],
                                                       c[:, dst], ALU.mult, ALU.add)
                        if n < 3:
                            link(ins)
                    ins.then_inc(gd.taps, 1)

                def silu(i, tile):
                    dve.wait_ge(gd.tanh, 4 * i + tile + 1)
                    dve.scalar_tensor_tensor(cq[:, tile, :], th[:, tile, :], 1.0, cq[:, tile, :], ALU.add,
                                             ALU.mult).then_inc(gd.silu, 1)

                def front(i, s, step):
                    if step == 0:
                        dve.wait_ge(gd.first, 4 * i + 2)
                        taps(i, 0)
                    elif step == 1:
                        taps(i, 1)
                        silu(i, 0)
                    elif step == 2:
                        silu(i, 1)
                        dve.wait_ge(gd.first, 4 * i + 4)
                        taps(i, 2)
                    elif step == 3:
                        taps(i, 3)
                        silu(i, 2)
                    elif step == 4:
                        silu(i, 3)
                        dve.wait_ge(gd.ztanh, i + 1)
                        dve.wait_ge(gd.zready, i) if not isinstance(i, int) or i > 0 else None
                        dve.scalar_tensor_tensor(zs[:], zt[:], 1.0, wb[:, 2, :].rearrange("p (t c) -> p t c", t=TT),
                                                 ALU.add, ALU.mult).then_inc(gd.zsilu, 1)

                def body(i, s, more):
                    link.iteration(i)
                    for d in range(2):
                        dve.wait_ge(gd.row, 2 * i + d + 1)
                        dve.wait_ge(gd.lgr, 2 * i + d + 1)
                        dve.tensor_tensor(DM[:, d].rearrange("p t v c -> p (t v c)"), acc[:, 2 + d, :],
                                          LG[:, d].rearrange("p t v c -> p (t v c)"), ALU.add).then_inc(gd.expo, 1)
                    for n, which in ((1, 1), (0, 0)):
                        dve.wait_ge(gd.qkr, 2 * i + n + 1)
                        dve.tensor_tensor(kq[:, :, 1 - which, :], cq[:, n, :].rearrange("p (t c) -> p t c", t=TT),
                                          lnq[:, n, :].rearrange("p (t c) -> p t c", t=TT), ALU.mult)\
                            .then_inc(gd.kq, 1)
                    dve.wait_ge(gd.kk, i + 1)
                    prod = wb[:, 3, :].rearrange("p (t a c) -> p t a c", t=TT, a=2)
                    for d in range(2):
                        dve.wait_ge(gd.db, 2 * i + d + 1)
                        dve.tensor_tensor(AM[:, d], bcast(prod[:, :, 0, :], 2, 2), DB[:, d], ALU.mult)\
                            .then_inc(gd.am, 1)
                    for d in range(2):
                        dve.tensor_tensor(QA[:, d], bcast(prod[:, :, 1, :], 2, 2), DM[:, d], ALU.mult)
                    for n in range(len(LEVELS)):
                        end = n == len(LEVELS) - 1
                        lm = const("levels")[:, 2 * n * P:(2 * n + 2) * P]
                        for d in range(2):
                            dve.wait_ge(gd.g, 12 * i + 2 * n + d + 1)
                            dve.tensor_tensor(GI[:, d].rearrange("p t v c -> p (t v) c"),
                                              acc[:, d, :].rearrange("p (q c) -> p q c", c=P),
                                              bcast(lm[:, d * P:(d + 1) * P], 1, 4), ALU.mult).then_inc(gd.gev, 1)
                        for d in range(2):
                            dve.wait_ge(gd.xg, 12 * i + 2 * n + d + 1)
                            m = (YI if end else XI)[:, d].rearrange("p t v c -> p (t v c)")
                            dve.tensor_tensor(m, m, acc[:, 2 + d, :], ALU.subtract).then_inc(gd.xev, 1)
                        if more and n < 5:
                            front(i + 1, 1 - s, n)
                    dve.wait_ge(gd.r1, i + 1)
                    dve.tensor_tensor(vn1[:], acc[:, 0, :].rearrange("p (t v c) -> p t v c", t=TT, v=2),
                                      pairs_at(gB, i, 0, 4, 3), ALU.mult).then_inc(gd.vn1, 1)
                    dve.wait_ge(gd.vn1, i + 1)
                    dve.tensor_tensor(vdec[:], vn1[:], pairs_at(gK, i, 0, 4, 3), ALU.mult).then_inc(gd.vdec, 1)
                    dve.wait_ge(gd.ks, 2 * i + 1)
                    link(dve.tensor_tensor(rb[:], acc[:, 2, :].rearrange("p (t v c) -> p t v c", t=TT, v=2),
                                           pairs_at(gE, i, 1, 3, 1), ALU.mult))
                    dve.tensor_tensor(rb[:], vtok[:], rb[:], ALU.subtract).then_inc(gd.rb, 1)
                    dve.wait_ge(gd.ks, 2 * i + 2)
                    dve.tensor_tensor(qse[:], acc[:, 3, :].rearrange("p (t v c) -> p t v c", t=TT, v=2),
                                      pairs_at(gE, i, 1, 3, 1), ALU.mult).then_inc(gd.qse, 1)
                    dve.wait_ge(gd.r2, i + 1)
                    dve.tensor_tensor(vn2[:], acc[:, 0, :].rearrange("p (t v c) -> p t v c", t=TT, v=2),
                                      pairs_at(gB, i, 1, 3, 1), ALU.mult).then_inc(gd.vn2, 1)
                    dve.wait_ge(gd.o, i + 1)
                    dve.wait_ge(gd.qse, i + 1)
                    dve.tensor_tensor(og[:].rearrange("p t v c -> p (t v c)"), acc[:, 1, :],
                                      qse[:].rearrange("p t v c -> p (t v c)"), ALU.add).then_inc(gd.osum, 2)
                    dve.wait_ge(gd.orms, i + 1)
                    flat = og[:].rearrange("p t v c -> p (t v) c")
                    link(dve.tensor_tensor(flat, flat, bcast(osr[:], 2, P), ALU.mult))
                    dve.wait_ge(gd.zready, i + 1)
                    dve.tensor_tensor(og[:].rearrange("p t v c -> p (t v c)"), og[:].rearrange("p t v c -> p (t v c)"),
                                      zn[:].rearrange("p t c -> p (t c)"), ALU.mult).then_inc(gd.on, 1)

                link.loop(12)
                link.iteration(0)
                for step in range(5):
                    front(0, 0, step)
                link.end(1)

                link.loop(14)
                in_pairs(dve, GH, body)
                link.end(GH, fewer=12)

            def layernorm(c, done, count, inc):
                dve.wait_ge(done, count)
                for t in range(TT):
                    x2 = xres[:, t, :].rearrange("p (n c) -> p n c", n=2)
                    dve.scalar_tensor_tensor(x2, x2, ALPHA, acc[:, 2 * t:2 * t + 2, :], ALU.mult, ALU.add)\
                        .then_inc(s_added, 1)
                if last == 6:
                    return
                for t in range(TT):
                    dve.wait_ge(s_added, 2 * c + t + 1)
                    for n in range(2):
                        link(dve.bn_stats(bst[:, t, n, :], xres[:, t, n * 512:(n + 1) * 512]))
                    ins = dve.bn_aggr(mv[:, t, :], bst[:, t])
                    if t:
                        ins.then_inc(s_lnvar, 1)
                    else:
                        link(ins)
                dve.wait_ge(s_lnroot, c + 1)
                dve.wait_ge(s_ln, 32 * (c + 1))
                link(dve.reciprocal(lrs[:], lrs[:]))
                for t in range(TT):
                    link(dve.tensor_scalar(xres[:, t, :], xres[:, t, :], mv[:, t, 0:1], lrs[:, t:t + 1],
                                           ALU.subtract, ALU.mult))
                    link(dve.tensor_tensor(xres[:, t, :], xres[:, t, :], gain[:], ALU.mult))
                    dve.tensor_tensor(xres[:, t, :], xres[:, t, :], offset[:], ALU.add).then_inc(s_xres, 1)

            def first_largest(x, n, top, onehot, work):
                link(dve.tensor_reduce(top, x, AX.X, ALU.max))
                link(dve.tensor_tensor(work, x, bcast(top, 2, n), ALU.is_ge))
                link(dve.tensor_tensor(work, work, bcast(const("rank")[:, 0:n], 1, TT), ALU.mult))
                link(dve.tensor_reduce(rA[:, 15, :], work, AX.X, ALU.max))
                link(dve.tensor_tensor(onehot, work, bcast(rA[:, 15, :], 2, n), ALU.is_equal))

            def route():
                dve.wait_ge(rt_pe, RT_LOGITS)
                link(dve.tensor_tensor(lg[:], acc[:, 0, 0:72].rearrange("p (t c) -> p t c", t=TT),
                                       bcast(br[:], 1, TT), ALU.add))
                first_largest(lg[:, :, 0:4], GROUPS, rA[:, 0, :], goh[:], rB[:, 0, :, 0:4])
                dve.tensor_tensor(gex[:], lg[:, :, 0:4], bcast(rA[:, 0, :], 2, 4), ALU.subtract).then_inc(rt_dve, 1)
                link(dve.tensor_tensor(sel[:], lg[:, :, 4:36].rearrange("p t (g e) -> p t g e", g=GROUPS),
                                       bcast(goh[:], 3, 8), ALU.mult))
                es, oh1, es2, oh2, work = (rB[:, n] for n in range(1, 6))
                link(dve.tensor_reduce(es, sel[:].rearrange("p t g e -> p t e g"), AX.X, ALU.add))
                first_largest(es, 8, rA[:, 1, :], oh1, work)
                link(dve.scalar_tensor_tensor(es2, oh1, NEG, es, ALU.mult, ALU.add))
                first_largest(es2, 8, rA[:, 2, :], oh2, work)
                dve.tensor_tensor(rA[:, 8, :], rA[:, 2, :], rA[:, 1, :], ALU.subtract).then_inc(rt_dve, 1)
                dve.wait_ge(rt_act, RT_GROUP_EXP)
                link(dve.tensor_reduce(rA[:, 3, :], gex[:], AX.X, ALU.add))
                dve.wait_ge(rt_act, RT_PAIR_EXP)
                link(dve.tensor_scalar(rA[:, 4, :], rA[:, 9, :], 1.0, None, ALU.add))
                link(dve.tensor_tensor(rA[:, 5, :], rA[:, 4, :], rA[:, 3, :], ALU.mult))
                link(dve.reciprocal(rA[:, 6, :], rA[:, 5, :]))
                link(dve.tensor_tensor(rA[:, 7, :], rA[:, 6, :], rA[:, 9, :], ALU.mult))
                link(dve.tensor_tensor(oh1, oh1, bcast(rA[:, 6, :], 2, 8), ALU.mult))
                link(dve.tensor_tensor(oh2, oh2, bcast(rA[:, 7, :], 2, 8), ALU.mult))
                link(dve.tensor_tensor(oh1, oh1, oh2, ALU.add))
                dve.tensor_tensor(comb[:], bcast(oh1, 2, GROUPS), bcast(goh[:], 3, 8), ALU.mult).then_inc(rt_dve, 1)
                dve.wait_ge(rt_dve, RT_COMB)
                dve.tensor_scalar(chosen[:], comb[:].rearrange("p t g e -> p t (g e)"), 0.0, None, ALU.is_gt)\
                    .then_inc(rt_dve, 1)
                dve.wait_ge(rt_pe, RT_COUNTED)
                link(dve.tensor_reduce(most[:], acc[:, 2, TT * EXPERTS:(TT + 1) * EXPERTS], AX.X, ALU.max))
                dve.tensor_copy(most_i[:], most[:]).then_inc(s_most, 1)
                link(dve.tensor_tensor(place[:], acc[:, 2, 0:TT * EXPERTS].rearrange("p (t e) -> p t e", t=TT),
                                       chosen[:], ALU.mult))
                dve.tensor_scalar(place[:], place[:], -1.0, None, ALU.add).then_inc(rt_dve, 1)
                dve.wait_ge(rt_dve, RT_PLACES)

            def experts():
                g = moe

                def one_hot(j):
                    dve.tensor_tensor(sel_in, bcast(bcast(const("place"), 1, 2), 1, TT),
                                      bcast(place[:, :, bass.ds(2 * j, 2)], 3, CAP), ALU.is_equal)\
                        .then_inc(r_sel, 1)

                def gathered(j):
                    dve.wait_ge(r_gath, 2 * j + 2)
                    dve.tensor_copy(xg[:, 4:8, :].rearrange("p k c -> p (k c)"), wb[:, 1, :]).then_inc(r_xd, 1)

                def routed(j, s, more):
                    if more:
                        one_hot(j + 1)
                    dve.wait_ge(r_silu, j + 1)
                    dve.tensor_tensor(aS, sgr, wb[:, 2, HID:2 * HID], ALU.mult).then_inc(r_act, 1)
                    half = j // 2 if isinstance(j, int) else (j - s) // 2
                    dve.wait_ge(r_back[s], 64 * (half + 1))
                    dve.scalar_tensor_tensor(sel_out, rows_r[:, s, 1, :], const("place_col"), rows_r[:, s, 0, :],
                                             ALU.is_equal, ALU.mult).then_inc(r_selout, 1)
                    if more:
                        gathered(j + 1)
                    dve.wait_ge(r_down, 2 * j + 2)
                    dve.tensor_copy(yR[:, 512:1024], wb[:, 3, :]).then_inc(r_yd, 1)

                def body(i, s, more):
                    link.iteration(i)
                    g.back_loaded(dve, i, s)
                    for f in range(2):
                        dve.wait_ge(g.silu, g.before["silu"] + 2 * i + f + 1)
                        dve.wait_ge(g.used, g.before["used"] + i)
                        link(dve.tensor_tensor(cg[:, f, 0, :], sg[:, f, :], wb[:, 2 * s + f, T:2 * T], ALU.mult))
                        dve.tensor_tensor(aT[:, s, f, :], cg[:, f, 0, :], cb[:, s, :], ALU.mult).then_inc(g.act, 1)

                with dve.If(dve.value_load(most_i[0:1, 0:1]) < CAP + 1):
                    one_hot(0)
                    gathered(0)
                    in_pairs(dve, PAIRS, routed)
                    dve.sem_inc(dve_chain, 2 * EXPERTS)
                with dve.Else():
                    link.loop(2)
                    in_pairs(dve, g.n, body)
                    link.end(g.n)

            rms(0)
            evac_norm(0, [(hT, 0)])
            heads(0)
            add_acc(0, att[0])
            if last >= 2:
                rms(1)
                evac_norm(1, [(hT, 24)])
                feed(0)
                add_acc(1, ffn[0])
            if last >= 3:
                dve.wait_ge(s_vec, VEC_LOADS * 16)
                rms(2)
                evac_norm(2, [(hT, 8), (hkT, 16)])
                heads(1)
                add_acc(2, att[1])
            if last >= 4:
                rms(3)
                evac_norm(3, [(hT, 32)])
                feed(1)
                add_acc(3, ffn[1])
            if last >= 5:
                final_norm()
            if last >= 6:
                evac_plain(0)
                delta_rule()
                layernorm(0, s_mixed, 1, 12)
            if last >= 8:
                evac_plain(1)
                route()
                experts()
                layernorm(1, s_moe_done, 1, 14)
            if last >= 9:
                evac_plain(2)
                for t in range(TT):
                    dve.wait_ge(ple_act, t + 2)
                    x2 = xn[:, t, :].rearrange("p (n c) -> p n c", n=2)
                    link(dve.tensor_tensor(x2, x2, wb[:, 2 * t:2 * t + 2, :], ALU.mult))
                    dve.tensor_tensor(xn[:, t, :], xn[:, t, :], xres[:, t, :], ALU.add).then_inc(s_prod, 1)

        @block.gpsimd
        def _(pool):
            pool.dma_start(xres[:], a["x"].rearrange("a (t p) n -> p (a t) n", p=P)).then_inc(s_x, 16)
            pool.dma_start(cst[:], consts).then_inc(s_const, 16)
            with nc.allow_non_contiguous_dma(reason="256 positions"):
                pool.dma_start(pos_i[:], a["positions"].rearrange("a (t p) -> p (a t)", p=P)).then_inc(s_pos, 16)
            loads = [(0, 0, a["attn_norm"].rearrange("l (k p) -> (l k) p", p=P)),
                     (0, 16, a["kv_norm"].rearrange("(k p) -> k p", p=P)),
                     (0, 24, a["ffn_norm"].rearrange("l (k p) -> (l k) p", p=P))]
            for l in range(2):
                cw = a["conv_w"][l].rearrange("j (k p) -> (j k) p", p=P)
                loads += [(1 + 2 * l, 0, cw[0:4 * FT]), (2 + 2 * l, 0, cw[4 * FT:6 * FT]),
                          (2 + 2 * l, 2 * FT, a["conv_b"][l].rearrange("(k p) -> k p", p=P))]
            gw = a["gdn_conv_w_2"][0].rearrange("j (k p) -> (j k) p", p=P)
            loads += [(5, 0, gw[0:96]), (6, 0, gw[96:160])]
            assert len(loads) == ROW_LOADS
            for n, r, src in loads:
                pool.dma_start(rows[r:r + src.shape[0], n, :], src).then_inc(s_rows, 16)
            vec = [(sink[:], a["sinks_b"]), (gain[:], a["final_norm"].rearrange("(a n) -> a n", a=1))]
            assert len(vec) == VEC_LOADS
            for dst, src in vec:
                pool.dma_start(dst, src.to_broadcast([P, src.shape[1]])).then_inc(s_vec, 16)
            small = [(dtb[:], a["gdn_dt_bias_2"].rearrange("a z h -> a (z h)").to_broadcast([P, 2 * GV])),
                     (alog[:], a["gdn_a_log_2"].rearrange("a z h -> a (z h)").to_broadcast([P, 2 * GV])),
                     (nwh[:], a["gdn_norm_w_2"].to_broadcast([P, P])),
                     (wab[:], a["gdn_w_in_2"][0].rearrange("(k p) c -> p k c", p=P)[:, :, 6 * D:6 * D + 64]),
                     (wr[:, :, 0:4], a["moe_w_group_2"][0].rearrange("(k p) c -> p k c", p=P)),
                     (wr[:, :, 4:36], a["moe_w_router_2"][0].rearrange("(k p) c -> p k c", p=P)),
                     (br[:, 0:4], a["moe_b_group_2"].to_broadcast([P, 4])),
                     (br[:, 4:36], a["moe_b_router_2"].to_broadcast([P, 32])),
                     (pt_in[:], a["p_2"][0].rearrange("b (t p) c -> p (b t) c", p=P))]
            assert len(small) == SMALL_LOADS
            for dst, src in small:
                pool.dma_start(dst, src).then_inc(s_small, 16)

            if last < 6:
                return
            pool.wait_ge(gd.gates_ready, 1)

            def heads_of(ap, i, d):
                return bcast(ap[:, :, d, bass.ds(2 * i, 2)], 3, P)

            def wide(ap):
                return bcast(bcast(ap, 1, 2), 1, TT)

            def sums(i):
                for d, m in ((0, const("le")), (1, const("ge"))):
                    if not isinstance(i, int) or i > 0:
                        pool.wait_ge(gd.row, 2 * i)
                        pool.wait_ge(gd.expo, 2 * i)
                    pool.tensor_tensor(gU[:, d], wide(m), heads_of(gG, i, d), ALU.mult).then_inc(gd.gu, 1)
                    pool.tensor_tensor(LG[:, d], wide(const("lim")[:, d * P:(d + 1) * P]), heads_of(gC, i, d),
                                       ALU.subtract).then_inc(gd.lgr, 1)

            def body(i, s, more):
                for d in range(2):
                    pool.wait_ge(gd.decay, 2 * i + d + 1)
                    pool.tensor_tensor(DB[:, d], DM[:, d], heads_of(gB, i, d), ALU.mult).then_inc(gd.db, 1)
                for d in range(2):
                    pool.wait_ge(gd.am, 2 * i + d + 1)
                    pool.tensor_tensor(YI[:, d].rearrange("p t v c -> p (t v) c"),
                                       AM[:, d].rearrange("p t v c -> p (t v) c"),
                                       bcast(const("first")[:, d * P:(d + 1) * P], 1, 4), ALU.mult)\
                        .then_inc(pool_chain, 1)
                    pool.wait_ge(pool_chain, 2 * i + d + 1)
                    pool.tensor_tensor(YI[:, d].rearrange("p t v c -> p (t v) c"),
                                       YI[:, d].rearrange("p t v c -> p (t v) c"),
                                       bcast(ident, 1, 4), ALU.add).then_inc(gd.y2, 1)
                if more:
                    sums(i + 1)
                pool.wait_ge(gd.zsilu, i + 1)
                pool.tensor_tensor(zn[:].rearrange("p t (v c) -> p (t v) c", v=2),
                                   zs[:].rearrange("p t (v c) -> p (t v) c", v=2),
                                   bcast(nwh[:], 1, 4), ALU.mult).then_inc(gd.zready, 1)
                pool.wait_ge(gd.r2, i + 1)
                pool.wait_ge(gd.on, i + 1)

            sums(0)
            in_pairs(pool, GH, body)


ROW_TILES = (40, 88, 88, 88, 88, 96, 64)
ROW_LOADS = 11
VEC_LOADS = 2
SMALL_LOADS = 9


def tap_col(j, tile, i):
    j = j if j < 3 else j - 3
    return 32 * j + (i if tile == 0 else i + GH if tile == 1 else 2 * i + 2 * GH + tile - 2)


def split_two_pi():
    a = 6.28125
    b = round((TWO_PI - a) * 2 ** 19) / 2 ** 19
    return a, b, TWO_PI - a - b


TWO_PI_PARTS = split_two_pi()

_UNUSED = ("m2_", "hg_", "gla_")


def kernel(**inputs):
    import numpy as _np
    import concourse.bacc as _bacc
    from concourse import mybir as _mybir
    from concourse.bass_utils import run_bass_kernel_spmd as _run

    nc = _bacc.Bacc("TRN2", target_bir_lowering=False, num_devices=1)
    arrays, args = {}, {}
    for name, value in inputs.items():
        if name.startswith(_UNUSED):
            continue
        v = _np.ascontiguousarray(value)
        arrays[f"in_{name}_dram"] = v
        args[name] = nc.dram_tensor(f"in_{name}_dram", v.shape, _mybir.dt.from_np(v.dtype), kind="ExternalInput").ap()
    table = _np.concatenate(list(constant_columns().values()), axis=1)
    arrays["constants"] = table
    consts = nc.dram_tensor("constants", table.shape, _mybir.dt.float32, kind="ExternalInput").ap()
    comb = nc.dram_tensor("comb_scratch", [EXPERTS, 2, T], _mybir.dt.float32, kind="Internal").ap()
    out = nc.dram_tensor("out_dram", [1, T, D], _mybir.dt.float32, kind="ExternalOutput").ap()
    build(nc, args, consts, comb, out, LAST)
    r = _run(nc, [arrays], core_ids=[0])
    return r.results[0]["out_dram"]


LAST = 9
```

```python
from contextlib import ExitStack

import numpy as np

import concourse.bass as bass
from concourse import mybir

F32 = mybir.dt.float32
BF16 = mybir.dt.bfloat16
I32 = mybir.dt.int32
ALU = mybir.AluOpType
ACT = mybir.ActivationFunctionType
AX = mybir.AxisListType

P = 128
T = 256
TT = T // P
D = 1024
KT = D // P
HD = 64
ROT = 16
FF = 2816
FT = FF // P
GH = 8
GV = 16
EXPERTS = 32
HID = 256
GROUPS = 4
SLOT = 8 * 1024
UNIT = 2 * 1024
EPS = 1e-6
LN_EPS = 1e-5
ALPHA = 2.0 ** 0.25
NEG = -1e30
LEVELS = (2, 4, 8, 16, 32, 64)
CAP = 64
PAIRS = EXPERTS // 2
TWO_PI = 6.283185307179586
MAGIC = 12582912.0


def level_mask(s):
    r = np.arange(P)
    same = (r[:, None] // (2 * s)) == (r[None, :] // (2 * s))
    return (same & ((r[:, None] // s) % 2 == 1) & ((r[None, :] // s) % 2 == 0)).astype(np.float32)


def constant_columns():
    r = np.arange(P)
    le = (r[:, None] <= r[None, :]).astype(np.float32)
    neg_above = np.where(r[None, :] > r[:, None], NEG, 0.0)
    neg_below = np.where(r[None, :] <= r[:, None], NEG, 0.0)
    zero = np.zeros((P, P))
    parts = {
        "ident": np.eye(P),
        "mask0": np.concatenate([neg_above, zero, neg_above], 1),
        "mask1": np.concatenate([neg_above, neg_below, neg_above], 1),
        "freq": np.broadcast_to(500000.0 ** (-np.arange(0, ROT, 2, dtype=np.float32) / ROT), (P, ROT // 2)),
        "eps": np.full((P, 1), EPS),
        "ones": np.ones((P, P)),
        "le": le,
        "ge": le.T,
        "lim": np.concatenate([np.where(le > 0, 0.0, NEG), np.where(le.T > 0, 0.0, NEG)], 1),
        "first": np.concatenate([-level_mask(1).T, -level_mask(1)], 1),
        "levels": np.concatenate([m for s in LEVELS for m in (level_mask(s), level_mask(s).T)], 1),
        "rank": np.broadcast_to(np.arange(8, 0, -1), (P, 8)),
        "qscale": np.full((P, 1), np.log(0.5 * P ** -0.5)),
        "kscale": np.full((P, 1), np.log(0.5)),
        "lneps": np.full((P, 1), LN_EPS),
        "place": np.broadcast_to(np.arange(CAP), (P, CAP)),
        "place_col": (r % CAP)[:, None],
    }
    return {k: np.ascontiguousarray(v, dtype=np.float32) for k, v in parts.items()}


def constant_slices():
    at, out = 0, {}
    for k, v in constant_columns().items():
        out[k] = (at, at + v.shape[1])
        at += v.shape[1]
    return out, at


class Chain:

    def __init__(self, eng, sem):
        self.eng, self.sem = eng, sem
        self.base, self.start, self.per, self.k = 0, 0, 0, 0

    def loop(self, per):
        self.base, self.per, self.k = self.start + self.k, per, per

    def iteration(self, i):
        assert self.k == self.per, (self.k, self.per)
        self.start, self.k = self.base + self.per * i, 0

    def end(self, n, fewer=0):
        assert self.k == self.per - fewer, (self.k, self.per)
        self.start, self.k = self.base + n * self.per - fewer, 0

    def __call__(self, ins):
        self.k += 1
        ins.then_inc(self.sem, 1)
        self.eng.wait_ge(self.sem, self.start + self.k)


def in_pairs(eng, n, body):
    m = 2 * ((n - 1) // 2)
    if m:
        with eng.Fori(0, m, 2) as i:
            body(i, 0, True)
            body(i + 1, 1, True)
    for j in range(m, n):
        body(j, j % 2, j < n - 1)


def build(nc, a, consts, comb_dram, out):
    ctx = ExitStack()
    with ctx:
        def sb(name, shape, dt=F32):
            return ctx.enter_context(nc.sbuf_tensor(name, shape, dt))

        def sem(name):
            return ctx.enter_context(nc.semaphore(name))

        where, n_const = constant_slices()
        cst = sb("cst", [P, n_const])

        def const(name):
            lo, hi = where[name]
            return cst[:, lo:hi]

        ident, ones = const("ident"), const("ones")

        class Arena:

            def __init__(self, name, words):
                self.words, self.mem, self.at = words, sb(name, [P, words]), 0

            def again(self):
                self.at = 0

            def take(self, *shape):
                n = int(np.prod(shape))
                ap = self.mem[:, self.at:self.at + n]
                self.at += n
                assert self.at <= self.words, (self.at, self.words)
                names = "abcd"[:len(shape)]
                if len(shape) > 1:
                    ap = ap.rearrange(f"p ({' '.join(names)}) -> p {' '.join(names)}",
                                      **dict(zip(names[1:], shape[1:])))
                return ap

        W = sb("W", [P, 2, SLOT])
        xres = sb("xres", [P, TT, D])
        wide = Arena("wide", GV * T)
        xn = wide.take(TT, D)
        hT = sb("hT", [P, KT, T])
        hkT = wide.take(KT, T)
        wide.again()
        OT = wide.take(GV, T)
        cols = sb("cols", [P, 7, 96])
        sink = sb("sink", [P, 16])
        gain = sb("gain", [P, D])
        offset = sb("offset", [P, D])
        pos_i = sb("pos_i", [P, TT], I32)
        pos_f = sb("pos_f", [P, TT])
        ang = sb("ang", [P, 4, TT, ROT // 2])
        cos16 = sb("cos16", [P, TT, ROT])
        sin16 = sb("sin16", [P, TT, ROT])
        ss = sb("ss", [P, TT])
        rstd = sb("rstd", [P, TT])
        zeros = sb("zeros", [P, 512], BF16)
        work = Arena("work", 12416)
        rows = work.take(7, P)[0:96]
        AW = 448
        st = work.take(2, TT, AW)
        rt = work.take(2, TT, 6, ROT)
        qT = work.take(2, T)
        kT = work.take(T)
        SM = work.take(2, 386)
        PR = work.take(2, 386)
        nm = work.take(2, 2)
        rs = work.take(2, 2)
        rr = work.take(2, 2)
        PT = work.take(2, 384)
        oT = work.take(2, T)
        cg = work.take(2, 2, T)
        sg = work.take(2, T)
        aT = work.take(2, 2, T)
        cb = work.take(2, T)
        work.again()
        sel_in = work.take(TT, 2, CAP)
        xg = work.take(KT, 2 * CAP)
        sgr = work.take(HID)
        aS = work.take(HID)
        aR = work.take(2, 2 * CAP)
        yR = work.take(D)
        sel_out = work.take(T)
        rows_r = work.take(2, 2, T)
        wd_odd = work.take(2, 2, D)
        wide.again()
        wd_even = wide.take(2, 2, D)
        work.again()
        wab = sb("wab", [P, KT, 4 * GV])
        gate_in = sb("gate_in", [P, 6, TT, 2 * GV])
        dtb = sb("dtb", [P, 2 * GV])
        alog = sb("alog", [P, 2 * GV])
        gG = sb("gG", [P, TT, 2, GV])
        gB = sb("gB", [P, TT, 2, GV])
        gC = sb("gC", [P, TT, 2, GV])
        gE = sb("gE", [P, TT, 2, GV])
        gK = sb("gK", [P, TT, 2, GV])
        nwh = sb("nwh", [P, P])
        cq = sb("cq", [P, 4, T])
        th = sb("th", [P, 4, T])
        sq = sb("sq", [P, 2, T])
        lnq = sq
        zt = sb("zt", [P, TT, 2 * P])
        zs = zt
        zn = sb("zn", [P, TT, 2 * P])
        ktok = sb("ktok", [P, 2, TT, P])
        gU = work.take(2, TT, 2, P)
        LG = work.take(2, TT, 2, P)
        DM = work.take(2, TT, 2, P)
        DB = LG
        QA = work.take(2, TT, 2, P)
        AM = work.take(2, TT, 2, P)
        XI = work.take(2, TT, 2, P)
        YI = work.take(2, TT, 2, P)
        GI = work.take(2, TT, 2, P)
        vn1 = work.take(TT, 2, P)
        vdec = work.take(TT, 2, P)
        vn2 = vdec
        Sst = work.take(2, 2, P)
        rb = work.take(TT, 2, P)
        qse = work.take(TT, 2, P)
        og = work.take(TT, 2, P)
        kq1, vtok1 = work.take(TT, 2, P), work.take(TT, 2, P)
        kq0, vtok0 = sb("kq0", [P, TT, 2, P])[:], sb("vtok0", [P, TT, 2, P])[:]
        kq = (kq0, kq1)
        vtok = (vtok0, vtok1)
        root_of_eps = sb("root_of_eps", [P, 1])
        oss = sb("oss", [P, 4])
        osl = sb("osl", [P, 4])
        osr = sb("osr", [P, 4])
        wr = sb("wr", [P, KT, 36])
        br = sb("br", [P, 36])
        bst = sb("bst", [P, TT, 2, 6])
        mv = sb("mv", [P, TT, 2])
        lrs = sb("lrs", [P, TT])
        lg = sb("lg", [P, TT, 36])
        rA = sb("rA", [P, 16, TT])
        rB = sb("rB", [P, 8, TT, 8])
        goh = sb("goh", [P, TT, GROUPS])
        gex = sb("gex", [P, TT, GROUPS])
        sel = sb("sel", [P, TT, GROUPS, 8])
        comb = sb("comb", [P, TT, GROUPS, 8])
        chosen = sb("chosen", [P, TT, EXPERTS])
        place = sb("place", [P, TT, EXPERTS])
        most = sb("most", [P, 1])
        most_i = sb("most_i", [P, 1], I32)
        combT = sb("combT", [EXPERTS, 2, T])
        pt_in = sb("pt_in", [P, TT, 2 * P])
        pT = sb("pT", [P, 2, T])
        acc = ctx.enter_context(nc.psum_tensor("acc", [P, 4, 512], F32))
        wb = ctx.enter_context(nc.psum_tensor("wb", [P, 4, 512], F32))
        all_acc = [acc[:, b, :] for b in range(4)]

        def bcast(ap, axis, n):
            x = ap.unsqueeze(axis)
            shape = list(x.shape)
            shape[axis] = n
            return x.to_broadcast(shape)

        s_const, s_x, s_rows, s_vec, s_pos = (sem(n) for n in ("const", "x_in", "rows_in", "vec_in", "pos_in"))
        s_zero = sem("zeros_set")
        dve_chain, act_chain, pool_chain = sem("dve_chain"), sem("act_chain"), sem("pool_chain")
        s_colT, s_cols = sem("cols_transposed"), sem("cols_ready")
        s_ang, s_sin = sem("angles_ready"), sem("sines_ready")
        s_sum, s_ms, s_root, s_rstd = sem("squares_summed"), sem("mean_square"), sem("root"), sem("rstd_ready")
        s_xn, s_trn, s_hT = sem("xn_ready"), sem("xn_transposed"), sem("hT_ready")
        s_hTa = sem("hT_ready_act")
        s_acc, s_xres = sem("acc_done"), sem("xres_ready")
        s_out = sem("out_written")
        s_ln = sem("layernorm_vectors_in")

        class Stage:

            def __init__(self, name, n, front_loads, back_loads, counts, like=None):
                self.n, self.front_loads, self.back_loads, self.counts = n, front_loads, back_loads, counts
                self.before = {**{k: 0 for k in counts}, "front_in": [0, 0], "back_in": [0, 0]}
                if like is None:
                    self.before["used"] = 1
                    self.front_in = [sem(f"{name}_front_loaded{s}") for s in range(2)]
                    self.back_in = [sem(f"{name}_back_loaded{s}") for s in range(2)]
                    return
                self.front_in, self.back_in = like.front_in, like.back_in
                old = like.before
                self.before = {k: old[k] + like.counts[k] * like.n for k in like.counts}
                uses = [(like.n + 1) // 2, like.n // 2]
                self.before["front_in"] = [old["front_in"][s] + 16 * like.front_loads * uses[s] for s in range(2)]
                self.before["back_in"] = [old["back_in"][s] + 16 * like.back_loads * uses[s] for s in range(2)]

            def front_loaded(self, eng, i, s):
                half = i // 2 if isinstance(i, int) else (i - s) // 2
                eng.wait_ge(self.front_in[s], self.before["front_in"][s] + 16 * self.front_loads * (half + 1))

            def back_loaded(self, eng, i, s):
                half = i // 2 if isinstance(i, int) else (i - s) // 2
                eng.wait_ge(self.back_in[s], self.before["back_in"][s] + 16 * self.back_loads * (half + 1))

        att = []
        for l, (n, pairs) in enumerate(((8, 1), (4, 2))):
            once = ("proj", "copied", "roped", "heads_transposed", "qT_ready", "kT_ready", "used")
            by_pair = ("scored", "probs_transposed", "pt_ready_act", "pt_ready_dve", "pv", "oT_ready")
            counts = {**{k: 1 for k in once}, **{k: pairs for k in by_pair},
                      "max_ready": 2 * pairs, "exped": 4 * pairs, "normed": 4 * pairs}
            att.append(Stage(f"att{l}", n, 3 + l, 1, counts, att[0] if l else None))
            att[l].pairs = pairs
        for g in att:
            first = g is att[0]
            g.proj = sem("att_proj") if first else att[0].proj
            g.copied = sem("att_copied") if first else att[0].copied
            g.roped = sem("att_roped") if first else att[0].roped
            g.heads_transposed = sem("att_heads_transposed") if first else att[0].heads_transposed
            g.qT_ready = sem("att_qT_ready") if first else att[0].qT_ready
            g.kT_ready = sem("att_kT_ready") if first else att[0].kT_ready
            g.scored = sem("att_scored") if first else att[0].scored
            g.max_ready = sem("att_max_ready") if first else att[0].max_ready
            g.exped = sem("att_exped") if first else att[0].exped
            g.normed = sem("att_normed") if first else att[0].normed
            g.probs_transposed = sem("att_probs_transposed") if first else att[0].probs_transposed
            g.pt_ready_act = sem("att_pt_ready_act") if first else att[0].pt_ready_act
            g.pt_ready_dve = sem("att_pt_ready_dve") if first else att[0].pt_ready_dve
            g.pv = sem("att_pv") if first else att[0].pv
            g.oT_ready = sem("att_oT_ready") if first else att[0].oT_ready
            g.used = sem("att_used") if first else att[0].used
        ffn = []
        for name, n in (("ffn0", FT // 2), ("ffn1", FT // 2), ("moe", EXPERTS)):
            counts = {"up": 2, "first": 4, "conv": 2, "silu": 2, "act": 2, "used": 1}
            ffn.append(Stage(name, n, 2, 2 if name == "moe" else 1, counts, ffn[-1] if ffn else None))
        for g in ffn:
            first = g is ffn[0]
            g.up = sem("ffn_up") if first else ffn[0].up
            g.first = sem("ffn_first") if first else ffn[0].first
            g.conv = sem("ffn_conv") if first else ffn[0].conv
            g.silu = sem("ffn_silu") if first else ffn[0].silu
            g.act = sem("ffn_act") if first else ffn[0].act
            g.used = sem("ffn_used") if first else ffn[0].used
        moe = ffn[2]

        gd = Stage("gdn", GH, 4, 1, {})
        gd.fronts = sem("gdn_projected")
        (gd.gates_in, gd.gates_added, gd.gates_exp, gd.gates_set, gd.gates_summed, gd.gates_ready) = (
            sem(f"gdn_gates_{n}") for n in ("projected", "added", "exp", "set", "summed", "ready"))
        gd.qk, gd.v, gd.z = sem("gdn_qk_projected"), sem("gdn_v_projected"), gd.fronts
        (gd.first, gd.taps, gd.tanh, gd.silu, gd.ztanh, gd.zsilu, gd.zready, gd.sq) = (
            sem(f"gdn_{n}") for n in ("first_tap", "taps", "tanh", "silu", "z_tanh", "z_silu", "z_ready", "squared"))
        (gd.ss, gd.vt, gd.row, gd.qkr, gd.kq, gd.vtok, gd.gu, gd.lgr, gd.expo, gd.decay) = (
            sem(f"gdn_{n}") for n in ("norms_summed", "v_transposed", "rows_summed", "norms_ready", "kq_ready",
                                      "vtok_ready", "gU_ready", "LG_ready", "exponent_ready", "decay_ready"))
        (gd.kk, gd.kt, gd.ktok, gd.db, gd.n1, gd.am, gd.y2, gd.x2t, gd.x2) = (
            sem(f"gdn_{n}") for n in ("products", "k_transposed", "ktok_ready", "decay_beta_ready",
                                      "first_quarters", "matrix_ready", "first_inverse_T", "first_transposed",
                                      "first_inverse"))
        (gd.g, gd.gev, gd.xg, gd.xev, gd.yg, gd.yev) = (
            sem(f"gdn_{n}") for n in ("level_row", "level_row_ready", "level_product", "level_inverse_ready",
                                      "level_product_T", "level_inverse_T_ready"))
        (gd.r1, gd.vn1, gd.vdec, gd.s, gd.sev, gd.ks, gd.rb, gd.qse, gd.r2, gd.vn2, gd.o, gd.osum, gd.orms,
         gd.on, gd.ot, gd.OT) = (
            sem(f"gdn_{n}") for n in ("first_solved", "vn1_ready", "vdec_ready", "state", "state_ready",
                                      "state_products", "rhs_ready", "state_out_ready", "second_solved", "vn2_ready",
                                      "output", "output_ready", "output_rms", "output_gated",
                                      "output_transposed", "OT_ready"))
        s_wout = [sem(f"w_out_loaded{s}") for s in range(2)]
        s_mixed = sem("gdn_output_projected")
        s_added, s_lnroot, s_lnvar = sem("ln_input_ready"), sem("ln_root"), sem("ln_var")
        s_small = sem("small_weights_in")
        rt_pe, rt_dve, rt_act = sem("router_tensor"), sem("router_vector"), sem("router_scalar")
        RT_LOGITS, RT_COUNTED, RT_TRANSPOSED = 1, 2, 3
        RT_GROUP_SHIFTED, RT_PAIR_DIFFERENCE, RT_COMB, RT_CHOSEN, RT_PLACES = 1, 2, 3, 4, 5
        RT_GROUP_EXP, RT_PAIR_EXP = 1, 2
        s_most, s_combT, s_comb_out = (sem(f"router_{n}") for n in ("most_ready", "combT_ready", "comb_stored"))
        s_moe_done = sem("experts_done")
        (r_sel, r_gath, r_xa, r_xd, r_up, r_silu, r_act, r_turned, r_aR, r_down, r_selout, r_ya, r_yd) = (
            sem(f"routed_{n}") for n in ("sel_in_ready", "gathered", "xg_ready_act", "xg_ready_dve", "up", "silu",
                                         "act", "act_transposed", "aR_ready", "down", "sel_out_ready",
                                         "y_ready_act", "y_ready_dve"))
        r_front = [sem(f"routed_front_loaded{s}") for s in range(2)]
        r_back = [sem(f"routed_back_loaded{s}") for s in range(2)]
        ple_pe, ple_act, s_wpe, s_prod = (sem(f"ple_{n}") for n in ("tensor", "scalar", "weights_in", "result"))

        def view(s, unit, shape):
            n = shape[0] * shape[1]
            return W[:, s, unit:unit + n].rearrange("p (a b) -> p a b", a=shape[0])

        def w_gate(s):
            return view(s, 0, (KT, 256))

        def w_up(s):
            return view(s, UNIT, (KT, 256))

        def w_down(s):
            return view(s, 2 * UNIT, (2, D))

        def w_both(s, x):
            return W[:, s, 2 * x * UNIT:(2 * x + 2) * UNIT].rearrange("p (h k c) -> p k h c", h=2, k=KT)

        def w_down_of(s):
            return wd_odd if s else wd_even

        def w_z(s):
            return view(s, 2 * UNIT, (KT, 256))

        def w_out(s):
            return view(s, 0, (8, D))

        def w_heads(l, s):
            return view(s, 0, (KT, 384 if l == 0 else 448))

        def w_o(l, s):
            return view(s, KT * 448, (l + 1, D))

        order = [att[0], ffn[0], att[1], ffn[1], ffn[2]]

        block = ctx.enter_context(nc.Block())


        @block.sync
        def _(sp):
            with nc.allow_non_contiguous_dma(reason="256 positions"):
                sp.dma_start(pos_i[:], a["positions"].rearrange("a (t p) -> p (a t)", p=P)).then_inc(s_pos, 16)
            early = where["ones"][0]
            sp.dma_start(cst[:, 0:early], consts[:, 0:early]).then_inc(s_const, 16)
            sp.dma_start(xres[:], a["x"].rearrange("a (t p) n -> p (a t) n", p=P)).then_inc(s_x, 16)
            sp.sem_inc(att[0].used, 1)
            sp.sem_inc(ffn[0].used, 1)
            sp.sem_inc(gd.OT, 1)

            def stage(k, g, fronts, fronts_before, per, load_front, load_back):
                for j in range(2):
                    if k:
                        prev = order[k - 1]
                        sp.wait_ge(prev.used, prev.before["used"] + prev.n - (prev.n - 1 - j) % 2)
                    load_front(j, j)
                    load_back(j, j)

                def later(i, s, _more):
                    sp.wait_ge(fronts, fronts_before + per * (i + 1))
                    load_front(i + 2, s)
                    sp.wait_ge(g.used, g.before["used"] + i + 1)
                    load_back(i + 2, s)

                in_pairs(sp, g.n - 2, later)

            def heads(l):
                g = att[l]
                w = a["w_qkv_a"][0] if l == 0 else a["w_q_b"][0]
                wo = a["w_o_a"][0] if l == 0 else a["w_o_b"][0]
                hw = 128 if l == 0 else 256

                def front(i, s):
                    dst = w_heads(l, s)
                    src = w.rearrange("(k p) c -> p k c", p=P)
                    if l == 0:
                        for part in range(3):
                            sp.dma_start(dst[:, :, part * P:(part + 1) * P],
                                         src[:, :, bass.ds(i * P + part * D, P)])\
                                .then_inc(g.front_in[s], 16)
                    else:
                        kv = a["w_kv_b"].rearrange("(k p) c -> p k c", p=P)
                        sp.dma_start(dst[:, :, 0:256], src[:, :, bass.ds(i * 256, 256)])\
                            .then_inc(g.front_in[s], 16)
                        for c in range(2):
                            sp.dma_start(dst[:, :, 256 + c * HD:256 + (c + 1) * HD],
                                         kv[:, :, bass.ds(i * HD, HD)]).then_inc(g.front_in[s], 16)
                        sp.dma_start(dst[:, :, 384:448], kv[:, :, bass.ds(i * HD + 256, HD)])\
                            .then_inc(g.front_in[s], 16)

                def back(i, s):
                    sp.dma_start(w_o(l, s), wo[bass.ds(i * hw, hw), :].rearrange("(f p) n -> p f n", p=P))\
                        .then_inc(g.back_in[s], 16)
                return front, back

            def feed(l):
                g = ffn[l]
                up = a["w_up"][l].rearrange("(k p) c -> p k c", p=P)

                def front(i, s):
                    sp.dma_start(w_gate(s), up[:, :, bass.ds(i * 256, 256)]).then_inc(g.front_in[s], 16)
                    sp.dma_start(w_up(s), up[:, :, bass.ds(i * 256 + FF, 256)]).then_inc(g.front_in[s], 16)

                def back(i, s):
                    sp.dma_start(w_down(s), a["w_down"][l][bass.ds(i * 256, 256), :]
                                 .rearrange("(f p) n -> p f n", p=P)).then_inc(g.back_in[s], 16)
                return front, back

            sp.wait_ge(s_rows, 16 * ROW_LOADS)
            stage(0, att[0], att[0].proj, att[0].before["proj"], 1, *heads(0))
            stage(1, ffn[0], ffn[0].up, ffn[0].before["up"], 2, *feed(0))
            stage(2, att[1], att[1].proj, att[1].before["proj"], 1, *heads(1))
            stage(3, ffn[1], ffn[1].up, ffn[1].before["up"], 2, *feed(1))

            def ln_vectors(c, version):
                sp.wait_ge(s_xres, 2 * version)
                sp.dma_start(gain[:], a["ln_g_2"][0, c:c + 1, :].to_broadcast([P, D])).then_inc(s_ln, 16)
                sp.dma_start(offset[:], a["ln_b_2"][0, c:c + 1, :].to_broadcast([P, D])).then_inc(s_ln, 16)

            w_in = a["gdn_w_in_2"][0].rearrange("(k p) c -> p k c", p=P)

            def gfront(i, s):
                for half, lo in ((0, 0), (1, D)):
                    sp.dma_start(w_gate(s)[:, :, half * P:(half + 1) * P], w_in[:, :, bass.ds(i * P + lo, P)])\
                        .then_inc(gd.front_in[s], 16)
                sp.dma_start(w_up(s), w_in[:, :, bass.ds(i * 256 + 2 * D, 256)]).then_inc(gd.front_in[s], 16)
                sp.dma_start(w_z(s), w_in[:, :, bass.ds(i * 256 + 4 * D, 256)]).then_inc(gd.front_in[s], 16)

            for j in range(2):
                sp.wait_ge(ffn[1].used, ffn[1].before["used"] + ffn[1].n - (ffn[1].n - 1 - j) % 2)
                gfront(j, j)

            def glater(i, s, _more):
                sp.wait_ge(gd.fronts, i + 1)
                gfront(i + 2, s)

            ln_vectors(0, 5)
            in_pairs(sp, GH - 2, glater)
            for s in range(2):
                sp.wait_ge(gd.fronts, GH - 1 + s)
                sp.dma_start(w_out(s), a["gdn_w_out_2"][0][s * D:(s + 1) * D, :]
                             .rearrange("(f p) n -> p f n", p=P)).then_inc(s_wout[s], 16)
            wg, wu, wd = (a[f"moe_w_{n}_2"][0].rearrange("g e r c -> (g e) r c") for n in ("gate", "up", "down"))

            def mfront(i, s):
                for dst, w in ((w_gate(s), wg), (w_up(s), wu)):
                    sp.dma_start(dst, w[bass.ds(i, 1)].rearrange("e (k p) c -> p (e k) c", p=P))\
                        .then_inc(moe.front_in[s], 16)

            def mdown(i, s):
                sp.dma_start(w_down(s), wd[bass.ds(i, 1)].rearrange("e (f p) n -> p (e f) n", p=P))\
                    .then_inc(moe.back_in[s], 16)

            def mcomb(i, s):
                sp.dma_start(cb[:, s, :], comb_dram[bass.ds(i, 1), 0, :].to_broadcast([P, T]))\
                    .then_inc(moe.back_in[s], 16)

            def rfront(j, s):
                for x in range(2):
                    for half, w in enumerate((wg, wu)):
                        sp.dma_start(w_both(s, x)[:, :, half, :],
                                     w[bass.ds(2 * j + x, 1)].rearrange("e (k p) c -> p (e k) c", p=P))\
                            .then_inc(r_front[s], 16)

            def rdown(j, s):
                for x in range(2):
                    sp.dma_start(w_down_of(s)[:, x],
                                 wd[bass.ds(2 * j + x, 1)].rearrange("e (f p) n -> p (e f) n", p=P))\
                        .then_inc(r_back[s], 16)

            def rrows(j, s):
                for x in range(2):
                    sp.dma_start(rows_r[x * CAP:(x + 1) * CAP, s],
                                 comb_dram[bass.ds(2 * j + x, 1)].to_broadcast([CAP, 2, T]))\
                        .then_inc(r_back[s], 16)

            def ple_gate(half):
                sp.dma_start(W[:, 0, half * 4 * D:(half + 1) * 4 * D].rearrange("p (k n) -> p k n", k=4),
                             a["pe_w_gate_2"][0].rearrange("(k p) n -> p k n", p=P)[:, half * 4:half * 4 + 4, :])\
                    .then_inc(s_wpe, 16)

            def ple_proj():
                sp.dma_start(view(1, 0, (2, D)), a["pe_w_proj_2"][0].rearrange("(k p) n -> p k n", p=P))\
                    .then_inc(s_wpe, 16)

            sp.wait_ge(s_mixed, 1)
            rfront(0, 0)
            sp.wait_ge(s_mixed, 2)
            rdown(0, 0)
            rfront(1, 1)
            rdown(1, 1)
            sp.wait_ge(s_combT, 1)
            sp.dma_start(comb_dram, combT[:]).then_inc(s_comb_out, 16)
            sp.wait_ge(s_comb_out, 16)
            ln_vectors(1, 6)

            def routed_later(j, s, _more):
                sp.wait_ge(r_up, j + 1)
                rfront(j + 2, s)
                sp.wait_ge(r_selout, j + 1)
                rrows(j + 2, s)
                sp.wait_ge(r_down, 2 * j + 2)
                rdown(j + 2, s)

            def mlater(i, s, _more):
                sp.wait_ge(moe.up, moe.before["up"] + 2 * i + 2)
                mfront(i + 2, s)
                sp.wait_ge(moe.used, moe.before["used"] + i + 1)
                mdown(i + 2, s)
                mcomb(i + 2, s)

            sp.wait_ge(s_most, 1)
            with sp.If(sp.value_load(most_i[0:1, 0:1]) < CAP + 1):
                for j in range(2):
                    rrows(j, j)
                in_pairs(sp, PAIRS - 2, routed_later)
                sp.wait_ge(r_up, PAIRS - 1)
                for half in range(2):
                    ple_gate(half)
                sp.wait_ge(r_up, PAIRS)
                ple_proj()
            with sp.Else():
                for j in range(2):
                    sp.wait_ge(r_front[j], 64)
                    sp.wait_ge(r_back[j], 32)
                for j in range(2):
                    mfront(j, j)
                    mdown(j, j)
                    mcomb(j, j)
                in_pairs(sp, EXPERTS - 2, mlater)
                sp.wait_ge(s_moe_done, 1)
                for half in range(2):
                    ple_gate(half)
                ple_proj()
            for t in range(TT):
                sp.wait_ge(s_prod, t + 1)
                sp.dma_start(out[0, t * P:(t + 1) * P, :], xn[:, t, :]).then_inc(s_out, 16)
            sp.wait_ge(s_out, 32)

        @block.tensor
        def _(pe):
            pe.wait_ge(s_const, 16)
            pe.wait_ge(s_rows, ROW_LOADS * 16)
            for n, r in enumerate(ROW_TILES):
                ins = pe.transpose(wb[:, n // 4, (n % 4) * 128:(n % 4) * 128 + r], rows[0:r, n, :],
                                   ident[0:r, 0:r])
            ins.then_inc(s_colT, 1)

            def transpose_norm(c):
                if c == 0:
                    pe.wait_ge(s_cols, 1)
                pe.wait_ge(s_xn, 2 * (c + 1))
                for b in range(4):
                    for j in range(2):
                        for t in range(TT):
                            ins = pe.transpose(wb[:, b, (2 * j + t) * P:(2 * j + t + 1) * P],
                                               xn[:, t, (2 * b + j) * P:(2 * b + j + 1) * P], ident)
                    ins.then_inc(s_trn, 1)

            def clear_acc(c):
                if c == 0:
                    pe.wait_ge(s_zero, 1)
                else:
                    pe.wait_ge(s_xres, 2 * c)
                for b in range(4):
                    pe.matmul(all_acc[b], zeros[:, 0:P], zeros[:], start=True, stop=False, skip_group_check=True)

            def heads(l, c):
                g = att[l]
                kcol, vcol = g.pairs * P, g.pairs * P + P

                def proj(i, s, q):
                    t, half = q // 2, q % 2
                    if q == 0:
                        if not isinstance(i, int) or i > 0:
                            pe.wait_ge(g.copied, g.before["copied"] + i)
                        g.front_loaded(pe, i, s)
                    w = w_heads(l, s)
                    for k in range(4 * half, 4 * half + 4):
                        tok = slice(t * P, (t + 1) * P)
                        if l == 0:
                            ins = pe.matmul(wb[:, t, 0:384], hT[:, k, tok], w[:, k, :],
                                            start=k == 0, stop=k == KT - 1)
                        else:
                            ins = pe.matmul(wb[:, t, 0:256], hT[:, k, tok], w[:, k, 0:256],
                                            start=k == 0, stop=k == KT - 1)
                    if l == 1 and half == 1:
                        for k in range(KT):
                            ins = pe.matmul(wb[:, t, 256:448], hkT[:, k, tok], w[:, k, 256:448],
                                            start=k == 0, stop=k == KT - 1)
                    if q == 3:
                        ins.then_inc(g.proj, 1)

                def body(i, s, more):
                    chunks = list(range(4)) if more else []

                    def fill():
                        if chunks:
                            proj(i + 1, 1 - s, chunks.pop(0))

                    pe.wait_ge(g.roped, g.before["roped"] + i + 1)
                    for p in range(g.pairs):
                        for t in range(TT):
                            pe.transpose(wb[:, 2, (2 * p + t) * P:(2 * p + t + 1) * P],
                                         st[:, s, t, p * P:(p + 1) * P], ident)
                    for t in range(TT):
                        ins = pe.transpose(wb[:, 3, t * P:(t + 1) * P], st[:, s, t, kcol:kcol + P], ident)
                    ins.then_inc(g.heads_transposed, 1)
                    if g.pairs > 1:
                        fill()
                    for p in range(g.pairs):
                        m = g.pairs * i + p
                        if p == 0:
                            pe.wait_ge(g.qT_ready, g.before["qT_ready"] + i + 1)
                            pe.wait_ge(g.kT_ready, g.before["kT_ready"] + i + 1)
                        else:
                            pe.wait_ge(g.oT_ready, g.before["oT_ready"] + m)
                        for lo, hi in ((0, P), (P, 3 * P)):
                            for h in range(2):
                                rw = slice(h * HD, (h + 1) * HD)
                                ins = pe.matmul(wb[:, 2 + h, lo:hi], qT[rw, p, lo:lo + P], kT[rw, 0:hi - lo],
                                                start=True, stop=True)
                        ins.then_inc(g.scored, 1)
                        for _ in range(3 - g.pairs):
                            fill()
                        pe.wait_ge(g.normed, g.before["normed"] + 4 * (m + 1))
                        for h in range(2):
                            pe.transpose(wb[:, 2 + h, 0:P], PR[:, h, 0:P], ident)
                            pe.transpose(wb[:, 2 + h, P:2 * P], PR[:, h, 129:257], ident)
                            ins = pe.transpose(wb[:, 2 + h, 2 * P:3 * P], PR[:, h, 257:385], ident)
                        ins.then_inc(g.probs_transposed, 1)
                        fill()
                        pe.wait_ge(g.pt_ready_act, g.before["pt_ready_act"] + m + 1)
                        pe.wait_ge(g.pt_ready_dve, g.before["pt_ready_dve"] + m + 1)
                        for t in range(TT):
                            for h in range(2):
                                v = slice(vcol + h * HD, vcol + (h + 1) * HD) if l == 0 else slice(vcol, vcol + HD)
                                rw = slice(h * HD, (h + 1) * HD)
                                ins = pe.matmul(wb[rw, 2, t * P:T], st[:, s, t, v],
                                                PT[:, h, 0:T] if t == 0 else PT[:, h, T:T + P],
                                                start=t == 0, stop=t == 1, skip_group_check=True)
                        ins.then_inc(g.pv, 1)
                    while chunks:
                        fill()
                    pe.wait_ge(g.oT_ready, g.before["oT_ready"] + g.pairs * (i + 1))
                    g.back_loaded(pe, i, s)
                    for t in range(TT):
                        for f in range(g.pairs):
                            for n in range(2):
                                ins = pe.matmul(all_acc[2 * t + n], oT[:, f, t * P:(t + 1) * P],
                                                w_o(l, s)[:, f, n * 512:(n + 1) * 512],
                                                start=False, stop=False, skip_group_check=True)
                        if not more and t == 0:
                            ins.then_inc(s_acc, 1)
                    ins.then_inc(g.used, 1)

                pe.wait_ge(s_hT, 4 * (c + 1) + (4 if l else 0))
                pe.wait_ge(s_hTa, 4 * (c + 1) + (4 if l else 0))
                for q in range(4):
                    proj(0, 0, q)
                clear_acc(c)
                in_pairs(pe, g.n, body)

            def feed(k, c):
                g = ffn[k]

                def up(i, s):
                    g.front_loaded(pe, i, s)
                    for f in range(2):
                        bank = 2 * s + f
                        for half, w in enumerate((w_gate(s), w_up(s))):
                            for kt in range(KT):
                                ins = pe.matmul(wb[:, bank, half * T:(half + 1) * T],
                                                w[:, kt, f * P:(f + 1) * P], hT[:, kt, :],
                                                start=kt == 0, stop=kt == KT - 1)
                        ins.then_inc(g.up, 1)

                def body(i, s, more):
                    if more:
                        up(i + 1, 1 - s)
                    g.back_loaded(pe, i, s)
                    if not more:
                        pe.wait_ge(g.act, g.before["act"] + 2 * i + 2)
                    for f, t in ([(f, t) for f in range(2) for t in range(TT)] if more else
                                 [(f, t) for t in range(TT) for f in range(2)]):
                        if more and t == 0:
                            pe.wait_ge(g.act, g.before["act"] + 2 * i + f + 1)
                        for n in range(2):
                            ins = pe.matmul(all_acc[2 * t + n], aT[:, s, f, t * P:(t + 1) * P],
                                            w_down(s)[:, f, n * 512:(n + 1) * 512],
                                            start=False, stop=False, skip_group_check=True)
                        if not more and k < 2 and (f, t) == (1, 0):
                            ins.then_inc(s_acc, 1)
                    ins.then_inc(g.used if k < 2 or more else s_moe_done, 1)

                if k < 2:
                    pe.wait_ge(s_hT, 4 * (c + 1) + (4 if c > 1 else 0))
                    pe.wait_ge(s_hTa, 4 * (c + 1) + (4 if c > 1 else 0))
                    clear_acc(c)
                    up(0, 0)
                else:
                    clear_acc(c)
                    up(0, 0)
                in_pairs(pe, g.n, body)

            def transpose_res(c, need):
                pe.wait_ge(s_xres, 2 * need)
                for b in range(4):
                    for j in range(2):
                        for t in range(TT):
                            ins = pe.transpose(wb[:, b, (2 * j + t) * P:(2 * j + t + 1) * P],
                                               xres[:, t, (2 * b + j) * P:(2 * b + j + 1) * P], ident)
                    ins.then_inc(s_trn, 1)

            def hT_plain(c):
                pe.wait_ge(s_hT, 20 + 2 * (c + 1))
                pe.wait_ge(s_hTa, 20 + 2 * (c + 1))

            def delta_rule():
                def problems():
                    return [(t, v) for t in range(TT) for v in range(2)]

                def col(ap, t, v):
                    return ap[:, (2 * t + v) * P:(2 * t + v + 1) * P]

                hT_plain(0)
                pe.wait_ge(s_small, 16 * SMALL_LOADS)
                for t in range(TT):
                    for k in range(KT):
                        ins = pe.matmul(acc[:, 0, t * 64:(t + 1) * 64], hT[:, k, t * P:(t + 1) * P], wab[:, k, :],
                                        start=k == 0, stop=k == KT - 1)
                ins.then_inc(gd.gates_in, 1)
                pe.wait_ge(gd.gates_set, 1)
                for t in range(TT):
                    for d, m in ((0, const("le")), (1, const("ge"))):
                        pe.matmul(acc[:, 1, (2 * t + d) * GV:(2 * t + d + 1) * GV], m, gG[:, t, d, :],
                                  start=True, stop=True)
                    ins = pe.matmul(acc[:, 1, 64 + t * 32:64 + (t + 1) * 32], ones,
                                    gG[:, t].rearrange("p d h -> p (d h)"), start=True, stop=True)
                ins.then_inc(gd.gates_summed, 1)

                def proj(i, s, q):
                    tile, half = q // 2, q % 2
                    if q == 0:
                        gd.front_loaded(pe, i, s)
                        if not isinstance(i, int) or i > 0:
                            pe.wait_ge(gd.taps, 4 * i)
                            pe.wait_ge(gd.zsilu, i)
                    if q == 8 and (not isinstance(i, int) or i > 0):
                        pe.wait_ge(gd.OT, i)
                    for k in range(4 * half, 4 * half + 4):
                        if tile < 4:
                            w = w_gate(s) if tile < 2 else w_up(s)
                            ins = pe.matmul(wb[:, tile // 2, tile % 2 * T:(tile % 2 + 1) * T],
                                            w[:, k, tile % 2 * P:(tile % 2 + 1) * P], hT[:, k, :],
                                            start=k == 0, stop=k == KT - 1)
                        else:
                            t = tile - 4
                            ins = pe.matmul(wb[:, 2, t * T:(t + 1) * T], hT[:, k, t * P:(t + 1) * P],
                                            w_z(s)[:, k, :], start=k == 0, stop=k == KT - 1)
                    if q in (3, 7, 11):
                        ins.then_inc({3: gd.qk, 7: gd.v, 11: gd.z}[q], 1)

                def norms(i):
                    pe.wait_ge(gd.sq, i + 1)
                    pe.matmul(wb[:, 3, :], ones, sq[:].rearrange("p a b -> p (a b)"), start=True, stop=True)\
                        .then_inc(gd.ss, 1)

                def decay_sums(i):
                    pe.wait_ge(gd.silu, 4 * (i + 1))
                    for d in range(2):
                        pe.wait_ge(gd.gu, 2 * i + d + 1)
                        pe.matmul(wb[:, d, :], ones, gU[:, d].rearrange("p t v c -> p (t v c)"),
                                  start=True, stop=True).then_inc(gd.row, 1)

                def turn_values(i):
                    pe.wait_ge(gd.zsilu, i + 1)
                    for t, v in problems():
                        ins = pe.transpose(col(wb[:, 2, :], t, v), cq[:, 2 + v, t * P:(t + 1) * P], ident)
                    ins.then_inc(gd.vt, 1)

                def products(i, s):
                    pe.wait_ge(gd.kq, 2 * (i + 1))
                    for t in range(TT):
                        ins = pe.matmul(wb[:, 3, t * T:(t + 1) * T], kq[s][:, t, 0, :],
                                        kq[s][:, t].rearrange("p a b -> p (a b)"), start=True, stop=True)
                    ins.then_inc(gd.kk, 1)
                    pe.wait_ge(gd.vtok, i + 1)
                    for t in range(TT):
                        ins = pe.transpose(wb[:, 2, t * P:(t + 1) * P], kq[s][:, t, 0, :], ident)
                    ins.then_inc(gd.kt, 1)

                def first_inverse(i):
                    for d in range(2):
                        pe.wait_ge(gd.y2, 2 * i + d + 1)
                        for t, v in problems():
                            ins = pe.transpose(col(acc[:, 2 + d, :], t, v), YI[:, d, t, v, :], ident)
                        ins.then_inc(gd.x2t, 1)

                early = 6

                def turn_output(i):
                    pe.wait_ge(gd.on, i + 1)
                    for v in range(2):
                        for t in range(TT):
                            ins = pe.transpose(wb[:, 2, (2 * v + t) * P:(2 * v + t + 1) * P], og[:, t, v, :], ident)
                    ins.then_inc(gd.ot, 1)

                def body(i, s, more):
                    chunks = list(range(early, 12)) if more else []
                    further = not isinstance(i, int) or i < GH - 2

                    def fill(n):
                        for _ in range(n):
                            if chunks:
                                proj(i + 1, 1 - s, chunks.pop(0))

                    first_chunks = list(range(early)) if further else []

                    def fill_early(n):
                        for _ in range(n):
                            if first_chunks:
                                proj(i + 2, s, first_chunks.pop(0))

                    for n in range(len(LEVELS)):
                        for d in range(2):
                            if n == 0:
                                pe.wait_ge(gd.x2, 2 * i + d + 1)
                                if d == 0:
                                    pe.wait_ge(gd.ktok, i + 1)
                                    pe.wait_ge(gd.vtok, i + 1)
                            else:
                                pe.wait_ge(gd.xev, 10 * i + 2 * (n - 1) + d + 1)
                                pe.wait_ge(gd.yev, 12 * i + 2 * (n - 1) + d + 1)
                            for t, v in problems():
                                ins = pe.matmul(col(acc[:, d, :], t, v), AM[:, d, t, v, :], XI[:, d, t, v, :],
                                                start=True, stop=True)
                            ins.then_inc(gd.g, 1)
                        fill(1)
                        for d in range(2):
                            pe.wait_ge(gd.gev, 12 * i + 2 * n + d + 1)
                            if n < len(LEVELS) - 1:
                                for t, v in problems():
                                    ins = pe.matmul(col(acc[:, 2 + d, :], t, v), YI[:, d, t, v, :],
                                                    GI[:, d, t, v, :], start=True, stop=True)
                                ins.then_inc(gd.xg, 1)
                            for t, v in problems():
                                ins = pe.matmul(col(acc[:, d, :], t, v), GI[:, d, t, v, :],
                                                YI[:, d, t, v, :], start=True, stop=True)
                            ins.then_inc(gd.yg, 1)
                        if n == 0:
                            fill(1)
                        elif n == 4:
                            fill(12)
                    if more:
                        norms(i + 1)
                    pe.wait_ge(gd.yev, 12 * (i + 1))
                    for t, v in problems():
                        ins = pe.matmul(col(acc[:, 0, :], t, v), YI[:, t, t, v, :], vtok[s][:, t, v, :],
                                        start=True, stop=True)
                    ins.then_inc(gd.r1, 1)
                    if more:
                        decay_sums(i + 1)
                        turn_values(i + 1)
                    pe.wait_ge(gd.vdec, i + 1)
                    for t in range(TT):
                        ins = pe.matmul(acc[:, 1, t * T:(t + 1) * T], ktok[:, s, t, :],
                                        vdec[:, t].rearrange("p v c -> p (v c)"), start=True, stop=True)
                    ins.then_inc(gd.s, 1)
                    pe.wait_ge(gd.sev, i + 1)
                    for which in range(2):
                        for t in range(TT):
                            ins = pe.matmul(acc[:, 2 + which, t * T:(t + 1) * T], kq[s][:, t, which, :],
                                            Sst[:, 1 - t].rearrange("p v c -> p (v c)"), start=True, stop=True)
                        ins.then_inc(gd.ks, 1)
                    if more:
                        products(i + 1, 1 - s)
                        pe.wait_ge(gd.expo, 2 * (i + 2))
                    fill_early(1)
                    pe.wait_ge(gd.rb, i + 1)
                    for t, v in problems():
                        ins = pe.matmul(col(acc[:, 0, :], t, v), YI[:, 1 - t, t, v, :], rb[:, t, v, :],
                                        start=True, stop=True)
                    ins.then_inc(gd.r2, 1)
                    fill_early(1)
                    pe.wait_ge(gd.vn2, i + 1)
                    for t, v in problems():
                        pe.matmul(col(acc[:, 1, :], t, v), QA[:, t, t, v, :], vn1[:, t, v, :],
                                  start=True, stop=False)
                        ins = pe.matmul(col(acc[:, 1, :], t, v), QA[:, 1 - t, t, v, :], vn2[:, t, v, :],
                                        start=False, stop=True)
                    ins.then_inc(gd.o, 1)
                    if more:
                        first_inverse(i + 1)
                        fill_early(early)
                        pe.wait_ge(gd.ktok, i + 2)
                        turn_output(i)

                for q in range(12):
                    proj(0, 0, q)
                pe.wait_ge(gd.gates_ready, 1)
                norms(0)
                decay_sums(0)
                turn_values(0)
                products(0, 0)
                first_inverse(0)
                for q in range(early):
                    proj(1, 1, q)
                in_pairs(pe, GH, body)
                pe.wait_ge(gd.OT, GH)
                pe.wait_ge(gd.osum, 2 * GH)
                for f in range(GV):
                    if f == GV - 2:
                        turn_output(GH - 1)
                        pe.wait_ge(gd.OT, GH + 1)
                    if f % 8 == 0:
                        pe.wait_ge(s_wout[f // 8], 16)
                    for t in range(TT):
                        for n in range(2):
                            ins = pe.matmul(all_acc[2 * t + n], OT[:, f, t * P:(t + 1) * P],
                                            w_out(f // 8)[:, f % 8, n * 512:(n + 1) * 512],
                                            start=f == 0, stop=f == GV - 1)
                        if f == GV - 1 and t == 0:
                            ins.then_inc(s_acc, 1)
                    if f % 8 == 7:
                        ins.then_inc(s_mixed, 1)

            def experts():
                hT_plain(1)
                for t in range(TT):
                    for k in range(KT):
                        ins = pe.matmul(acc[:, 0, t * 36:(t + 1) * 36], hT[:, k, t * P:(t + 1) * P], wr[:, k, :],
                                        start=k == 0, stop=k == KT - 1)
                ins.then_inc(rt_pe, 1)

            def route():
                pe.wait_ge(rt_dve, RT_COMB)
                for t in range(TT):
                    ins = pe.transpose(acc[0:EXPERTS, 1, t * P:(t + 1) * P],
                                       comb[:, t].rearrange("p g e -> p (g e)"), ident)
                pe.wait_ge(rt_dve, RT_CHOSEN)
                for t in range(TT):
                    for tile in range(t + 1):
                        pe.matmul(acc[:, 2, t * EXPERTS:(t + 1) * EXPERTS], const("le") if tile == t else ones,
                                  chosen[:, tile, :], start=tile == 0, stop=tile == t)
                for tile in range(TT):
                    ins = pe.matmul(acc[:, 2, TT * EXPERTS:(TT + 1) * EXPERTS], ones, chosen[:, tile, :],
                                    start=tile == 0, stop=tile == TT - 1)
                ins.then_inc(rt_pe, 1)
                pe.wait_ge(rt_dve, RT_PLACES)
                for t in range(TT):
                    ins = pe.transpose(acc[0:EXPERTS, 1, T + t * P:T + (t + 1) * P], place[:, t, :], ident)
                ins.then_inc(rt_pe, 1)
                pe.wait_ge(s_combT, 1)
                pe.wait_ge(s_most, 1)

            def routed():
                def gather(j, half):
                    for k in range(4 * half, 4 * half + 4):
                        for t in range(TT):
                            ins = pe.matmul(wb[:, half, (k % 4) * P:(k % 4 + 1) * P],
                                            xres[:, t, k * P:(k + 1) * P],
                                            sel_in[:, t].rearrange("p x c -> p (x c)"),
                                            start=t == 0, stop=t == TT - 1)
                    ins.then_inc(r_gath, 1)

                def body(j, s, more):
                    half = j // 2 if isinstance(j, int) else (j - s) // 2
                    pe.wait_ge(r_xa, j + 1)
                    pe.wait_ge(r_xd, j + 1)
                    pe.wait_ge(r_front[s], 64 * (half + 1))
                    for k in range(KT):
                        for x in range(2):
                            ins = pe.matmul(wb[x * CAP:(x + 1) * CAP, 2, :].rearrange("p (h c) -> p h c", h=2),
                                            xg[:, k, x * CAP:(x + 1) * CAP], w_both(s, x)[:, k],
                                            start=k == 0, stop=k == KT - 1)
                    ins.then_inc(r_up, 1)
                    if more:
                        pe.wait_ge(r_sel, j + 2)
                        gather(j + 1, 0)
                    pe.wait_ge(r_act, j + 1)
                    for f in range(2):
                        ins = pe.transpose(wb[:, 3, f * P:(f + 1) * P], aS[:, f * P:(f + 1) * P], ident)
                    ins.then_inc(r_turned, 1)
                    if more:
                        gather(j + 1, 1)
                    pe.wait_ge(r_aR, j + 1)
                    pe.wait_ge(r_back[s], 64 * (half + 1))
                    for h in range(2):
                        for f in range(2):
                            for x in range(2):
                                ins = pe.matmul(wb[x * CAP:(x + 1) * CAP, 2 + h, :],
                                                aR[:, f, x * CAP:(x + 1) * CAP],
                                                w_down_of(s)[:, x, f, h * 512:(h + 1) * 512],
                                                start=f == 0, stop=f == 1)
                        ins.then_inc(r_down, 1)
                    pe.wait_ge(r_selout, j + 1)
                    for h, ready in enumerate((r_ya, r_yd)):
                        pe.wait_ge(ready, j + 1)
                        for t in range(TT):
                            ins = pe.matmul(all_acc[2 * t + h], sel_out[:, t * P:(t + 1) * P],
                                            yR[:, h * 512:(h + 1) * 512],
                                            start=False, stop=False, skip_group_check=True)
                    if not more:
                        ins.then_inc(s_moe_done, 1)

                clear_acc(6)
                pe.wait_ge(r_sel, 1)
                for half in range(2):
                    gather(0, half)
                in_pairs(pe, PAIRS, body)

            transpose_norm(0)
            heads(0, 0)
            transpose_norm(1)
            feed(0, 1)
            transpose_norm(2)
            heads(1, 2)
            transpose_norm(3)
            feed(1, 3)
            transpose_res(0, 5)
            delta_rule()
            transpose_res(1, 6)
            experts()
            route()
            with pe.If(pe.value_load(most_i[0:1, 0:1]) < CAP + 1):
                routed()
            with pe.Else():
                feed(2, 6)
            for k in range(2):
                for t in range(TT):
                    ins = pe.transpose(wb[:, 0, (2 * k + t) * P:(2 * k + t + 1) * P],
                                       pt_in[:, t, k * P:(k + 1) * P], ident)
            ins.then_inc(ple_pe, 1)
            pe.wait_ge(ple_act, 1)
            transpose_res(2, 7)
            hT_plain(2)
            pe.wait_ge(s_wpe, 48)
            for t in range(TT):
                for n in range(2):
                    for k in range(KT):
                        pe.matmul(all_acc[2 * t + n], hT[:, k, t * P:(t + 1) * P],
                                  W[:, 0, k * D + n * 512:k * D + (n + 1) * 512],
                                  start=k == 0, stop=k == KT - 1)
                    for k in range(2):
                        ins = pe.matmul(wb[:, 2 * t + n, :], pT[:, k, t * P:(t + 1) * P],
                                        view(1, 0, (2, D))[:, k, n * 512:(n + 1) * 512],
                                        start=k == 0, stop=k == 1)
                ins.then_inc(ple_pe, 1)

        @block.scalar
        def _(act):
            loads = [(0, 0, a["attn_norm"].rearrange("l (k p) -> (l k) p", p=P)),
                     (0, 16, a["kv_norm"].rearrange("(k p) -> k p", p=P)),
                     (0, 24, a["ffn_norm"].rearrange("l (k p) -> (l k) p", p=P))]
            for l in range(2):
                cw = a["conv_w"][l].rearrange("j (k p) -> (j k) p", p=P)
                loads += [(1 + 2 * l, 0, cw[0:4 * FT]), (2 + 2 * l, 0, cw[4 * FT:6 * FT]),
                          (2 + 2 * l, 2 * FT, a["conv_b"][l].rearrange("(k p) -> k p", p=P))]
            gw = a["gdn_conv_w_2"][0].rearrange("j (k p) -> (j k) p", p=P)
            loads += [(5, 0, gw[0:96]), (6, 0, gw[96:160])]
            assert len(loads) == ROW_LOADS
            for n, r, src in loads:
                act.dma_start(rows[r:r + src.shape[0], n, :], src).then_inc(s_rows, 16)
            link = Chain(act, act_chain)
            act.wait_ge(s_ang, 1)
            act.activation(sin16[:, :, 8:16], ang[:, 0], ACT.Sin).then_inc(s_sin, 1)
            act.activation(cos16[:, :, 0:8], ang[:, 0], ACT.Sin, scale=0.5).then_inc(s_sin, 1)

            def squares(c, normalise=True):
                act.wait_ge(s_const, 16)
                act.activation(root_of_eps[:], const("eps"), ACT.Sqrt)
                if c:
                    act.wait_ge(s_trn, 4 * c)
                else:
                    act.wait_ge(s_x, 16)
                for t in range(TT):
                    if c:
                        act.wait_ge(s_xres, 2 * (c - 1) + t + 1)
                    act.activation(xn[:, t, :], xres[:, t, :], ACT.Square, accum_out=ss[:, t:t + 1])\
                        .then_inc(s_sum, 1)
                act.wait_ge(s_ms, c + 1)
                act.activation(rstd[:], ss[:], ACT.Sqrt).then_inc(s_root, 1)
                if not normalise:
                    return
                act.wait_ge(s_rstd, c + 1)
                act.activation(xn[:, 1, :], xres[:, 1, :], ACT.Copy, scale=rstd[:, 1:2]).then_inc(s_xn, 1)

            def evac_norm(c, gains):
                act.wait_ge(s_cols, 1)
                for b in (1, 3):
                    act.wait_ge(s_trn, 4 * c + b + 1)
                    for k in (2 * b, 2 * b + 1):
                        for dst, base in gains:
                            act.activation(dst[:, k, :], wb[:, b, k % 2 * T:(k % 2 + 1) * T], ACT.Copy,
                                           scale=cols[:, 0, base + k:base + k + 1]).then_inc(s_hTa, 1)

            def heads(l):
                g = att[l]
                width = 384 if l == 0 else 448

                def body(i, s, more):
                    act.wait_ge(g.proj, g.before["proj"] + i + 1)
                    act.activation(st[:, s, :, 0:width], wb[:, 0:2, 0:width], ACT.Copy).then_inc(g.copied, 1)
                    act.wait_ge(g.heads_transposed, g.before["heads_transposed"] + i + 1)
                    act.activation(qT[:, 0:g.pairs, :], wb[:, 2, 0:g.pairs * T].rearrange("p (a b) -> p a b", b=T),
                                   ACT.Copy, scale=HD ** -0.5).then_inc(g.qT_ready, 1)
                    for p in range(g.pairs):
                        m = g.pairs * i + p
                        for q, (lo, hi) in enumerate(((0, 128 + l), (129, 385 + l))):
                            act.wait_ge(g.max_ready, g.before["max_ready"] + 2 * m + q + 1)
                            for h in range(2):
                                act.activation(PR[:, h, lo:hi], SM[:, h, lo:hi], ACT.Exp, bias=nm[:, q, h:h + 1],
                                               accum_out=rs[:, h, q:q + 1]).then_inc(g.exped, 1)
                        act.wait_ge(g.probs_transposed, g.before["probs_transposed"] + m + 1)
                        act.activation(PT[:, 0, :], wb[:, 2, 0:384], ACT.Copy).then_inc(g.pt_ready_act, 1)
                        act.wait_ge(g.pv, g.before["pv"] + m + 1)
                        act.activation(oT[:, p, :], wb[:, 2, 0:T], ACT.Copy).then_inc(g.oT_ready, 1)

                in_pairs(act, g.n, body)

            def feed(l):
                g = ffn[l]
                w2, bias = cols[:, 2 + 2 * l, 0:2 * FT], cols[:, 2 + 2 * l, 2 * FT:4 * FT]

                def body(i, s, more):
                    for f in range(2):
                        act.wait_ge(g.up, g.before["up"] + 2 * i + f + 1)
                        for half in range(2):
                            col = 2 * i + f + half * FT
                            act.activation(cg[:, f, half, :], wb[:, 2 * s + f, half * T:(half + 1) * T],
                                           ACT.Identity, bias=bias[:, bass.ds(col, 1)],
                                           scale=w2[:, bass.ds(col, 1)]).then_inc(g.first, 1)
                    for f in range(2):
                        act.wait_ge(g.conv, g.before["conv"] + 2 * i + f + 1)
                        act.activation(sg[:, f, :], cg[:, f, 0, :], ACT.Silu).then_inc(g.silu, 1)
                    act.wait_ge(g.act, g.before["act"] + 2 * (i + 1))

                in_pairs(act, g.n, body)

            def evac_plain(c):
                for b in (1, 3):
                    act.wait_ge(s_trn, 16 + 4 * c + b + 1)
                    act.activation(hT[:, 2 * b:2 * b + 2, :], wb[:, b, :].rearrange("p (a b) -> p a b", a=2),
                                   ACT.Copy).then_inc(s_hTa, 1)

            def delta_rule():
                act.wait_ge(gd.gates_added, 1)
                act.activation(gate_in[:, 3], gate_in[:, 2], ACT.Exp).then_inc(gd.gates_exp, 1)
                act.activation(gate_in[:, 4], gate_in[:, 1], ACT.Exp, scale=-1.0).then_inc(gd.gates_exp, 1)
                act.wait_ge(s_small, 16 * SMALL_LOADS)
                act.activation(alog[:], alog[:], ACT.Exp).then_inc(gd.gates_exp, 1)
                act.wait_ge(gd.gates_exp, 3)
                act.activation(gate_in[:, 5], gate_in[:, 3], ACT.Ln, bias=ones[:, 0:1]).then_inc(gd.gates_exp, 1)
                act.wait_ge(gd.gates_summed, 1)
                link(act.activation(gC[:].rearrange("p t d h -> p (t d h)"), acc[:, 1, 0:64], ACT.Copy))
                act.activation(gE[:], gC[:], ACT.Exp).then_inc(gd.gates_exp, 1)
                act.wait_ge(gd.gates_added, 2)
                act.activation(gK[:], gK[:], ACT.Exp).then_inc(gd.gates_exp, 1)

                def first(i, s, tile):
                    bank = wb[:, tile // 2, tile % 2 * T:(tile % 2 + 1) * T]
                    act.activation(cq[:, tile, :], bank, ACT.Copy,
                                   scale=cols[:, 5, bass.ds(tap_col(2, tile, i), 1)]).then_inc(gd.first, 1)

                def tanh(i, tile):
                    act.wait_ge(gd.taps, 4 * i + tile + 1)
                    act.activation(th[:, tile, :], cq[:, tile, :], ACT.Tanh, scale=0.5).then_inc(gd.tanh, 1)

                def ztanh(i):
                    act.wait_ge(gd.z, i + 1)
                    if not isinstance(i, int) or i > 0:
                        act.wait_ge(gd.zready, i)
                    act.activation(zt[:], wb[:, 2, :].rearrange("p (t c) -> p t c", t=TT), ACT.Tanh, scale=0.5)\
                        .then_inc(gd.ztanh, 1)

                def front(i, s, step):
                    if step == 0:
                        act.wait_ge(gd.qk, i + 1)
                        if not isinstance(i, int) or i > 0:
                            act.wait_ge(gd.kq, 2 * i)
                        first(i, s, 0)
                        first(i, s, 1)
                    elif step == 1:
                        tanh(i, 0)
                    elif step == 2:
                        tanh(i, 1)
                        act.wait_ge(gd.v, i + 1)
                        if not isinstance(i, int) or i > 0:
                            act.wait_ge(gd.vt, i)
                        first(i, s, 2)
                        first(i, s, 3)
                    elif step == 3:
                        tanh(i, 2)
                    elif step == 4:
                        tanh(i, 3)
                        ztanh(i)
                        act.wait_ge(gd.silu, 4 * i + 2)
                        act.activation(sq[:], cq[:, 0:2, :], ACT.Square).then_inc(gd.sq, 1)

                def norms(i):
                    act.wait_ge(gd.ss, i + 1)
                    link(act.activation(lnq[:], wb[:, 3, :].rearrange("p (a b) -> p a b", a=2), ACT.Ln, scale=0.25,
                                        bias=const("eps")))
                    act.activation(lnq[:, 0], lnq[:, 0], ACT.Exp, scale=-0.5, bias=const("qscale"))\
                        .then_inc(gd.qkr, 1)
                    act.activation(lnq[:, 1], lnq[:, 1], ACT.Exp, scale=-0.5, bias=const("kscale"))\
                        .then_inc(gd.qkr, 1)

                def values(i, s):
                    act.wait_ge(gd.vt, i + 1)
                    act.activation(vtok[s].rearrange("p t v c -> p (t v c)"), wb[:, 2, :], ACT.Copy, scale=0.5)\
                        .then_inc(gd.vtok, 1)

                def decays(i):
                    for d in range(2):
                        act.wait_ge(gd.expo, 2 * i + d + 1)
                        act.activation(DM[:, d], DM[:, d], ACT.Exp).then_inc(gd.decay, 1)

                def keys(i, s):
                    act.wait_ge(gd.kt, i + 1)
                    act.activation(ktok[:, s].rearrange("p t c -> p (t c)"), wb[:, 2, 0:T], ACT.Copy)\
                        .then_inc(gd.ktok, 1)

                def first_inverse(i):
                    for d in range(2):
                        act.wait_ge(gd.x2t, 2 * i + d + 1)
                        act.activation(XI[:, d].rearrange("p t v c -> p (t v c)"), acc[:, 2 + d, :], ACT.Copy)\
                            .then_inc(gd.x2, 1)

                def body(i, s, more):
                    link.iteration(i)
                    for n in range(len(LEVELS) - 1):
                        if more:
                            front(i + 1, 1 - s, n)
                    if more:
                        norms(i + 1)
                        values(i + 1, 1 - s)
                    act.wait_ge(gd.s, i + 1)
                    act.activation(Sst[:].rearrange("p d v c -> p (d v c)"), acc[:, 1, :], ACT.Copy)\
                        .then_inc(gd.sev, 1)
                    if more:
                        decays(i + 1)
                        keys(i + 1, 1 - s)
                        first_inverse(i + 1)
                    act.wait_ge(gd.osum, 2 * (i + 1))
                    for n, (t, v) in enumerate((t, v) for t in range(TT) for v in range(2)):
                        link(act.activation(rb[:, t, v, :], og[:, t, v, :], ACT.Square, accum_out=oss[:, n:n + 1]))
                    link(act.activation(osl[:], oss[:], ACT.Ln, scale=1.0 / P, bias=const("eps")))
                    act.activation(osr[:], osl[:], ACT.Exp, scale=-0.5).then_inc(gd.orms, 1)
                    act.wait_ge(gd.ot, i + 1)
                    act.activation(OT[:, bass.ds(2 * i, 2), :], wb[:, 2, :].rearrange("p (v c) -> p v c", v=2),
                                   ACT.Copy).then_inc(gd.OT, 1)

                for step in range(5):
                    front(0, 0, step)
                link.loop(1)
                link.iteration(0)
                norms(0)
                link.end(1)
                values(0, 0)
                decays(0)
                keys(0, 0)
                first_inverse(0)
                link.loop(6)
                in_pairs(act, GH, body)
                link.end(GH, fewer=1)

            def layernorm(c):
                act.activation(root_of_eps[:], const("eps"), ACT.Sqrt)
                act.wait_ge(s_lnvar, 2 * c + 1)
                act.activation(lrs[:], mv[:, :, 1], ACT.Sqrt, bias=const("lneps")).then_inc(s_lnroot, 1)
                act.wait_ge(s_lnvar, 2 * c + 2)
                act.activation(xres[:, 1, :], xres[:, 1, :], ACT.Copy, scale=lrs[:, 1:2]).then_inc(s_lnroot, 1)

            def experts():
                g = moe
                act.wait_ge(rt_dve, RT_GROUP_SHIFTED)
                act.activation(gex[:], gex[:], ACT.Exp).then_inc(rt_act, 1)
                act.wait_ge(rt_dve, RT_PAIR_DIFFERENCE)
                act.activation(rA[:, 9, :], rA[:, 8, :], ACT.Exp).then_inc(rt_act, 1)
                act.wait_ge(rt_pe, RT_TRANSPOSED)
                act.activation(combT[:], acc[0:EXPERTS, 1, :].rearrange("p (a b) -> p a b", a=2), ACT.Copy)\
                    .then_inc(s_combT, 1)

                def gathered(j):
                    act.wait_ge(r_gath, 2 * j + 1)
                    act.activation(xg[:, 0:4, :].rearrange("p k c -> p (k c)"), wb[:, 0, :], ACT.Copy)\
                        .then_inc(r_xa, 1)

                def routed(j, s, more):
                    act.wait_ge(r_up, j + 1)
                    act.activation(sgr, wb[:, 2, 0:HID], ACT.Silu).then_inc(r_silu, 1)
                    if more:
                        gathered(j + 1)
                    act.wait_ge(r_turned, j + 1)
                    act.activation(aR.rearrange("p f c -> p (f c)"), wb[:, 3, 0:2 * P], ACT.Copy).then_inc(r_aR, 1)
                    act.wait_ge(r_down, 2 * j + 1)
                    act.activation(yR[:, 0:512], wb[:, 2, :], ACT.Copy).then_inc(r_ya, 1)

                def body(i, s, more):
                    for f in range(2):
                        act.wait_ge(g.up, g.before["up"] + 2 * i + f + 1)
                        act.activation(sg[:, f, :], wb[:, 2 * s + f, 0:T], ACT.Silu).then_inc(g.silu, 1)
                    act.wait_ge(g.act, g.before["act"] + 2 * (i + 1))

                act.wait_ge(s_most, 1)
                with act.If(act.value_load(most_i[0:1, 0:1]) < CAP + 1):
                    gathered(0)
                    in_pairs(act, PAIRS, routed)
                with act.Else():
                    in_pairs(act, g.n, body)

            squares(0)
            evac_norm(0, [(hT, 0)])
            heads(0)
            squares(1)
            evac_norm(1, [(hT, 24)])
            feed(0)
            squares(2)
            evac_norm(2, [(hT, 8), (hkT, 16)])
            heads(1)
            squares(3)
            evac_norm(3, [(hT, 32)])
            feed(1)
            squares(4, normalise=False)
            evac_plain(0)
            delta_rule()
            layernorm(0)
            evac_plain(1)
            experts()
            layernorm(1)
            act.wait_ge(ple_pe, 1)
            act.activation(pT[:], wb[:, 0, :].rearrange("p (a b) -> p a b", a=2), ACT.Copy).then_inc(ple_act, 1)
            evac_plain(2)
            for t in range(TT):
                act.wait_ge(ple_pe, t + 2)
                act.activation(xn[:, t, :].rearrange("p (n c) -> p n c", n=2), acc[:, 2 * t:2 * t + 2, :],
                               ACT.Sigmoid).then_inc(ple_act, 1)

        @block.vector
        def _(dve):
            link = Chain(dve, dve_chain)
            dve.memset(zeros[:], 0.0).then_inc(s_zero, 1)
            dve.wait_ge(s_const, 16)
            dve.wait_ge(s_pos, 16)
            link(dve.tensor_copy(pos_f[:], pos_i[:]))
            link(dve.tensor_tensor(ang[:, 0], bcast(pos_f[:], 2, 8), bcast(const("freq"), 1, TT), ALU.mult))
            link(dve.tensor_scalar(ang[:, 1], ang[:, 0], 1.0 / TWO_PI, MAGIC, ALU.mult, ALU.add))
            link(dve.tensor_scalar(ang[:, 2], ang[:, 1], -MAGIC, None, ALU.add))
            for part in TWO_PI_PARTS:
                link(dve.scalar_tensor_tensor(ang[:, 0], ang[:, 2], -part, ang[:, 0], ALU.mult, ALU.add))
            dve.tensor_scalar(ang[:, 0], ang[:, 0], 3.1415925, -3.1415925, ALU.min, ALU.max).then_inc(s_ang, 1)
            dve.wait_ge(s_colT, 1)
            link(dve.memset(cols[:, 0:1, 40:96], 0.0))
            for n, r in enumerate(ROW_TILES):
                ins = dve.tensor_copy(cols[:, n, 0:r], wb[:, n // 4, (n % 4) * P:(n % 4) * P + r])
            ins.then_inc(s_cols, 1)
            dve.wait_ge(s_sin, 2)
            link(dve.tensor_tensor(cos16[:, :, 8:16], cos16[:, :, 0:8], cos16[:, :, 0:8], ALU.mult))
            link(dve.tensor_scalar(cos16[:, :, 0:8], cos16[:, :, 8:16], -2.0, 1.0, ALU.mult, ALU.add))
            link(dve.tensor_copy(cos16[:, :, 8:16], cos16[:, :, 0:8]))
            link(dve.tensor_scalar(sin16[:, :, 0:8], sin16[:, :, 8:16], -1.0, None, ALU.mult))

            def rms(c):
                dve.wait_ge(s_sum, 2 * (c + 1))
                dve.tensor_scalar(ss[:], ss[:], 1.0 / D, EPS, ALU.mult, ALU.add).then_inc(s_ms, 1)
                dve.wait_ge(s_root, c + 1)
                dve.reciprocal(rstd[:], rstd[:]).then_inc(s_rstd, 1)
                dve.wait_ge(s_rstd, c + 1)
                dve.tensor_scalar(xn[:, 0, :], xres[:, 0, :], rstd[:, 0:1], None, ALU.mult).then_inc(s_xn, 1)

            def evac_norm(c, gains):
                dve.wait_ge(s_cols, 1)
                for b in (0, 2):
                    dve.wait_ge(s_trn, 4 * c + b + 1)
                    for k in (2 * b, 2 * b + 1):
                        for dst, base in gains:
                            dve.tensor_scalar(dst[:, k, :], wb[:, b, k % 2 * T:(k % 2 + 1) * T],
                                              cols[:, 0, base + k:base + k + 1], None, ALU.mult).then_inc(s_hT, 1)

            def add_acc(c, g):
                for t in range(TT):
                    if t == 0:
                        dve.wait_ge(s_acc, c + 1)
                    else:
                        dve.wait_ge(g.used, g.before["used"] + g.n)
                    dve.tensor_tensor(xres[:, t, :].rearrange("p (n c) -> p n c", n=2), acc[:, 2 * t:2 * t + 2, :],
                                      xres[:, t, :].rearrange("p (n c) -> p n c", n=2), ALU.add)\
                        .then_inc(s_xres, 1)

            def heads(l):
                g = att[l]
                nh = 2 * g.pairs + 2
                mask = const(f"mask{l}")
                per = 3 + g.pairs * (4 + l)

                def body(i, s, more):
                    link.iteration(i)
                    dve.wait_ge(g.copied, g.before["copied"] + i + 1)
                    sv = st[:, s, :, 0:nh * HD].rearrange("p t (h e) -> p t h e", e=HD)
                    c16, s16 = bcast(cos16[:], 2, nh), bcast(sin16[:], 2, nh)
                    link(dve.tensor_tensor(rt[:, 0, :, 0:nh, :], sv[:, :, :, 0:ROT], c16, ALU.mult))
                    link(dve.tensor_tensor(rt[:, 1, :, 0:nh, 0:8], sv[:, :, :, 8:16], s16[:, :, :, 0:8], ALU.mult))
                    link(dve.tensor_tensor(rt[:, 1, :, 0:nh, 8:16], sv[:, :, :, 0:8], s16[:, :, :, 8:16], ALU.mult))
                    dve.tensor_tensor(sv[:, :, :, 0:ROT], rt[:, 0, :, 0:nh, :], rt[:, 1, :, 0:nh, :], ALU.add)\
                        .then_inc(g.roped, 1)
                    dve.wait_ge(g.heads_transposed, g.before["heads_transposed"] + i + 1)
                    dve.tensor_copy(kT[:], wb[:, 3, 0:T]).then_inc(g.kT_ready, 1)
                    for p in range(g.pairs):
                        m = g.pairs * i + p
                        dve.wait_ge(g.scored, g.before["scored"] + m + 1)
                        if l:
                            link(dve.tensor_copy(SM[:, :, 128:386:257],
                                                 bcast(sink[:, bass.ds(2 * m, 2)], 2, 2)))
                        for q, (lo, n, keys) in enumerate(((0, 128 + l, slice(0, P)),
                                                           (129, 256 + l, slice(P, 3 * P)))):
                            link(dve.tensor_tensor(SM[:, :, lo:lo + 128 * (q + 1)], wb[:, 2:4, keys],
                                                   bcast(mask[:, keys], 1, 2), ALU.add))
                            dve.tensor_reduce(nm[:, q, :], SM[:, :, lo:lo + n], AX.X, ALU.max, negate=True)\
                                .then_inc(g.max_ready, 1)
                        for q, (lo, hi) in enumerate(((0, 128), (129, 385))):
                            dve.wait_ge(g.exped, g.before["exped"] + 4 * m + 2 * q + 2)
                            link(dve.reciprocal(rr[:, :, q], rs[:, :, q]))
                            for h in range(2):
                                dve.tensor_scalar(PR[:, h, lo:hi], PR[:, h, lo:hi], rr[:, h, q:q + 1], None,
                                                  ALU.mult).then_inc(g.normed, 1)
                        dve.wait_ge(g.probs_transposed, g.before["probs_transposed"] + m + 1)
                        dve.tensor_copy(PT[:, 1, :], wb[:, 3, 0:384]).then_inc(g.pt_ready_dve, 1)

                link.loop(per)
                in_pairs(dve, g.n, body)
                link.end(g.n)

            def feed(l):
                g = ffn[l]
                taps = [cols[:, 1 + 2 * l, j * 2 * FT:(j + 1) * 2 * FT] for j in range(2)]

                def body(i, s, more):
                    link.iteration(i)
                    for f in range(2):
                        dve.wait_ge(g.first, g.before["first"] + 4 * i + 2 * f + 2)
                        for half in range(2):
                            col = 2 * i + f + half * FT
                            u = wb[:, 2 * s + f, half * T:(half + 1) * T]
                            c = cg[:, f, half, :]
                            link(dve.scalar_tensor_tensor(c[:, 1:T], u[:, 0:T - 1], taps[1][:, bass.ds(col, 1)],
                                                          c[:, 1:T], ALU.mult, ALU.add))
                            ins = dve.scalar_tensor_tensor(c[:, 2:T], u[:, 0:T - 2], taps[0][:, bass.ds(col, 1)],
                                                           c[:, 2:T], ALU.mult, ALU.add)
                            if half:
                                ins.then_inc(g.conv, 1)
                            else:
                                link(ins)
                    for f in range(2):
                        dve.wait_ge(g.silu, g.before["silu"] + 2 * i + f + 1)
                        dve.wait_ge(g.conv, g.before["conv"] + 2 * i + f + 1)
                        dve.wait_ge(g.used, g.before["used"] + i)
                        dve.tensor_tensor(aT[:, s, f, :], sg[:, f, :], cg[:, f, 1, :], ALU.mult).then_inc(g.act, 1)

                link.loop(6)
                in_pairs(dve, g.n, body)
                link.end(g.n)

            def final_norm():
                dve.wait_ge(s_sum, 2 * 5)
                dve.tensor_scalar(ss[:], ss[:], 1.0 / D, EPS, ALU.mult, ALU.add).then_inc(s_ms, 1)
                dve.wait_ge(s_root, 5)
                link(dve.reciprocal(rstd[:], rstd[:]))
                for t in range(TT):
                    dve.scalar_tensor_tensor(xres[:, t, :], xres[:, t, :], rstd[:, t:t + 1], gain[:], ALU.mult,
                                             ALU.mult).then_inc(s_xres, 1)

            def evac_plain(c):
                for b in (0, 2):
                    dve.wait_ge(s_trn, 16 + 4 * c + b + 1)
                    dve.tensor_copy(hT[:, 2 * b:2 * b + 2, :], wb[:, b, :].rearrange("p (a b) -> p a b", a=2))\
                        .then_inc(s_hT, 1)

            def pairs_at(ap, i, lo, hi, step):
                x = ap[:].rearrange("p t d h -> p (t d) h")[:, lo:hi:step, bass.ds(2 * i, 2)]
                return bcast(x, 3, P)

            def delta_rule():
                dve.wait_ge(gd.gates_in, 1)
                dve.wait_ge(s_small, 16 * SMALL_LOADS)
                ab = acc[:, 0, 0:128].rearrange("p (t c) -> p t c", t=TT)
                link(dve.tensor_tensor(gate_in[:, 0], ab[:, :, 0:32], bcast(dtb[:], 1, TT), ALU.add))
                link(dve.tensor_copy(gate_in[:, 1], ab[:, :, 32:64]))
                link(dve.tensor_scalar(gate_in[:, 2], gate_in[:, 0], -1.0, None, ALU.mult))
                dve.tensor_tensor(gate_in[:, 2], gate_in[:, 2], gate_in[:, 0], ALU.min).then_inc(gd.gates_added, 1)
                link(dve.tensor_scalar(gate_in[:, 0], gate_in[:, 0], 0.0, None, ALU.max))
                dve.wait_ge(gd.gates_exp, 4)
                link(dve.tensor_tensor(gate_in[:, 0], gate_in[:, 0], gate_in[:, 5], ALU.add))
                gg = gG[:].rearrange("p t d h -> p t (d h)")
                link(dve.tensor_tensor(gg, gate_in[:, 0], bcast(alog[:], 1, TT), ALU.mult))
                dve.tensor_scalar(gG[:], gG[:], -1.0, None, ALU.mult).then_inc(gd.gates_set, 1)
                link(dve.tensor_scalar(gate_in[:, 4], gate_in[:, 4], 1.0, None, ALU.add))
                link(dve.reciprocal(gB[:].rearrange("p t d h -> p t (d h)"), gate_in[:, 4]))
                dve.wait_ge(gd.gates_exp, 5)
                dve.tensor_tensor(gK[:].rearrange("p t d h -> p (t d h)"), acc[:, 1, 64:128],
                                  gC[:].rearrange("p t d h -> p (t d h)"), ALU.subtract)\
                    .then_inc(gd.gates_added, 1)
                dve.wait_ge(gd.gates_exp, 6)
                link(dve.tensor_scalar(nwh[:], nwh[:], 0.5, None, ALU.mult))
                dve.memset(gate_in[:, 0], 0.0).then_inc(gd.gates_ready, 1)

                def taps(i, tile):
                    u = wb[:, tile // 2, tile % 2 * T:(tile % 2 + 1) * T]
                    c = cq[:, tile, :]
                    for n, (j, dst, src) in enumerate(((0, slice(2, T), slice(0, T - 2)),
                                                       (1, slice(1, T), slice(0, T - 1)),
                                                       (3, slice(0, T - 1), slice(1, T)),
                                                       (4, slice(0, T - 2), slice(2, T)))):
                        row = 5 if j < 3 else 6
                        ins = dve.scalar_tensor_tensor(c[:, dst], u[:, src],
                                                       cols[:, row, bass.ds(tap_col(j, tile, i), 1)],
                                                       c[:, dst], ALU.mult, ALU.add)
                        if n < 3:
                            link(ins)
                    ins.then_inc(gd.taps, 1)

                def silu(i, tile):
                    dve.wait_ge(gd.tanh, 4 * i + tile + 1)
                    dve.scalar_tensor_tensor(cq[:, tile, :], th[:, tile, :], 1.0, cq[:, tile, :], ALU.add,
                                             ALU.mult).then_inc(gd.silu, 1)

                def front(i, step):
                    if step in (0, 2):
                        dve.wait_ge(gd.first, 4 * i + 2 + step)
                    if step < 4:
                        taps(i, step)

                def front_silu(i, step):
                    if step:
                        silu(i, step - 1)
                    if step == 4:
                        dve.wait_ge(gd.ztanh, i + 1)
                        if not isinstance(i, int) or i > 0:
                            dve.wait_ge(gd.zready, i)
                        dve.scalar_tensor_tensor(zs[:], zt[:], 1.0, wb[:, 2, :].rearrange("p (t c) -> p t c", t=TT),
                                                 ALU.add, ALU.mult).then_inc(gd.zsilu, 1)

                def exponents(i):
                    for d in range(2):
                        dve.wait_ge(gd.row, 2 * i + d + 1)
                        dve.wait_ge(gd.lgr, 2 * i + d + 1)
                        dve.tensor_tensor(DM[:, d].rearrange("p t v c -> p (t v c)"), wb[:, d, :],
                                          LG[:, d].rearrange("p t v c -> p (t v c)"), ALU.add).then_inc(gd.expo, 1)

                def normalise(i, s):
                    for n, which in ((1, 1), (0, 0)):
                        dve.wait_ge(gd.qkr, 2 * i + n + 1)
                        dve.tensor_tensor(kq[s][:, :, 1 - which, :], cq[:, n, :].rearrange("p (t c) -> p t c", t=TT),
                                          lnq[:, n, :].rearrange("p (t c) -> p t c", t=TT), ALU.mult)\
                            .then_inc(gd.kq, 1)

                def matrices(i):
                    dve.wait_ge(gd.kk, i + 1)
                    for d in range(2):
                        dve.wait_ge(gd.db, 2 * i + d + 1)
                        dve.tensor_tensor(AM[:, d], bcast(prod[:, :, 0, :], 2, 2), DB[:, d], ALU.mult)\
                            .then_inc(gd.am, 1)

                def attention():
                    for d in range(2):
                        dve.tensor_tensor(QA[:, d], bcast(prod[:, :, 1, :], 2, 2), DM[:, d], ALU.mult)

                prod = wb[:, 3, :].rearrange("p (t a c) -> p t a c", t=TT, a=2)

                def body(i, s, more):
                    link.iteration(i)
                    for n in range(len(LEVELS)):
                        end = n == len(LEVELS) - 1
                        lm = const("levels")[:, 2 * n * P:(2 * n + 2) * P]
                        for d in range(2):
                            dve.wait_ge(gd.g, 12 * i + 2 * n + d + 1)
                            dve.tensor_tensor(GI[:, d].rearrange("p t v c -> p (t v) c"),
                                              acc[:, d, :].rearrange("p (q c) -> p q c", c=P),
                                              bcast(lm[:, d * P:(d + 1) * P], 1, 4), ALU.mult).then_inc(gd.gev, 1)
                        if more and n:
                            front_silu(i + 1, n - 1)
                        for d in range(2):
                            for m, bank, done, count, ready in ((XI, 2 + d, gd.xg, 10, gd.xev),
                                                                (YI, d, gd.yg, 12, gd.yev)):
                                if end and m is XI:
                                    continue
                                dve.wait_ge(done, count * i + 2 * n + d + 1)
                                x = m[:, d].rearrange("p t v c -> p (t v c)")
                                dve.tensor_tensor(x, x, acc[:, bank, :], ALU.subtract).then_inc(ready, 1)
                        if more and n < 5:
                            front(i + 1, n)
                    dve.wait_ge(gd.r1, i + 1)
                    dve.tensor_tensor(vn1[:], acc[:, 0, :].rearrange("p (t v c) -> p t v c", t=TT, v=2),
                                      pairs_at(gB, i, 0, 4, 3), ALU.mult).then_inc(gd.vn1, 1)
                    dve.wait_ge(gd.vn1, i + 1)
                    dve.tensor_tensor(vdec[:], vn1[:], pairs_at(gK, i, 0, 4, 3), ALU.mult).then_inc(gd.vdec, 1)
                    if more:
                        exponents(i + 1)
                        normalise(i + 1, 1 - s)
                    dve.wait_ge(gd.ks, 2 * i + 1)
                    link(dve.tensor_tensor(rb[:], acc[:, 2, :].rearrange("p (t v c) -> p t v c", t=TT, v=2),
                                           pairs_at(gE, i, 1, 3, 1), ALU.mult))
                    dve.tensor_tensor(rb[:], vtok[s], rb[:], ALU.subtract).then_inc(gd.rb, 1)
                    dve.wait_ge(gd.ks, 2 * i + 2)
                    dve.tensor_tensor(qse[:], acc[:, 3, :].rearrange("p (t v c) -> p t v c", t=TT, v=2),
                                      pairs_at(gE, i, 1, 3, 1), ALU.mult).then_inc(gd.qse, 1)
                    if more:
                        matrices(i + 1)
                    dve.wait_ge(gd.r2, i + 1)
                    dve.tensor_tensor(vn2[:], acc[:, 0, :].rearrange("p (t v c) -> p t v c", t=TT, v=2),
                                      pairs_at(gB, i, 1, 3, 1), ALU.mult).then_inc(gd.vn2, 1)
                    dve.wait_ge(gd.o, i + 1)
                    dve.wait_ge(gd.qse, i + 1)
                    dve.tensor_tensor(og[:].rearrange("p t v c -> p (t v c)"), acc[:, 1, :],
                                      qse[:].rearrange("p t v c -> p (t v c)"), ALU.add).then_inc(gd.osum, 2)
                    if more:
                        attention()
                    dve.wait_ge(gd.orms, i + 1)
                    flat = og[:].rearrange("p t v c -> p (t v) c")
                    link(dve.tensor_tensor(flat, flat, bcast(osr[:], 2, P), ALU.mult))
                    dve.wait_ge(gd.zready, i + 1)
                    dve.tensor_tensor(og[:].rearrange("p t v c -> p (t v c)"), og[:].rearrange("p t v c -> p (t v c)"),
                                      zn[:].rearrange("p t c -> p (t c)"), ALU.mult).then_inc(gd.on, 1)

                link.loop(12)
                link.iteration(0)
                for step in range(5):
                    front(0, step)
                    front_silu(0, step)
                link.end(1)
                exponents(0)
                normalise(0, 0)
                matrices(0)
                attention()

                link.loop(14)
                in_pairs(dve, GH, body)
                link.end(GH, fewer=12)

            def layernorm(c, done, count, inc):
                for t in range(TT):
                    if t == 0 and c == 0:
                        dve.wait_ge(s_acc, 5)
                    else:
                        dve.wait_ge(done, count)
                    x2 = xres[:, t, :].rearrange("p (n c) -> p n c", n=2)
                    dve.scalar_tensor_tensor(x2, x2, ALPHA, acc[:, 2 * t:2 * t + 2, :], ALU.mult, ALU.add)\
                        .then_inc(s_added, 1)
                    dve.wait_ge(s_added, 2 * c + t + 1)
                    for n in range(2):
                        link(dve.bn_stats(bst[:, t, n, :], xres[:, t, n * 512:(n + 1) * 512]))
                    ins = dve.bn_aggr(mv[:, t, :], bst[:, t])
                    if t:
                        ins.then_inc(s_lnvar, 1)
                    else:
                        link(ins)
                dve.wait_ge(s_ln, 32 * (c + 1))
                dve.wait_ge(s_lnvar, 2 * c + 1)
                dve.wait_ge(s_lnroot, 2 * c + 1)
                link(dve.reciprocal(lrs[:], lrs[:]))
                dve.scalar_tensor_tensor(xres[:, 1, :], xres[:, 1, :], mv[:, 1, 0:1], gain[:],
                                         ALU.subtract, ALU.mult).then_inc(s_lnvar, 1)
                link(dve.scalar_tensor_tensor(xres[:, 0, :], xres[:, 0, :], mv[:, 0, 0:1], gain[:],
                                              ALU.subtract, ALU.mult))
                dve.scalar_tensor_tensor(xres[:, 0, :], xres[:, 0, :], lrs[:, 0:1], offset[:], ALU.mult, ALU.add)\
                    .then_inc(s_xres, 1)

            def first_largest(x, n, top, onehot, work):
                link(dve.tensor_reduce(top, x, AX.X, ALU.max))
                link(dve.tensor_tensor(work, x, bcast(top, 2, n), ALU.is_ge))
                link(dve.tensor_tensor(work, work, bcast(const("rank")[:, 0:n], 1, TT), ALU.mult))
                link(dve.tensor_reduce(rA[:, 15, :], work, AX.X, ALU.max))
                link(dve.tensor_tensor(onehot, work, bcast(rA[:, 15, :], 2, n), ALU.is_equal))

            def route():
                dve.wait_ge(rt_pe, RT_LOGITS)
                link(dve.tensor_tensor(lg[:], acc[:, 0, 0:72].rearrange("p (t c) -> p t c", t=TT),
                                       bcast(br[:], 1, TT), ALU.add))
                first_largest(lg[:, :, 0:4], GROUPS, rA[:, 0, :], goh[:], rB[:, 0, :, 0:4])
                dve.tensor_tensor(gex[:], lg[:, :, 0:4], bcast(rA[:, 0, :], 2, 4), ALU.subtract).then_inc(rt_dve, 1)
                link(dve.tensor_tensor(sel[:], lg[:, :, 4:36].rearrange("p t (g e) -> p t g e", g=GROUPS),
                                       bcast(goh[:], 3, 8), ALU.mult))
                es, oh1, es2, oh2, work = (rB[:, n] for n in range(1, 6))
                link(dve.tensor_reduce(es, sel[:].rearrange("p t g e -> p t e g"), AX.X, ALU.add))
                first_largest(es, 8, rA[:, 1, :], oh1, work)
                link(dve.scalar_tensor_tensor(es2, oh1, NEG, es, ALU.mult, ALU.add))
                first_largest(es2, 8, rA[:, 2, :], oh2, work)
                dve.tensor_tensor(rA[:, 8, :], rA[:, 2, :], rA[:, 1, :], ALU.subtract).then_inc(rt_dve, 1)
                dve.wait_ge(rt_act, RT_GROUP_EXP)
                link(dve.tensor_reduce(rA[:, 3, :], gex[:], AX.X, ALU.add))
                dve.wait_ge(rt_act, RT_PAIR_EXP)
                link(dve.tensor_scalar(rA[:, 4, :], rA[:, 9, :], 1.0, None, ALU.add))
                link(dve.tensor_tensor(rA[:, 5, :], rA[:, 4, :], rA[:, 3, :], ALU.mult))
                link(dve.reciprocal(rA[:, 6, :], rA[:, 5, :]))
                link(dve.tensor_tensor(rA[:, 7, :], rA[:, 6, :], rA[:, 9, :], ALU.mult))
                link(dve.tensor_tensor(oh1, oh1, bcast(rA[:, 6, :], 2, 8), ALU.mult))
                link(dve.tensor_tensor(oh2, oh2, bcast(rA[:, 7, :], 2, 8), ALU.mult))
                link(dve.tensor_tensor(oh1, oh1, oh2, ALU.add))
                dve.tensor_tensor(comb[:], bcast(oh1, 2, GROUPS), bcast(goh[:], 3, 8), ALU.mult).then_inc(rt_dve, 1)
                dve.wait_ge(rt_dve, RT_COMB)
                dve.tensor_scalar(chosen[:], comb[:].rearrange("p t g e -> p t (g e)"), 0.0, None, ALU.is_gt)\
                    .then_inc(rt_dve, 1)
                dve.wait_ge(rt_pe, RT_COUNTED)
                link(dve.tensor_reduce(most[:], acc[:, 2, TT * EXPERTS:(TT + 1) * EXPERTS], AX.X, ALU.max))
                dve.tensor_copy(most_i[:], most[:]).then_inc(s_most, 1)
                link(dve.tensor_tensor(place[:], acc[:, 2, 0:TT * EXPERTS].rearrange("p (t e) -> p t e", t=TT),
                                       chosen[:], ALU.mult))
                dve.tensor_scalar(place[:], place[:], -1.0, None, ALU.add).then_inc(rt_dve, 1)
                dve.wait_ge(rt_dve, RT_PLACES)

            def experts():
                g = moe

                def one_hot(j):
                    dve.tensor_tensor(sel_in, bcast(bcast(const("place"), 1, 2), 1, TT),
                                      bcast(place[:, :, bass.ds(2 * j, 2)], 3, CAP), ALU.is_equal)\
                        .then_inc(r_sel, 1)

                def gathered(j):
                    dve.wait_ge(r_gath, 2 * j + 2)
                    dve.tensor_copy(xg[:, 4:8, :].rearrange("p k c -> p (k c)"), wb[:, 1, :]).then_inc(r_xd, 1)

                def routed(j, s, more):
                    if more:
                        one_hot(j + 1)
                    dve.wait_ge(r_silu, j + 1)
                    dve.tensor_tensor(aS, sgr, wb[:, 2, HID:2 * HID], ALU.mult).then_inc(r_act, 1)
                    half = j // 2 if isinstance(j, int) else (j - s) // 2
                    dve.wait_ge(r_back[s], 64 * (half + 1))
                    dve.scalar_tensor_tensor(sel_out, rows_r[:, s, 1, :], const("place_col"), rows_r[:, s, 0, :],
                                             ALU.is_equal, ALU.mult).then_inc(r_selout, 1)
                    if more:
                        gathered(j + 1)
                    dve.wait_ge(r_down, 2 * j + 2)
                    dve.tensor_copy(yR[:, 512:1024], wb[:, 3, :]).then_inc(r_yd, 1)

                def body(i, s, more):
                    link.iteration(i)
                    g.back_loaded(dve, i, s)
                    for f in range(2):
                        dve.wait_ge(g.silu, g.before["silu"] + 2 * i + f + 1)
                        dve.wait_ge(g.used, g.before["used"] + i)
                        link(dve.tensor_tensor(cg[:, f, 0, :], sg[:, f, :], wb[:, 2 * s + f, T:2 * T], ALU.mult))
                        dve.tensor_tensor(aT[:, s, f, :], cg[:, f, 0, :], cb[:, s, :], ALU.mult).then_inc(g.act, 1)

                with dve.If(dve.value_load(most_i[0:1, 0:1]) < CAP + 1):
                    one_hot(0)
                    gathered(0)
                    in_pairs(dve, PAIRS, routed)
                    dve.sem_inc(dve_chain, 2 * EXPERTS)
                with dve.Else():
                    link.loop(2)
                    in_pairs(dve, g.n, body)
                    link.end(g.n)

            rms(0)
            evac_norm(0, [(hT, 0)])
            heads(0)
            add_acc(0, att[0])
            rms(1)
            evac_norm(1, [(hT, 24)])
            feed(0)
            add_acc(1, ffn[0])
            dve.wait_ge(s_vec, VEC_LOADS * 16)
            rms(2)
            evac_norm(2, [(hT, 8), (hkT, 16)])
            heads(1)
            add_acc(2, att[1])
            rms(3)
            evac_norm(3, [(hT, 32)])
            feed(1)
            add_acc(3, ffn[1])
            final_norm()
            evac_plain(0)
            delta_rule()
            layernorm(0, s_mixed, 2, 12)
            evac_plain(1)
            route()
            experts()
            layernorm(1, s_moe_done, 1, 14)
            evac_plain(2)
            for t in range(TT):
                dve.wait_ge(ple_act, t + 2)
                x2 = xn[:, t, :].rearrange("p (n c) -> p n c", n=2)
                link(dve.tensor_tensor(x2, x2, wb[:, 2 * t:2 * t + 2, :], ALU.mult))
                dve.tensor_tensor(xn[:, t, :], xn[:, t, :], xres[:, t, :], ALU.add).then_inc(s_prod, 1)

        @block.gpsimd
        def _(pool):
            pool.wait_ge(att[0].front_in[0], 48)
            vec = [(sink[:], a["sinks_b"]), (gain[:], a["final_norm"].rearrange("(a n) -> a n", a=1))]
            assert len(vec) == VEC_LOADS
            for dst, src in vec:
                pool.dma_start(dst, src.to_broadcast([P, src.shape[1]])).then_inc(s_vec, 16)
            small = [(dtb[:], a["gdn_dt_bias_2"].rearrange("a z h -> a (z h)").to_broadcast([P, 2 * GV])),
                     (alog[:], a["gdn_a_log_2"].rearrange("a z h -> a (z h)").to_broadcast([P, 2 * GV])),
                     (nwh[:], a["gdn_norm_w_2"].to_broadcast([P, P])),
                     (wab[:], a["gdn_w_in_2"][0].rearrange("(k p) c -> p k c", p=P)[:, :, 6 * D:6 * D + 64]),
                     (wr[:, :, 0:4], a["moe_w_group_2"][0].rearrange("(k p) c -> p k c", p=P)),
                     (wr[:, :, 4:36], a["moe_w_router_2"][0].rearrange("(k p) c -> p k c", p=P)),
                     (br[:, 0:4], a["moe_b_group_2"].to_broadcast([P, 4])),
                     (br[:, 4:36], a["moe_b_router_2"].to_broadcast([P, 32])),
                     (pt_in[:], a["p_2"][0].rearrange("b (t p) c -> p (b t) c", p=P))]
            late = where["ones"][0]
            small.append((cst[:, late:], consts[:, late:]))
            assert len(small) == SMALL_LOADS
            for dst, src in small:
                pool.dma_start(dst, src).then_inc(s_small, 16)

            pool.wait_ge(gd.gates_ready, 1)

            def heads_of(ap, i, d):
                return bcast(ap[:, :, d, bass.ds(2 * i, 2)], 3, P)

            def wide(ap):
                return bcast(bcast(ap, 1, 2), 1, TT)

            def sums(i):
                for d, m in ((0, const("le")), (1, const("ge"))):
                    if not isinstance(i, int) or i > 0:
                        pool.wait_ge(gd.row, 2 * i)
                        pool.wait_ge(gd.expo, 2 * i)
                    pool.tensor_tensor(gU[:, d], wide(m), heads_of(gG, i, d), ALU.mult).then_inc(gd.gu, 1)
                    pool.tensor_tensor(LG[:, d], wide(const("lim")[:, d * P:(d + 1) * P]), heads_of(gC, i, d),
                                       ALU.subtract).then_inc(gd.lgr, 1)

            def decays(i):
                for d in range(2):
                    pool.wait_ge(gd.decay, 2 * i + d + 1)
                    pool.tensor_tensor(DB[:, d], DM[:, d], heads_of(gB, i, d), ALU.mult).then_inc(gd.db, 1)

            def quarters(i):
                for d in range(2):
                    pool.wait_ge(gd.am, 2 * i + d + 1)
                    pool.tensor_tensor(GI[:, d].rearrange("p t v c -> p (t v) c"),
                                       AM[:, d].rearrange("p t v c -> p (t v) c"),
                                       bcast(const("first")[:, d * P:(d + 1) * P], 1, 4), ALU.mult)\
                        .then_inc(gd.n1, 1)

            def first_inverse(i):
                pool.wait_ge(gd.n1, 2 * i + 2)
                for d in range(2):
                    pool.tensor_tensor(YI[:, d].rearrange("p t v c -> p (t v) c"),
                                       GI[:, d].rearrange("p t v c -> p (t v) c"),
                                       bcast(ident, 1, 4), ALU.add).then_inc(gd.y2, 1)

            def body(i, s, more):
                pool.wait_ge(gd.zsilu, i + 1)
                pool.tensor_tensor(zn[:].rearrange("p t (v c) -> p (t v) c", v=2),
                                   zs[:].rearrange("p t (v c) -> p (t v) c", v=2),
                                   bcast(nwh[:], 1, 4), ALU.mult).then_inc(gd.zready, 1)
                if more:
                    sums(i + 1)
                    decays(i + 1)
                    quarters(i + 1)
                    pool.wait_ge(gd.r2, i + 1)
                    first_inverse(i + 1)
                pool.wait_ge(gd.on, i + 1)

            sums(0)
            decays(0)
            quarters(0)
            first_inverse(0)
            in_pairs(pool, GH, body)
            for c in range(2):
                pool.wait_ge(s_ln, 32 * (c + 1))
                pool.wait_ge(s_lnroot, 2 * c + 2)
                pool.tensor_tensor(xres[:, 1, :], xres[:, 1, :], offset[:], ALU.add).then_inc(s_xres, 1)


ROW_TILES = (40, 88, 88, 88, 88, 96, 64)
ROW_LOADS = 11
VEC_LOADS = 2
SMALL_LOADS = 10


def tap_col(j, tile, i):
    j = j if j < 3 else j - 3
    return 32 * j + (i if tile == 0 else i + GH if tile == 1 else 2 * i + 2 * GH + tile - 2)


def split_two_pi():
    a = 6.28125
    b = round((TWO_PI - a) * 2 ** 19) / 2 ** 19
    return a, b, TWO_PI - a - b


TWO_PI_PARTS = split_two_pi()

_UNUSED = ("m2_", "hg_", "gla_")


def kernel(**inputs):
    import numpy as _np
    import concourse.bacc as _bacc
    from concourse import mybir as _mybir
    from concourse.bass_utils import run_bass_kernel_spmd as _run

    nc = _bacc.Bacc("TRN2", target_bir_lowering=False, num_devices=1)
    arrays, args = {}, {}
    for name, value in inputs.items():
        if name.startswith(_UNUSED):
            continue
        v = _np.ascontiguousarray(value)
        arrays[f"in_{name}_dram"] = v
        args[name] = nc.dram_tensor(f"in_{name}_dram", v.shape, _mybir.dt.from_np(v.dtype), kind="ExternalInput").ap()
    table = _np.concatenate(list(constant_columns().values()), axis=1)
    arrays["constants"] = table
    consts = nc.dram_tensor("constants", table.shape, _mybir.dt.float32, kind="ExternalInput").ap()
    comb = nc.dram_tensor("comb_scratch", [EXPERTS, 2, T], _mybir.dt.float32, kind="Internal").ap()
    out = nc.dram_tensor("out_dram", [1, T, D], _mybir.dt.float32, kind="ExternalOutput").ap()
    build(nc, args, consts, comb, out)
    r = _run(nc, [arrays], core_ids=[0])
    return r.results[0]["out_dram"]
```
